# Optimizing a Trainium2 kernel written in Bass

```python
import math
import jax
import jax.numpy as jnp
from jax import lax
import numpy as np

D_MODEL = 1024
BATCH = 1
SEQ = 1024
DEPTH = 1
DEC_BATCH = 1
DEC_SEQ = 32
PAST_LEN = 256

CHUNK = 64
D_SSM = D_MODEL // 2
SSM_GROUP_DIM = 16
SSM_GROUPS = D_SSM // SSM_GROUP_DIM
SSM_STATE = 64
D_POOL = D_MODEL // 2
POOL_WINDOWS = (2, 4, 8, 16)
POOL_GROUPS = len(POOL_WINDOWS)
POOL_GROUP_DIM = D_POOL // POOL_GROUPS
POOL_OUT_DIM = D_MODEL // POOL_GROUPS
POOL_MAXW = max(POOL_WINDOWS)
POOL_HIST = POOL_MAXW - 1
D_FF = 2816
D_IN_PROJ = D_SSM + D_POOL + 2 * D_MODEL
EPS = 1e-6
DT_MIN = 1e-3
DT_MAX = 1e-1

kernel_name = "gated_s5_pool_macaron_stream_step"

def rms_norm(x, g):
    xf = x.astype(jnp.float32)
    y = xf * lax.rsqrt(jnp.mean(xf * xf, axis=-1, keepdims=True) + EPS)
    return (y * g.astype(jnp.float32)).astype(x.dtype)

def swiglu(h, w_in, w_out):
    a, b = jnp.split(h @ w_in, 2, axis=-1)
    return (jax.nn.silu(a) * b) @ w_out

def _complex_scan_combine(e1, e2):
    a1r, a1i, b1r, b1i = e1
    a2r, a2i, b2r, b2i = e2
    return (a2r * a1r - a2i * a1i,
            a2r * a1i + a2i * a1r,
            a2r * b1r - a2i * b1i + b2r,
            a2r * b1i + a2i * b1r + b2i)

def s5_branch(u, h0_re, h0_im, lam_re, lam_im, log_step, b_re, b_im, c_re, c_im, d_skip, w_glu, b_glu):
    f32 = jnp.float32
    bsz, t_len, _ = u.shape
    uf = u.astype(f32)
    ug = uf.reshape(bsz, t_len, SSM_GROUPS, SSM_GROUP_DIM)
    lr = lam_re.astype(f32)
    li = lam_im.astype(f32)
    dt = jnp.exp(log_step.astype(f32))[:, None]
    mag = jnp.exp(lr * dt)
    ab_re = mag * jnp.cos(li * dt)
    ab_im = mag * jnp.sin(li * dt)
    den = lr * lr + li * li
    nr = ab_re - 1.0
    f_re = (nr * lr + ab_im * li) / den
    f_im = (ab_im * lr - nr * li) / den
    br = b_re.astype(f32)
    bi = b_im.astype(f32)
    bb_re = f_re[..., None] * br - f_im[..., None] * bi
    bb_im = f_re[..., None] * bi + f_im[..., None] * br
    v_re = jnp.einsum("btgc,gpc->tbgp", ug, bb_re)
    v_im = jnp.einsum("btgc,gpc->tbgp", ug, bb_im)
    if h0_re is not None:
        hr = h0_re.astype(f32)
        hi = h0_im.astype(f32)
        v_re = v_re.at[0].add(ab_re * hr - ab_im * hi)
        v_im = v_im.at[0].add(ab_re * hi + ab_im * hr)
    a_shape = (t_len, 1, SSM_GROUPS, SSM_STATE)
    a_re = jnp.broadcast_to(ab_re, a_shape)
    a_im = jnp.broadcast_to(ab_im, a_shape)
    _, _, s_re, s_im = lax.associative_scan(_complex_scan_combine, (a_re, a_im, v_re, v_im), axis=0)
    y = (jnp.einsum("tbgp,gcp->btgc", s_re, c_re.astype(f32))
         - jnp.einsum("tbgp,gcp->btgc", s_im, c_im.astype(f32)))
    y = y.reshape(bsz, t_len, D_SSM) + d_skip.astype(f32) * uf
    y = jax.nn.gelu(y).astype(u.dtype)
    a, g = jnp.split(y @ w_glu + b_glu, 2, axis=-1)
    return a * jax.nn.sigmoid(g), s_re[-1], s_im[-1]

def pool_branch(u, hist, pos0, pool_w, pool_scale):
    f32 = jnp.float32
    bsz, t_len, _ = u.shape
    n_hist = hist.shape[1]
    ext = jnp.concatenate([hist, u], axis=1).astype(f32)
    lead = jnp.zeros((bsz, POOL_MAXW, D_POOL), f32)
    cs = jnp.concatenate([lead, jnp.cumsum(ext, axis=1)], axis=1)
    start = POOL_MAXW + n_hist
    hi = cs[:, start:start + t_len]
    cur = ext[:, n_hist:]
    pos = pos0 + jnp.arange(t_len, dtype=jnp.int32)
    parts = []
    for gi, w in enumerate(POOL_WINDOWS):
        sl = slice(gi * POOL_GROUP_DIM, (gi + 1) * POOL_GROUP_DIM)
        lo = cs[:, start - w:start - w + t_len, sl]
        cnt = jnp.minimum(pos + 1, w).astype(f32)[None, :, None]
        parts.append((hi[..., sl] - lo) / cnt - cur[..., sl])
    pooled = jnp.stack(parts, axis=2)
    out = jnp.einsum("btgc,gco->btgo", pooled, pool_w.astype(f32))
    out = out.reshape(bsz, t_len, D_MODEL) * pool_scale.astype(f32)
    return out.astype(u.dtype)

def encoder_layer(x, h0_re, h0_im, hist, pos0, p):
    h = x + 0.5 * rms_norm(swiglu(rms_norm(x, p["ffn1_pre_g"]), p["ffn1_w_in"], p["ffn1_w_out"]), p["ffn1_post_g"])
    z = rms_norm(h, p["mix_pre_g"])
    proj = z @ p["w_in"] + p["b_in"]
    u_ssm = proj[..., :D_SSM]
    u_pool = proj[..., D_SSM:D_SSM + D_POOL]
    gates = jax.nn.sigmoid(proj[..., D_SSM + D_POOL:].astype(jnp.float32)).astype(x.dtype)
    g_ssm, g_pool = jnp.split(gates, 2, axis=-1)
    y_ssm, s_re, s_im = s5_branch(u_ssm, h0_re, h0_im, p["ssm_lambda_re"], p["ssm_lambda_im"], p["ssm_log_step"],
                                  p["ssm_b_re"], p["ssm_b_im"], p["ssm_c_re"], p["ssm_c_im"], p["ssm_d"],
                                  p["ssm_w_glu"], p["ssm_b_glu"])
    if hist is None:
        hist = u_pool[:, :0]
    y_pool = pool_branch(u_pool, hist, pos0, p["pool_w"], p["pool_scale"])
    merged = g_ssm * y_ssm + g_pool * y_pool
    h = h + rms_norm(merged @ p["w_out"], p["mix_post_g"])
    h = h + 0.5 * rms_norm(swiglu(rms_norm(h, p["ffn2_pre_g"]), p["ffn2_w_in"], p["ffn2_w_out"]), p["ffn2_post_g"])
    new_hist = jnp.concatenate([hist, u_pool], axis=1)[:, -POOL_HIST:]
    return h, s_re.astype(x.dtype), s_im.astype(x.dtype), new_hist

def setup_inputs(seed: int = 0) -> dict:
    key = jax.random.key(seed)
    ks = jax.random.split(key, 32)
    f32 = jnp.float32

    def nrm(k, shape, s):
        return s * jax.random.normal(k, shape, f32)

    def gain(k):
        return 1.0 + 0.05 * jax.random.normal(k, (DEPTH, D_MODEL), f32)

    n_idx = jnp.arange(SSM_STATE, dtype=f32)
    lam_re = -0.5 + 0.01 * jax.random.normal(ks[10], (DEPTH, SSM_GROUPS, SSM_STATE), f32)
    lam_im = jnp.pi * n_idx + 0.01 * jax.random.normal(ks[11], (DEPTH, SSM_GROUPS, SSM_STATE), f32)
    log_step = jax.random.uniform(ks[12], (DEPTH, SSM_GROUPS), f32, math.log(DT_MIN), math.log(DT_MAX))
    return {
        "x_prompt": nrm(ks[0], (BATCH, SEQ, D_MODEL), 1.0),
        "x_sample": nrm(ks[1], (DEC_BATCH, DEC_SEQ, D_MODEL), 1.0),
        "state_ssm_re": nrm(ks[2], (DEPTH, DEC_BATCH, SSM_GROUPS, SSM_STATE), 0.5),
        "state_ssm_im": nrm(ks[3], (DEPTH, DEC_BATCH, SSM_GROUPS, SSM_STATE), 0.5),
        "cache_pool": nrm(ks[4], (DEPTH, DEC_BATCH, POOL_HIST, D_POOL), 1.0),
        "ffn1_pre_g": gain(ks[5]),
        "ffn1_w_in": nrm(ks[6], (DEPTH, D_MODEL, 2 * D_FF), D_MODEL ** -0.5),
        "ffn1_w_out": nrm(ks[7], (DEPTH, D_FF, D_MODEL), D_FF ** -0.5),
        "ffn1_post_g": gain(ks[8]),
        "mix_pre_g": gain(ks[9]),
        "w_in": nrm(ks[13], (DEPTH, D_MODEL, D_IN_PROJ), D_MODEL ** -0.5),
        "b_in": nrm(ks[14], (DEPTH, D_IN_PROJ), 0.02),
        "ssm_lambda_re": lam_re,
        "ssm_lambda_im": lam_im,
        "ssm_log_step": log_step,
        "ssm_b_re": nrm(ks[15], (DEPTH, SSM_GROUPS, SSM_STATE, SSM_GROUP_DIM), (2 * SSM_GROUP_DIM) ** -0.5),
        "ssm_b_im": nrm(ks[16], (DEPTH, SSM_GROUPS, SSM_STATE, SSM_GROUP_DIM), (2 * SSM_GROUP_DIM) ** -0.5),
        "ssm_c_re": nrm(ks[17], (DEPTH, SSM_GROUPS, SSM_GROUP_DIM, SSM_STATE), (2 * SSM_STATE) ** -0.5),
        "ssm_c_im": nrm(ks[18], (DEPTH, SSM_GROUPS, SSM_GROUP_DIM, SSM_STATE), (2 * SSM_STATE) ** -0.5),
        "ssm_d": nrm(ks[19], (DEPTH, D_SSM), 1.0),
        "ssm_w_glu": nrm(ks[20], (DEPTH, D_SSM, 2 * D_MODEL), D_SSM ** -0.5),
        "ssm_b_glu": nrm(ks[21], (DEPTH, 2 * D_MODEL), 0.02),
        "pool_w": nrm(ks[22], (DEPTH, POOL_GROUPS, POOL_GROUP_DIM, POOL_OUT_DIM), POOL_GROUP_DIM ** -0.5),
        "pool_scale": 1.0 + 0.1 * jax.random.normal(ks[23], (DEPTH, D_MODEL), f32),
        "w_out": nrm(ks[24], (DEPTH, D_MODEL, D_MODEL), D_MODEL ** -0.5),
        "mix_post_g": gain(ks[25]),
        "ffn2_pre_g": gain(ks[26]),
        "ffn2_w_in": nrm(ks[27], (DEPTH, D_MODEL, 2 * D_FF), D_MODEL ** -0.5),
        "ffn2_w_out": nrm(ks[28], (DEPTH, D_FF, D_MODEL), D_FF ** -0.5),
        "ffn2_post_g": gain(ks[29]),
    }

def reference(x_prompt, x_sample, state_ssm_re, state_ssm_im, cache_pool,
              ffn1_pre_g, ffn1_w_in, ffn1_w_out, ffn1_post_g, mix_pre_g, w_in, b_in,
              ssm_lambda_re, ssm_lambda_im, ssm_log_step, ssm_b_re, ssm_b_im, ssm_c_re, ssm_c_im,
              ssm_d, ssm_w_glu, ssm_b_glu, pool_w, pool_scale, w_out, mix_post_g,
              ffn2_pre_g, ffn2_w_in, ffn2_w_out, ffn2_post_g):
    hp = x_prompt
    hs = x_sample
    pr_re, pr_im, pr_pool, sm_re, sm_im, sm_pool = [], [], [], [], [], []
    for l in range(DEPTH):
        p = {
            "ffn1_pre_g": ffn1_pre_g[l], "ffn1_w_in": ffn1_w_in[l], "ffn1_w_out": ffn1_w_out[l],
            "ffn1_post_g": ffn1_post_g[l], "mix_pre_g": mix_pre_g[l], "w_in": w_in[l], "b_in": b_in[l],
            "ssm_lambda_re": ssm_lambda_re[l], "ssm_lambda_im": ssm_lambda_im[l],
            "ssm_log_step": ssm_log_step[l], "ssm_b_re": ssm_b_re[l], "ssm_b_im": ssm_b_im[l],
            "ssm_c_re": ssm_c_re[l], "ssm_c_im": ssm_c_im[l], "ssm_d": ssm_d[l],
            "ssm_w_glu": ssm_w_glu[l], "ssm_b_glu": ssm_b_glu[l], "pool_w": pool_w[l],
            "pool_scale": pool_scale[l], "w_out": w_out[l], "mix_post_g": mix_post_g[l],
            "ffn2_pre_g": ffn2_pre_g[l], "ffn2_w_in": ffn2_w_in[l], "ffn2_w_out": ffn2_w_out[l],
            "ffn2_post_g": ffn2_post_g[l],
        }
        hp, s_re, s_im, s_pool = encoder_layer(hp, None, None, None, 0, p)
        pr_re.append(s_re)
        pr_im.append(s_im)
        pr_pool.append(s_pool)
        hs, s_re, s_im, s_pool = encoder_layer(hs, state_ssm_re[l], state_ssm_im[l], cache_pool[l], PAST_LEN, p)
        sm_re.append(s_re)
        sm_im.append(s_im)
        sm_pool.append(s_pool)
    return (hp, hs, jnp.stack(pr_re), jnp.stack(pr_im), jnp.stack(pr_pool),
            jnp.stack(sm_re), jnp.stack(sm_im), jnp.stack(sm_pool))


_drawn_inputs = setup_inputs


def setup_inputs(seed=0):
    import zlib

    import numpy as np

    out = dict(_drawn_inputs(seed))
    spreads = {}
    factors = {'ssm_lambda_re': 55.56, 'ssm_b_glu': 6.942, 'ffn2_post_g': 3.711}
    for name, (base, spread) in spreads.items():
        noise = np.random.default_rng([zlib.crc32(name.encode()), seed]).standard_normal(out[name].shape)
        drawn = base * np.exp(spread * noise) if base else spread * noise
        out[name] = jnp.asarray(drawn.astype(out[name].dtype))
    for name, factor in factors.items():
        out[name] = (out[name] * factor).astype(out[name].dtype)
    return out
```

```python
from contextlib import ExitStack
from math import pi, sqrt

import numpy as np

import concourse.bass as bass
from concourse import mybir

F32 = mybir.dt.float32
F32R = mybir.dt.float32r
I32 = mybir.dt.int32
ACT = mybir.ActivationFunctionType
ALU = mybir.AluOpType
ds = bass.ds

P = 128
D = 1024
DT = D // P
DFF = 2816
HT = DFF // P
SEQ, DEC = 1024, 32
L = 8
KP, KS = SEQ // L, DEC // L
K = KP + KS
T = L * K
NB = 3
BW = T // NB
G, GC, NS = 32, 16, 64
NPAIR = G // 2
DS = 512
HIST = 15
EPS = 1e-6
RAW_SLOTS, SPLIT_SLOTS = 3, 3
WU = D

V_PRE1, V_POST1, V_PREM, V_POSTM, V_PRE2, V_POST2, V_PSC, V_BIN, V_BGLU, V_D = 0, 8, 16, 24, 32, 40, 48, 56, 80, 96


class Along:

    def __init__(self, i, n, a, b):
        self.i, self.n, self.a, self.b = i, n, a, b

    def __add__(self, k):
        return Along(self.i, self.n, self.a, self.b + k)


def of(f, x):
    if not isinstance(x, Along):
        return f(x)
    v = [f(x.a * k + x.b) for k in range(x.n)]
    step = v[1] - v[0]
    assert all(q - p == step for p, q in zip(v, v[1:])), v
    return v[0] if step == 0 else x.i * step + v[0]


class Plan:

    def __init__(self):
        self.unit, self.block, self.last = {}, {}, []
        self.n = 0

    def add(self, key, units, blocks_of_unit, together=False):
        self.unit[key], self.block[key] = len(self.last), self.n
        for _ in range(units):
            self.n += 0 if together else blocks_of_unit
            self.last.append(self.n)
        if together:
            self.n += blocks_of_unit
            for u in range(units):
                self.last[-1 - u] = self.n


def groups(n):
    order = [("in", 0)]
    for g in range(1, n):
        order += [("in", g), ("out", g - 1)]
    return order + [("out", n - 1)]


FG = HT // 2
MG = DT // 2
plan = Plan()
for f in (1, 2):
    if f == 2:
        for t in range(4):
            plan.add(("mix", t), 6, NB)
        plan.add("pool", 1, NB * DT)
        for what, g in groups(MG):
            plan.add(("glu" if what == "in" else "merge", g), 2, *((NB,) if what == "in" else (NB * DT, True)))
    for what, g in groups(FG):
        plan.add((f, what, g), *((4, NB) if what == "in" else (2, NB * DT, True)))
UNITS = len(plan.last)


def layer(nc, a, outs):
    (y_prompt, y_sample, re_prompt, im_prompt, pool_prompt, re_sample, im_sample, pool_sample) = outs
    ctx = ExitStack()
    with ctx:
        def sb(name, shape, dt=F32, on=ctx):
            return on.enter_context(nc.sbuf_tensor(name, shape, dt))

        def sem(name):
            return ctx.enter_context(nc.semaphore(name))

        def scratch(name, shape):
            return nc.dram_tensor(name, shape, F32, kind="Internal").ap()

        h_dram = scratch("h_dram", (P, DT, T))
        u_dram = scratch("u_dram", (4, P, T))
        gate_dram = scratch("gate_dram", (2 * DT, P, T))
        prod_dram = scratch("prod_dram", (DT, P, T))
        taps_dram = scratch("taps_dram", (P, 2 * P))
        yhi_dram = scratch("yhi_dram", (DS, L, K))
        ylo_dram = scratch("ylo_dram", (DS, L, K))

        w_raw = sb("w_raw", [P, RAW_SLOTS, WU])
        w_hi = sb("w_hi", [P, SPLIT_SLOTS, WU], F32R)
        w_lo = sb("w_lo", [P, SPLIT_SLOTS, WU], F32R)
        rstd = sb("rstd", [P, T])
        ident = sb("ident", [P, P])
        ones = sb("ones", [P, P])
        vecs = sb("vecs", [P, P])
        ta = sb("ta", [P, 2, BW])
        tb = sb("tb", [P, 2, BW])
        std = sb("std", [P, BW])
        rpost = sb("rpost", [P, BW])
        sq = sb("sq", [P, 2, BW])
        ssum = sb("ssum", [P, 2, BW])
        epsc = sb("epsc", [P, 1])

        with ExitStack() as s:
            yrow = sb("yrow", [P, 4, D], F32, s)
        z_hi = sb("z_hi", [P, DT, T], F32R)
        z_lo = sb("z_lo", [P, DT, T], F32R)
        y_hi, y_lo, pl_hi, pl_lo = z_hi[:, 0:4], z_lo[:, 0:4], z_hi[:, 4:8], z_lo[:, 4:8]

        with ExitStack() as s:
            hid_hi = sb("hid_hi", [P, 4, T], F32R, s)
            hid_lo = sb("hid_lo", [P, 4, T], F32R, s)
            acc = sb("acc", [P, DT, T], F32, s)
            xres = sb("xres", [P, DT, T], F32, s)
        with ExitStack() as s:
            xrow = sb("xrow", [P, 9, D], F32, s)
            vrow = sb("vrow", [P, P], F32, s)
        with ExitStack() as s:
            gp_in = sb("gp_in", [P, 2, T], F32, s)
            gp_out = sb("gp_out", [P, 2, T], F32, s)
        with ExitStack() as s:
            srow = sb("srow", [P, P], F32, s)
            crow = sb("crow", [P, 2, 4, 2, NS], F32, s)
            lsrow = sb("lsrow", [P, 2], F32, s)
            sp_ = sb("sp_", [P, 80], F32, s)
            sm = sb("sm", [P, 34, NPAIR], F32, s)
            smi = sb("smi", [P, NPAIR], I32, s)
            apw = sb("apw", [P, 2, NPAIR, 9], F32, s)
            arev = sb("arev", [P, 2, NPAIR, 8], F32, s)
            braw = sb("braw", [P, 2, NPAIR, GC], F32, s)
            bb = sb("bb", [P, 2, NPAIR, GC], F32, s)
            cc = sb("cc", [P, 2, NPAIR, GC], F32, s)
            wlo = sb("wlo", [P, 2, NPAIR, 16], F32, s)
            whi = sb("whi", [P, 2, NPAIR, 8], F32, s)
            ctmp = sb("ctmp", [P, 2, NPAIR * GC], F32, s)
            hfin = sb("hfin", [P, 4, NPAIR], F32, s)
            hfrow = sb("hfrow", [64, P], F32, s)
            mask = sb("mask", [P, K], F32, s)
            hrow = sb("hrow", [16, DS], F32, s)
            hcol = sb("hcol", [P, 4, 16], F32, s)
            cnt = sb("cnt", [P, 4, 16], F32, s)
            pt = sb("pt", [P, 2, 4, L, GC], F32, s)
            qt = sb("qt", [P, 2, 4, L + 1, GC], F32, s)
            mtmp = sb("mtmp", [P, 2, 4, (L + 1) * GC], F32, s)
            bbst = sb("bbst", [P, 2, 4, 2, GC], F32, s)
            bint = sb("bint", [P, 2, 4, P], F32, s)
            taps = sb("taps", [P, 2 * P], F32, s)
            toep = sb("toep", [P, 8, P], F32, s)
            ur = sb("ur", [P, 8, K], F32, s)
            wt = sb("wt", [P, 2, 4, K], F32, s)
            dec = sb("dec", [P, 4, K], F32, s)
            dst_ = sb("dst_", [P, 8], F32, s)
            bst = sb("bst", [P, 6], F32, s)
            r1 = sb("r1", [P, 2, K], F32, s)
            r2 = sb("r2", [P, 2, K], F32, s)
            r3 = sb("r3", [P, 2, K], F32, s)
            r4 = sb("r4", [P, 2, K], F32, s)
            vr = sb("vr", [P, 2, K], F32, s)
            vi = sb("vi", [P, 2, K], F32, s)
            hb = sb("hb", [P, 2, 2, K + 1], F32, s)
            yv = sb("yv", [P, 4, K], F32, s)
            ya = sb("ya", [P, 4, K], F32, s)
            yhs = sb("yhs", [P, 4, K], F32R, s)
            yls = sb("yls", [P, 4, K], F32R, s)
            up = sb("up", [P, 4 * T], F32, s)
            ext = sb("ext", [P, L, K + 4], F32, s)
            sum_a = sb("sum_a", [P, L, K + 4], F32, s)
            tail = sb("tail", [P, 4, 2, 16], F32, s)
        mt = [ta[:, 0, :], ta[:, 1, :], tb[:, 0, :]]
        og = [tb[:, 1, :], std[:, :], rpost[:, :]]
        prow = mtmp[0:16].rearrange("p a b c -> p (a b c)")[:, 0:2 * DS].rearrange("p (w d) -> p w d", w=2)

        bank = [ctx.enter_context(nc.psum_tensor(f"bank{i}", [P, 512], F32)) for i in range(8)]
        PA, PB, PC = bank[0:3], bank[3:6], bank[6:8]

        w_loaded = [sem(f"w_loaded{i}") for i in range(RAW_SLOTS)]
        glu_value_loaded = sem("glu_value_loaded")
        w_hi_done, w_ready, pe_block = sem("w_hi_done"), sem("w_ready"), sem("pe_block")
        const_ready, vec_loaded = sem("const_ready"), sem("vec_loaded")
        vec_mm, vec_ready = sem("vec_mm"), sem("vec_ready")
        x_loaded = [sem(f"x_loaded{i}") for i in range(9)]
        x_turned, x_dve, x_act = sem("x_turned"), sem("x_dve"), sem("x_act")
        sq_done, sum_done, stat_done, std_done, recip_done = (sem(n) for n in ("sq_done", "sum_done", "stat_done", "std_done", "recip_done"))
        zhi_done, z_ready, h_done, t_done = sem("zhi_done"), sem("z_ready"), sem("h_done"), sem("t_done")
        acc_zero, acc_done = sem("acc_zero"), sem("acc_done")
        in_free, ta_done, silu_done, h_mul, hid_hi_done, hid_ready, out_free = (
            {f: sem(f"{n}{f}") for f in (1, 2, 3)} for n in ("in_free", "ta_done", "silu_done", "h_mul", "hid_hi_done", "hid_ready", "out_free"))
        h_spilled, h_back = sem("h_spilled"), sem("h_back")
        own = {n: sem(f"{n}_step") for n in ("dve_prep", "dve_mix", "dve_pool", "act_prep", "pool_prep")}
        sp_loaded, sp_mm, sp_ev = sem("sp_loaded"), sem("sp_mm"), sem("sp_ev")
        prep_act, prep_dve = sem("prep_act"), sem("prep_dve")
        m_scaled, m_out = sem("m_scaled"), sem("m_out")
        m_stored = [sem(f"m_stored{b}") for b in range(NB)]
        pq_ready, prep_mm, prep_ev = sem("pq_ready"), sem("prep_mm"), sem("prep_ev")
        taps_stored, toep_loaded, ur_loaded = sem("taps_stored"), sem("toep_loaded"), sem("ur_loaded")
        e_mm, e_read, hb_ready, y_mm, y_ev, gelu_in, sig_done, y_full, yhs_done, yls_done, y_stored = (
            sem(n) for n in ("e_mm", "e_read", "hb_ready", "y_mm", "y_ev", "gelu_in", "sig_done", "y_full", "yhs_done", "yls_done", "y_stored"))
        y_loaded, pooled, pl_hi_done, pl_ready = sem("y_loaded"), sem("pooled"), sem("pl_hi_done"), sem("pl_ready")
        hist_mm, hist_ev, tail_ready, last_mm, last_ev = sem("hist_mm"), sem("hist_ev"), sem("tail_ready"), sem("last_mm"), sem("last_ev")
        gp_loaded = [sem(f"gp_loaded{i}") for i in range(2)]
        gp_stored = [sem(f"gp_stored{i}") for i in range(2)]
        pool_free, gp_done = sem("pool_free"), sem("gp_done")
        side_loaded = [sem(f"side_loaded{i}") for i in range(2)]
        sig_m, merge_a, merge_t, merge_read = sem("sig_m"), sem("merge_a"), sem("merge_t"), sem("merge_read")
        dcol_done, y_turned, yrow_ready = sem("dcol_done"), sem("y_turned"), sem("yrow_ready")
        y_out = [sem(f"y_out{i}") for i in range(4)]
        state_out = sem("state_out")

        block = ctx.enter_context(nc.Block())
        cols = lambda b: slice(b * BW, (b + 1) * BW)

        def unit_source(key, g, q):
            if isinstance(key, tuple) and key[0] in (1, 2):
                f, what = key
                if what == "in":
                    c = of(lambda x: (2 * x + q // 2) * P + (q % 2) * DFF, g)
                    return a[f"ffn{f}_w_in"].rearrange("(k p) n -> p k n", p=P)[:, :, ds(c, P)], "k"
                return a[f"ffn{f}_w_out"][ds(of(lambda x: (2 * x + q) * P, g), P), :], None
            if key == "mix":
                c = of(lambda x: (x * P, 4 * P + x * P)[q] if q < 2 else 8 * P + (4 * x + q - 2) * P, g)
                return a["w_in"].rearrange("(k p) n -> p k n", p=P)[:, :, ds(c, P)], "k"
            if key == "pool":
                return a["pool_w"].rearrange("g c o -> c g o"), "g"
            if key == "glu":
                c = (2 * g + q) * P
                return a["ssm_w_glu"].rearrange("(k p) (h n) -> p k h n", p=P, h=2)[:, :, :, c:c + P], "kh"
            return a["w_out"][(2 * g + q) * P:(2 * g + q + 1) * P, :], None

        def load_unit(sp, key, g, q):
            name = key if isinstance(key, tuple) else (key,)
            u_of = lambda x: plan.unit[(*name, x) if key != "pool" else "pool"] + q
            slot = of(lambda x: u_of(x) % RAW_SLOTS, g)
            if isinstance(g, Along) or u_of(g) >= RAW_SLOTS:
                sp.wait_ge(w_ready, of(lambda x: u_of(x) - RAW_SLOTS + 1, g))
            src, form = unit_source(key, g, q)
            dst = w_raw[:, slot, :]
            if form == "k":
                dst = dst.rearrange("p (k n) -> p k n", k=DT)
            elif form == "g":
                dst = dst.rearrange("p (g o) -> p g o", g=4)
            elif form == "kh":
                dst = dst.rearrange("p (k h n) -> p k h n", k=4, h=2)
                sp.dma_start(dst[:, :, 0, :], src[:, :, 0, :]).then_inc(glu_value_loaded, 16)
                sp.wait_ge(glu_value_loaded, 16 * (2 * g + q + 1))
                sp.dma_start(dst[:, :, 1, :], src[:, :, 1, :]).then_inc(w_loaded[slot], 16)
                return
            sp.dma_start(dst, src).then_inc(w_loaded[slot], 16)

        def loaded_value(u):
            return 16 * (u // RAW_SLOTS + 1)

        def split_hi(act, u):
            slot = of(lambda x: x % RAW_SLOTS, u)
            out = of(lambda x: x % SPLIT_SLOTS, u)
            act.wait_ge(w_loaded[slot], of(loaded_value, u))
            if isinstance(u, Along) or u >= SPLIT_SLOTS:
                act.wait_ge(pe_block, of(lambda x: plan.last[x - SPLIT_SLOTS], u))
            nc.scalar.activation(w_hi[:, out, :], w_raw[:, slot, :], ACT.Copy).then_inc(w_hi_done, 1)

        def split_lo(dve, u):
            slot = of(lambda x: x % RAW_SLOTS, u)
            out = of(lambda x: x % SPLIT_SLOTS, u)
            dve.wait_ge(w_hi_done, of(lambda x: x + 1, u))
            nc.vector.tensor_tensor(w_lo[:, out, :], w_raw[:, slot, :], w_hi[:, out, :].bitcast(F32),
                                    ALU.subtract).then_inc(w_ready, 1)

        def three(out, lhs, rhs, first, last):
            (lh, ll), (rh, rl) = lhs, rhs
            nc.tensor.matmul(out, lh, rh, start=first, stop=False)
            nc.tensor.matmul(out, lh, rl, start=False, stop=False)
            return nc.tensor.matmul(out, ll, rh, start=False, stop=last)

        def wslices(slot, lo, hi):
            return w_hi[:, slot, lo:hi], w_lo[:, slot, lo:hi]

        def job(stage, kind, b):
            return {0: 0, 1: 3, 2: 9, 3: 15}[stage] + (3 if kind == "h" and stage else 0) + b

        def square(act, J, m, src):
            need = {0: 7 * (J - 1) + 6, 1: 7 * (J - 1) + 7, 2: 7 * J + 1}.get(m, 7 * J + m - 2)
            if need > 0:
                act.wait_ge(sum_done, need)
            nc.scalar.activation(sq[:, m % 2, :], src, ACT.Square).then_inc(sq_done, 1)

        def add_squares(pool, J):
            for m in range(1, DT):
                pool.wait_ge(sq_done, DT * J + m + 1)
                if m == 1 and J >= 2:
                    pool.wait_ge(stat_done, J - 1)
                if m > 1:
                    pool.wait_ge(sum_done, 7 * J + m - 1)
                nc.gpsimd.tensor_tensor(ssum[:, J % 2, :], sq[:, 0, :] if m == 1 else ssum[:, J % 2, :],
                                        sq[:, m % 2, :], ALU.add).then_inc(sum_done, 1)

        def stat(pe, J, out, free=None):
            pe.wait_ge(sum_done, 7 * J + 7)
            if free is not None:
                pe.wait_ge(*free)
            nc.tensor.matmul(out[:, 0:BW], ones[:, :], ssum[:, J % 2, :], start=True, stop=True).then_inc(stat_done, 1)

        def root(act, J, src):
            act.wait_ge(stat_done, J + 1)
            if J:
                act.wait_ge(recip_done, J)
            nc.scalar.activation(std[:, :], src[:, 0:BW], ACT.Sqrt, bias=epsc[:, 0:1], scale=1.0 / D).then_inc(std_done, 1)

        def recip(dve, J, dst):
            dve.wait_ge(std_done, J + 1)
            nc.vector.reciprocal(dst, std[:, :]).then_inc(recip_done, 1)

        STAT_H = [PC[0], PC[1], PC[0]]

        def z_hi_part(act, stage, b, m, gain):
            if stage:
                act.wait_ge(h_done, 24 * (stage - 1) + 8 * b + m + 1)
            nc.scalar.activation(z_hi[:, m, cols(b)], xres[:, m, cols(b)], ACT.Copy,
                                 scale=vecs[:, gain + m:gain + m + 1]).then_inc(zhi_done, 1)

        def z_lo_part(dve, stage, b, m, gain):
            dve.wait_ge(zhi_done, 24 * stage + 8 * b + m + 1)
            nc.vector.scalar_tensor_tensor(z_lo[:, m, cols(b)], xres[:, m, cols(b)], vecs[:, gain + m:gain + m + 1],
                                           z_hi[:, m, cols(b)].bitcast(F32), ALU.mult, ALU.subtract).then_inc(z_ready, 1)

        GAIN = {0: V_PRE1, 1: V_PREM, 2: V_PRE2}
        POST = {1: V_POST1, 2: V_POSTM, 3: V_POST2}
        tcount = [0]

        def residual(dve, stage, b):
            for m in range(DT + 1):
                if m < DT:
                    yield ("h", m)
                if m and stage < 3:
                    yield ("z", m - 1)

        def residual_step(dve, stage, b, what, m):
            if what == "z":
                z_lo_part(dve, stage, b, m, GAIN[stage])
                return
            g = POST[stage] + m
            slot = tcount[0] % 2
            nc.vector.scalar_tensor_tensor(ta[:, slot, :], acc[:, m, cols(b)], vecs[:, g:g + 1], rpost[:, :],
                                           ALU.mult, ALU.mult).then_inc(t_done, 1)
            tcount[0] += 1
            dve.wait_ge(t_done, tcount[0])
            if stage == 2 and m == 0:
                dve.wait_ge(h_back, 16 * (b + 1))
            nc.vector.scalar_tensor_tensor(xres[:, m, cols(b)], ta[:, slot, :], 0.5 if stage != 2 else 1.0,
                                           xres[:, m, cols(b)], ALU.mult, ALU.add).then_inc(h_done, 1)

        def out_key(ph, g):
            return (ph, "out", g) if ph != 3 else ("merge", g)

        def in_key(ph, g):
            return (ph, "in", g) if ph != 3 else ("glu", g)

        def pe_out(pe, ph, g, after=None):
            u = of(lambda x: plan.unit[out_key(ph, x)], g)
            s0 = of(lambda x: plan.unit[out_key(ph, x)] % SPLIT_SLOTS, g)
            hs = of(lambda x: 2 * (x % 2), g)
            pe.wait_ge(w_ready, u + 2)
            for b in range(NB):
                pe.wait_ge(hid_ready[ph], of(lambda x: 6 * x + 3 + b + 1, g))
                for m in range(DT):
                    pe.wait_ge(out_free[ph], of(lambda x: 24 * x + 8 * b + m + 25, g))
                    out = PC[m % 2][:, 0:BW]
                    for k in range(2):
                        mm = three(out, wslices((s0 + k) % SPLIT_SLOTS, m * P, m * P + P),
                                   (hid_hi[:, hs + k, cols(b)], hid_lo[:, hs + k, cols(b)]), k == 0, k == 1)
                    mm.then_inc(pe_block, 1)
                if after:
                    after(b)

        def dve_out(dve, ph, g, b, m):
            dve.wait_ge(pe_block, of(lambda x: plan.block[out_key(ph, x)] + 8 * b + m + 1, g))
            dst = acc[:, m, cols(b)]
            dve.wait_ge(out_free[ph], of(lambda x: 24 * x + 8 * b + m + 3, g))
            nc.vector.tensor_tensor(dst, dst, PC[m % 2][:, 0:BW], ALU.add).then_inc(out_free[ph], 1)

        def last_group(ph):
            return (FG if ph != 3 else MG) - 1

        def stage_of(ph):
            return {1: 1, 3: 2, 2: 3}[ph]

        def pe_last(pe, ph):
            st = stage_of(ph)

            def after(b):
                if b == 1:
                    stat(pe, job(st, "acc", 0), PA[0])
                if b == 2:
                    stat(pe, job(st, "acc", 1), PA[1])
                    stat(pe, job(st, "acc", 2), PA[2])
            pe_out(pe, ph, last_group(ph), after)

        def dve_last(dve, ph, next_units):
            st, g = stage_of(ph), last_group(ph)
            for b in range(2):
                for m in range(DT):
                    dve_out(dve, ph, g, b, m)
            recip(dve, job(st, "acc", 0), rpost[:, :])
            dve.wait_ge(recip_done, job(st, "acc", 0) + 1)
            if st < 3:
                split_lo(dve, out_unit(ph, g) + 2)
            steps = list(residual(dve, st, 0))
            for m in range(DT):
                dve_out(dve, ph, g, 2, m)
                for s in steps[2 * m:2 * m + 2]:
                    residual_step(dve, st, 0, *s)
            for s in steps[2 * DT:]:
                residual_step(dve, st, 0, *s)
            for b in (1, 2):
                recip(dve, job(st, "acc", b), rpost[:, :])
                if b == 2:
                    for u in next_units:
                        split_lo(dve, u)
                dve.wait_ge(recip_done, job(st, "acc", b) + 1)
                for s in residual(dve, st, b):
                    residual_step(dve, st, b, *s)

        def act_last(act, ph, next_units):
            st, g = stage_of(ph), last_group(ph)

            def sqa(b, m):
                act.wait_ge(out_free[ph], 24 * g + 8 * b + m + 1 + 26)
                square(act, job(st, "acc", b), m, acc[:, m, cols(b)])
            for b in range(2):
                for m in range(DT):
                    sqa(b, m)
            if st < 3:
                split_hi(act, out_unit(ph, g) + 2)
            root(act, job(st, "acc", 0), PA[0])
            for m in range(DT):
                sqa(2, m)
                if st < 3:
                    z_hi_part(act, st, 0, m, GAIN[st])
            root(act, job(st, "acc", 1), PA[1])
            if st < 3:
                for m in range(DT):
                    z_hi_part(act, st, 1, m, GAIN[st])
            root(act, job(st, "acc", 2), PA[2])
            for u in next_units:
                split_hi(act, u)
            if st < 3:
                for m in range(DT):
                    z_hi_part(act, st, 2, m, GAIN[st])
                    square(act, job(st, "h", 0), m, xres[:, m, cols(0)])
                for m in range(DT):
                    square(act, job(st, "h", 1), m, xres[:, m, cols(1)])
                if st == 1:
                    root(act, job(st, "h", 0), STAT_H[0])
                for m in range(DT):
                    square(act, job(st, "h", 2), m, xres[:, m, cols(2)])
                if st == 1:
                    root(act, job(st, "h", 1), STAT_H[1])
                    root(act, job(st, "h", 2), STAT_H[2])

        def pool_stage(pool, st):
            for b in range(NB):
                add_squares(pool, job(st, "acc", b))
            if st == 1:
                pool.wait_ge(pe_block, plan.block[("mix", 0)])
                nc.gpsimd.memset(hrow[:, :], 0.0).then_inc(const_ready, 1)
            if st < 3:
                for b in range(NB):
                    add_squares(pool, job(st, "h", b))

        def stats_h(pe, stage, b):
            J = job(stage, "h", b)
            stat(pe, J, STAT_H[b], (std_done, J - 1) if b == 2 else None)

        def pe_in(pe, f, g, hooks=None):
            z_all = 24 * (1 if f == 1 else 3)
            for q in range(4):
                u = of(lambda x: plan.unit[(f, "in", x)] + q, g)
                slot = of(lambda x: (plan.unit[(f, "in", x)] + q) % SPLIT_SLOTS, g)
                pe.wait_ge(w_ready, u + 1)
                for b in range(NB):
                    out = (PA, PB)[q % 2][b][:, 0:BW]
                    if q % 2 == 0:
                        pe.wait_ge(in_free[f], of(lambda x: 3 * (2 * x + q // 2) + b + 1, g))
                    if hooks and q == 0:
                        pe.wait_ge(z_ready, z_all - 24 + 8 * b + 8)
                    for k in range(DT):
                        mm = three(out, wslices(slot, k * P, k * P + P), (z_hi[:, k, cols(b)], z_lo[:, k, cols(b)]),
                                   k == 0, k == DT - 1)
                    mm.then_inc(pe_block, 1)
                    if hooks and (q, b) in hooks:
                        hooks[q, b]()

        def pe_ffn(pe, f):
            st = 0 if f == 1 else 2
            pe_in(pe, f, 0, {(0, 0): lambda: stats_h(pe, st, 0), (0, 1): lambda: stats_h(pe, st, 1),
                             (1, 0): lambda: stats_h(pe, st, 2)})
            pe_in(pe, f, 1)
            with pe.Fori(0, 4) as i:
                g = Along(i, 4, 2, 0)
                pe_out(pe, f, g)
                pe_in(pe, f, g + 2)
                pe_out(pe, f, g + 1)
                pe_in(pe, f, g + 3)
            pe_out(pe, f, 8)
            pe_in(pe, f, 10)
            pe_out(pe, f, 9)
            pe_last(pe, f)

        def tile_blocks(g):
            return [(j, b, of(lambda x: 3 * (2 * x + j) + b, g)) for j in range(2) for b in range(NB)]

        def dve_ffn_in(dve, f, g, before=None):
            for j, b, n in tile_blocks(g):
                if b == 0:
                    for q in (0, 1):
                        split_lo(dve, unit_along(f, g, 2 * j + q + 2))
                if before and j == 0:
                    before(b)
                dve.wait_ge(pe_block, of(lambda x: plan.block[(f, "in", x)] + 6 * j + 3 + b + 1, g))
                s = (3 * j + b) % 2
                nc.vector.tensor_tensor(ta[:, s, :], PA[b][:, 0:BW], rstd[:, cols(b)], ALU.mult).then_inc(ta_done[f], 1)
                nc.vector.tensor_tensor(tb[:, s, :], PB[b][:, 0:BW], rstd[:, cols(b)], ALU.mult).then_inc(in_free[f], 1)
                dve.wait_ge(silu_done[f], n + 1)
                dve.wait_ge(in_free[f], n + 1 + 3)
                nc.vector.tensor_tensor(tb[:, s, :], tb[:, s, :], ta[:, s, :], ALU.mult).then_inc(h_mul[f], 1)
                dve.wait_ge(hid_hi_done[f], n + 1)
                hs = of(lambda x: 2 * (x % 2) + j, g)
                nc.vector.tensor_tensor(hid_lo[:, hs, cols(b)], tb[:, s, :], hid_hi[:, hs, cols(b)].bitcast(F32),
                                        ALU.subtract).then_inc(hid_ready[f], 1)

        def unit_along(f, g, ahead):
            if isinstance(g, Along):
                v = [plan.unit[(f, "in", g.a * k + g.b)] + ahead for k in range(g.n)]
                return Along(g.i, g.n, v[1] - v[0], v[0])
            return plan.unit[(f, "in", g)] + ahead

        def act_ffn_in(act, f, g, first=False, before=None):
            for j, b, n in tile_blocks(g):
                if b == 0:
                    for q in (0, 1):
                        split_hi(act, unit_along(f, g, 2 * j + q + 2))
                s = (3 * j + b) % 2
                if before and j == 0:
                    before(b)
                act.wait_ge(ta_done[f], n + 1)
                nc.scalar.activation(ta[:, s, :], ta[:, s, :], ACT.Silu).then_inc(silu_done[f], 1)
                act.wait_ge(h_mul[f], n + 1)
                if not first and j == 0 and b == 0:
                    act.wait_ge(pe_block, of(lambda x: plan.block[(f, "out", x - 2)] + 24, g))
                hs = of(lambda x: 2 * (x % 2) + j, g)
                nc.scalar.activation(hid_hi[:, hs, cols(b)], tb[:, s, :], ACT.Copy).then_inc(hid_hi_done[f], 1)

        def out_unit(ph, g):
            if isinstance(g, Along):
                v = [plan.unit[out_key(ph, g.a * k + g.b)] for k in range(g.n)]
                return Along(g.i, g.n, v[1] - v[0], v[0])
            return plan.unit[out_key(ph, g)]

        def dve_outs(dve, ph, g):
            split_lo(dve, out_unit(ph, g) + 2)
            for b in range(NB):
                for m in range(DT):
                    dve_out(dve, ph, g, b, m)
            split_lo(dve, out_unit(ph, g) + 3)

        def act_outs(act, ph, g):
            split_hi(act, out_unit(ph, g) + 2)
            split_hi(act, out_unit(ph, g) + 3)

        def dve_ffn(dve, f, before, next_units):
            if f == 2:
                dve.sem_inc(in_free[f], 3)
            dve_ffn_in(dve, f, 0, before)
            dve_ffn_in(dve, f, 1)
            dve.wait_ge(acc_zero, 1 if f == 1 else 3)
            dve.sem_inc(out_free[f], 26)
            with dve.Fori(0, 4) as i:
                g = Along(i, 4, 2, 0)
                dve_outs(dve, f, g)
                dve_ffn_in(dve, f, g + 2)
                dve_outs(dve, f, g + 1)
                dve_ffn_in(dve, f, g + 3)
            dve_outs(dve, f, 8)
            dve_ffn_in(dve, f, 10)
            dve_outs(dve, f, 9)
            dve_last(dve, f, next_units)

        def act_ffn(act, f, next_units):
            st = 0 if f == 1 else 2
            act_ffn_in(act, f, 0, True, lambda b: root(act, job(st, "h", b), STAT_H[b]))
            act_ffn_in(act, f, 1, True)
            with act.Fori(0, 4) as i:
                g = Along(i, 4, 2, 0)
                act_outs(act, f, g)
                act_ffn_in(act, f, g + 2)
                act_outs(act, f, g + 1)
                act_ffn_in(act, f, g + 3)
            act_outs(act, f, 8)
            act_ffn_in(act, f, 10)
            act_outs(act, f, 9)
            act_last(act, f, next_units)

        def sp_ffn(sp, f, skip=0):
            def ins(g, start=0):
                for q in range(start, 4):
                    load_unit(sp, (f, "in"), g, q)

            def outs(g):
                for q in range(2):
                    load_unit(sp, (f, "out"), g, q)
            ins(0, skip)
            ins(1)
            with sp.Fori(0, 4) as i:
                g = Along(i, 4, 2, 0)
                outs(g)
                ins(g + 2)
                outs(g + 1)
                ins(g + 3)
            outs(8)
            ins(10)
            outs(9)
            outs(10)

        def vec_rows(sp):
            names = [("ffn1_pre_g", V_PRE1), ("ffn1_post_g", V_POST1), ("mix_pre_g", V_PREM), ("mix_post_g", V_POSTM),
                     ("ffn2_pre_g", V_PRE2), ("ffn2_post_g", V_POST2), ("pool_scale", V_PSC), ("b_in", V_BIN),
                     ("ssm_b_glu", V_BGLU)]
            for name, r in names:
                n = a[name].shape[0] // P
                sp.dma_start(vrow[r:r + n, :], a[name].rearrange("(n p) -> n p", p=P)).then_inc(vec_loaded, 16)
            for t in range(L):
                sp.dma_start(vrow[V_D:V_D + G, t * GC:(t + 1) * GC],
                             a["ssm_d"].rearrange("(g c) -> g c", c=GC)).then_inc(vec_loaded, 16)
            return 16 * (len(names) + L)
        VEC_DMAS = 16 * 17
        ORDER = [8, 0, 1, 2, 3, 4, 5, 6, 7]

        def sp_start(sp):
            xp = a["x_prompt"].rearrange("(k s) d -> s k d", s=L)
            for n, tile in enumerate(ORDER):
                if tile == 8:
                    sp.dma_start(xrow[0:DEC, 8, :], a["x_sample"]).then_inc(x_loaded[8], 16)
                else:
                    sp.dma_start(xrow[:, tile, :], xp[tile]).then_inc(x_loaded[tile], 16)
                if n == 1:
                    vec_rows(sp)
                if n == 3:
                    for q in range(3):
                        load_unit(sp, (1, "in"), 0, q)

        def pe_start(pe):
            pe.wait_ge(const_ready, 5)
            pe.wait_ge(vec_loaded, VEC_DMAS)
            nc.tensor.transpose(PC[0][:, 0:P], vrow[:, :], ident[:, :]).then_inc(vec_mm, 1)
            F = 0
            for tile in ORDER:
                rows = DEC if tile == 8 else P
                pe.wait_ge(x_loaded[tile], 16)
                for half in range(2):
                    if F >= 6:
                        pe.wait_ge(x_dve if F % 2 == 0 else x_act, (F - 6) // 2 + 1)
                    for j in range(4):
                        m = 4 * half + j
                        mm = nc.tensor.transpose(bank[F % 6][:, j * P:j * P + rows], xrow[0:rows, tile, m * P:(m + 1) * P],
                                                 ident[0:rows, 0:rows])
                    mm.then_inc(x_turned, 1)
                    F += 1

        def empty_x(eng, copy, which, done):
            F = 0
            for tile in ORDER:
                for half in range(2):
                    if F % 2 == which:
                        eng.wait_ge(x_turned, F + 1)
                        src = bank[F % 6][:, :].rearrange("p (j t) -> p j t", j=4)
                        dst = xres[:, 4 * half:4 * half + 4, :]
                        if tile < 8:
                            copy(dst[:, :, tile * K:tile * K + KP], src[:, :, 0:P]).then_inc(done, 1)
                        else:
                            for j in range(4):
                                ins = copy(dst[:, j, :].rearrange("p (s k) -> p s k", s=L)[:, :, KP:K],
                                           src[:, j, 0:DEC].rearrange("p (k s) -> p s k", s=L))
                            ins.then_inc(done, 1)
                    F += 1

        S = {n: k for k, n in enumerate("dt mag th n r sn sh cs ar ai den rden nr fr fi t0 t1 p x w2r w2i w4r w4i w8r w8i m2 m4 m8 rhr rhi un lrdt e0 e1".split())}
        LRE, LIM, H0R, H0I, LST = range(0, 80, 16)
        PREP_DMAS = 16 * 14

        def sp_prep(sp):
            sp.wait_ge(pe_block, plan.block[("mix", 0)])
            rows = lambda n: a[n].rearrange("(j g) s -> j (g s)", g=2)
            for r, n in ((LRE, "ssm_lambda_re"), (LIM, "ssm_lambda_im"), (H0R, "state_ssm_re"), (H0I, "state_ssm_im")):
                sp.dma_start(srow[r:r + 16, :], rows(n)).then_inc(sp_loaded, 16)
            sp.dma_start(lsrow[LST:LST + 16, :], a["ssm_log_step"].rearrange("(j g) -> j g", g=2)).then_inc(sp_loaded, 16)
            for c, n in enumerate(("ssm_b_re", "ssm_b_im")):
                sp.dma_start(braw[:, c], a[n].rearrange("(j g) s c -> g s j c", g=2).rearrange("g s j c -> (g s) j c")
                             ).then_inc(sp_loaded, 16)
            for c, n in enumerate(("ssm_c_re", "ssm_c_im")):
                for twice in range(2):
                    sp.dma_start(crow[:, c, :, twice, :], a[n].rearrange("g c s -> (g c) s").rearrange("(t p) s -> p t s", p=P)
                                 ).then_inc(sp_loaded, 16)
            sp.wait_ge(const_ready, 6)
            sp.dma_start(hrow[1:16, :], a["cache_pool"]).then_inc(sp_loaded, 16)
            sp.dma_start(cnt[:, :, :], a["window_counts"]).then_inc(sp_loaded, 16)
            sp.dma_start(mask[:, :], a["scan_mask"]).then_inc(sp_loaded, 16)

        def pe_prep(pe):
            pe.wait_ge(sp_loaded, PREP_DMAS)
            pe.wait_ge(prep_dve, 1)
            nc.tensor.transpose(PB[0][:, 0:80], srow[0:80, :], ident[0:80, 0:80])
            for g in range(4):
                nc.tensor.transpose(PB[0][:, P + 16 * g:P + 16 * g + 16], hrow[:, g * P:(g + 1) * P], ident[0:16, 0:16])
            for c in range(2):
                for t in range(4):
                    mm = nc.tensor.transpose(PB[1 + c][:, t * P:(t + 1) * P],
                                             crow[:, c, t].rearrange("p a s -> p (a s)"), ident[:, :])
            mm.then_inc(sp_mm, 1)

        class Steps:

            def __init__(self, eng, s, i=None, per=0, base=0):
                self.eng, self.s, self.i, self.per, self.base, self.n = eng, s, i, per, base, 0

            def do(self, ins):
                self.n += 1
                ins.then_inc(self.s, 1)

            def sync(self):
                if self.base + self.n > 0 or self.i is not None:
                    v = self.base + self.n
                    self.eng.wait_ge(self.s, v if self.i is None else self.i * self.per + v)

        def take(dst, src):
            return nc.vector.tensor_scalar(dst, src, 1.0, None, ALU.mult)

        def cmul(st, out, x, y, tmp, conj_x=False, neg_im=False):
            tt = nc.vector.tensor_tensor
            (xr, xi), (yr, yi), (t0, t1) = x, y, tmp
            st.do(tt(t0, xr, yr, ALU.mult))
            st.do(tt(t1, xi, yi, ALU.mult))
            st.sync()
            st.do(tt(out[0], t0, t1, ALU.add if conj_x else ALU.subtract))
            st.sync()
            st.do(tt(t0, xr, yi, ALU.mult))
            st.do(tt(t1, xi, yr, ALU.mult))
            st.sync()
            if neg_im:
                st.do(nc.vector.scalar_tensor_tensor(out[1], t0, -1.0, t1, ALU.mult, ALU.subtract))
            else:
                st.do(tt(out[1], t0, t1, ALU.subtract if conj_x else ALU.add))

        v = lambda n: sm[:, S[n], :]
        MAGIC = 12582912.0

        def chain_exp(st, out, x):
            ts, stt = nc.vector.tensor_scalar, nc.vector.scalar_tensor_tensor
            st.sync(); st.do(ts(v("x"), x, -87.0, 87.0, ALU.max, ALU.min))
            st.sync(); st.do(ts(v("t0"), v("x"), 1.4426950408889634, MAGIC, ALU.mult, ALU.add))
            st.sync(); st.do(ts(v("n"), v("t0"), MAGIC, None, ALU.subtract))
            st.sync(); st.do(stt(v("r"), v("n"), -0.693359375, v("x"), ALU.mult, ALU.add))
            st.do(ts(smi[:, :], v("n"), 127.0, 8388608.0, ALU.add, ALU.mult))
            st.sync(); st.do(stt(v("x"), v("n"), 2.12194440054690583e-4, v("r"), ALU.mult, ALU.add))
            st.sync(); st.do(ts(v("p"), v("x"), 1 / 5040, None, ALU.mult))
            for c in (1 / 720, 1 / 120, 1 / 24, 1 / 6, 0.5, 1.0):
                st.sync(); st.do(stt(v("p"), v("p"), c, v("x"), ALU.add, ALU.mult))
            st.sync(); st.do(stt(out, v("p"), 1.0, smi[:, :].bitcast(F32), ALU.add, ALU.mult))

        def dve_prep_a(dve):
            ts, stt, tt, cp = nc.vector.tensor_scalar, nc.vector.scalar_tensor_tensor, nc.vector.tensor_tensor, nc.vector.tensor_copy
            dve.wait_ge(sp_loaded, PREP_DMAS)
            nc.vector.tensor_copy(srow[LST:LST + 16, :].rearrange("j (g s) -> j g s", g=2),
                                  lsrow[LST:LST + 16, :].unsqueeze(2).broadcast_to([16, 2, NS])).then_inc(prep_dve, 1)
            st = Steps(dve, own["dve_prep"])
            dve.wait_ge(sp_mm, 1)
            st.do(cp(sp_[:, :], PB[0][:, 0:80]))
            st.do(cp(hcol[:, :, :].rearrange("p g r -> p (g r)"), PB[0][:, P:P + 64]))
            for c in range(2):
                for h in range(2):
                    half = slice(64 * h, 64 * h + 64)
                    st.do(cp(cc[half, c], PB[1 + c][half, :].rearrange("p (j g c) -> p j g c", g=2, c=GC)[:, :, h, :]))
            chain_exp(st, v("dt"), sp_[:, LST:LST + 16])
            st.sync()
            st.do(tt(v("lrdt"), sp_[:, LRE:LRE + 16], v("dt"), ALU.mult))
            st.do(tt(v("th"), sp_[:, LIM:LIM + 16], v("dt"), ALU.mult))
            chain_exp(st, v("mag"), v("lrdt"))
            st.sync(); st.do(ts(v("t0"), v("th"), 1 / (2 * pi), MAGIC, ALU.mult, ALU.add))
            st.sync(); st.do(ts(v("n"), v("t0"), MAGIC, None, ALU.subtract))
            x = v("th")
            for c in (6.28125, 0.00193500518798828125, 3.0199159819567e-7):
                st.sync(); st.do(stt(v("r"), v("n"), -c, x, ALU.mult, ALU.add))
                x = v("r")
            st.sync(); st.do(ts(v("r"), v("r"), -3.1415925, 3.1415925, ALU.max, ALU.min))
            st.sync()
            dve.sem_inc(prep_dve, 1)
            return st

        def act_prep(act):
            act.wait_ge(prep_dve, 2)
            nc.scalar.activation(v("sn"), v("r"), ACT.Sin).then_inc(prep_act, 1)
            nc.scalar.activation(v("sh"), v("r"), ACT.Sin, scale=0.5).then_inc(prep_act, 1)

        def dve_prep_b(dve, st):
            ts, stt, tt, cp = nc.vector.tensor_scalar, nc.vector.scalar_tensor_tensor, nc.vector.tensor_tensor, nc.vector.tensor_copy
            dve.wait_ge(prep_act, 2)
            st.do(tt(v("t0"), v("sh"), v("sh"), ALU.mult))
            st.sync(); st.do(ts(v("cs"), v("t0"), -2.0, 1.0, ALU.mult, ALU.add))
            st.sync()
            st.do(tt(v("ar"), v("mag"), v("cs"), ALU.mult))
            st.do(tt(v("ai"), v("mag"), v("sn"), ALU.mult))
            lr, li = sp_[:, LRE:LRE + 16], sp_[:, LIM:LIM + 16]
            st.do(tt(v("t0"), lr, lr, ALU.mult))
            st.do(tt(v("t1"), li, li, ALU.mult))
            st.sync()
            st.do(tt(v("den"), v("t0"), v("t1"), ALU.add))
            st.do(ts(v("nr"), v("ar"), 1.0, None, ALU.subtract))
            st.sync(); st.do(nc.vector.reciprocal(v("rden"), v("den")))
            cmul(st, (v("fr"), v("fi")), (lr, li), (v("nr"), v("ai")), (v("t0"), v("t1")), conj_x=True)
            st.sync()
            st.do(tt(v("fr"), v("fr"), v("rden"), ALU.mult))
            st.do(tt(v("fi"), v("fi"), v("rden"), ALU.mult))
            st.sync()
            f3 = lambda n: v(n).unsqueeze(2).broadcast_to([P, NPAIR, GC])
            tmp = [ctmp[:, c, :].rearrange("p (j c) -> p j c", c=GC) for c in range(2)]
            cmul(st, (bb[:, 0], bb[:, 1]), (f3("fr"), f3("fi")), (braw[:, 0], braw[:, 1]), tmp)
            st.do(nc.vector.memset(apw[:, 0, :, 0:1], 1.0))
            st.do(nc.vector.memset(apw[:, 1, :, 0:1], 0.0))
            st.do(cp(apw[:, 0, :, 1:2], v("ar").unsqueeze(2)))
            st.do(cp(apw[:, 1, :, 1:2], v("ai").unsqueeze(2)))

            def powers(tab, lo, n, by):
                st.sync()
                t = [ctmp[:, c, 0:NPAIR * n].rearrange("p (j k) -> p j k", k=n) for c in range(2)]
                cmul(st, [tab[:, c, :, by + 1 if lo else by + 1:by + 1 + n] for c in range(2)],
                     [tab[:, c, :, lo:lo + n] for c in range(2)],
                     [tab[:, c, :, by:by + 1].broadcast_to([P, NPAIR, n]) for c in range(2)], t)
            powers(apw, 1, 1, 1)
            powers(apw, 1, 2, 2)
            powers(apw, 1, 4, 4)
            st.sync()
            for c in range(2):
                for k in range(L):
                    st.do(cp(arev[:, c, :, L - 1 - k:L - k], apw[:, c, :, k:k + 1]))
            x = ("cs", "sn")
            for y in (("w2r", "w2i"), ("w4r", "w4i"), ("w8r", "w8i")):
                st.sync()
                cmul(st, (v(y[0]), v(y[1])), (v(x[0]), v(x[1])), (v(x[0]), v(x[1])), (v("t0"), v("t1")))
                x = y
            x = "mag"
            for y in ("m2", "m4", "m8"):
                st.sync(); st.do(tt(v(y), v(x), v(x), ALU.mult))
                x = y
            st.sync()
            for c, n in enumerate(("w8r", "w8i")):
                st.do(cp(wlo[:, c, :, 0:1], v(n).unsqueeze(2)))
                st.do(nc.vector.memset(whi[:, c, :, 0:1], 1.0 - c))
                st.do(tt(v(("rhr", "rhi")[c]), v("m8"), sp_[:, (H0R, H0I)[c]:(H0R, H0I)[c] + 16], ALU.mult))

            def spread(tab, lo, n, by):
                st.sync()
                t = [ctmp[:, c, 0:NPAIR * n].rearrange("p (j k) -> p j k", k=n) for c in range(2)]
                cmul(st, [tab[:, c, :, by + 1:by + 1 + n] for c in range(2)],
                     [tab[:, c, :, lo:lo + n] for c in range(2)],
                     [tab[:, c, :, by:by + 1].broadcast_to([P, NPAIR, n]) for c in range(2)], t)
            for n in (1, 2, 4, 8):
                spread(wlo, 0, n, n - 1)
            st.sync()
            for c in range(2):
                st.do(cp(whi[:, c, :, 1:2], wlo[:, c, :, 15:16]))
            spread(whi, 1, 1, 1)
            spread(whi, 1, 1, 2)
            spread(whi, 1, 3, 3)
            spread(whi, 1, 1, 6)
            st.sync()

        def mix_unit(i, q):
            return Along(i, 4, 6, plan.unit[("mix", 0)] + q)

        def mix_block(i, q, b):
            v0 = plan.block[("mix", 0)]
            return i * 18 + (v0 + 3 * q + b + 1)

        def pe_mix(pe):
            for b in range(NB):
                stats_h(pe, 1, b)
            pe.wait_ge(z_ready, 48)
            with pe.Fori(0, 4) as i:
                for q in range(6):
                    pe.wait_ge(w_ready, i * 6 + (plan.unit[("mix", 0)] + q + 1))
                    slot = (plan.unit[("mix", 0)] + q) % SPLIT_SLOTS
                    for b in range(NB):
                        pe.wait_ge(m_scaled, i * 18 + (3 * q + b + 1))
                        for k in range(DT):
                            mm = three(PA[b][:, 0:BW], wslices(slot, k * P, k * P + P),
                                       (z_hi[:, k, cols(b)], z_lo[:, k, cols(b)]), k == 0, k == DT - 1)
                        mm.then_inc(pe_block, 1)
                    if q == 0:
                        pe_tables(pe, i)
                    if q in (2, 4):
                        pe_states(pe, i, q // 2 - 1)
                    if q in (3, 5):
                        pe_y(pe, i, q // 2 - 1)

        def pe_tables(pe, i):
            pe.wait_ge(pq_ready, i + 1)
            pe.wait_ge(e_read, i * 2 + 1)
            for c in range(2):
                for p in range(4):
                    mm = nc.tensor.transpose(PB[c][:, p * P:(p + 1) * P], pt[:, c, p].rearrange("p s c -> p (s c)"), ident[:, :])
                mm.then_inc(prep_mm, 1)
            for p in range(4):
                for c in range(2):
                    mm = nc.tensor.matmul(PB[2][32 * p:32 * p + 32, 0:P], bbst[:, c, p].rearrange("p g c -> p (g c)"),
                                          qt[:, c, p, 0:L, :].rearrange("p k c -> p (k c)"), start=(c == 0), stop=(c == 1))
            mm.then_inc(prep_mm, 1)

        def pe_states(pe, i, hf):
            if hf == 0:
                pe.wait_ge(prep_ev, i * 3 + 3)
                pe.wait_ge(ur_loaded, (i + 1) * 128)
            else:
                pe.wait_ge(e_read, i * 2 + 2)
            for c in range(2):
                for qq in range(2):
                    for h in range(2):
                        p = 2 * hf + qq
                        mm = nc.tensor.matmul(PB[c][64 * h:64 * h + 64, qq * K:(qq + 1) * K], bint[:, c, p, 64 * h:64 * h + 64],
                                              ur[:, 2 * p + h, :], start=True, stop=True)
            mm.then_inc(e_mm, 1)

        def pe_y(pe, i, hf):
            if hf == 0:
                pe.wait_ge(toep_loaded, (i + 1) * 128)
            pe.wait_ge(hb_ready, i * 2 + (hf + 1))
            pe.wait_ge(y_ev, i * 2 + (hf + 1))
            for qq in range(2):
                p = 2 * hf + qq
                out = [PC[h][:, qq * K:(qq + 1) * K] for h in range(2)]
                for h in range(2):
                    nc.tensor.matmul(out[h], toep[:, 2 * p + h, :], ur[:, 2 * p + h, :], start=True, stop=False)
                for h in range(2):
                    rows = slice(64 * h, 64 * h + 64)
                    for c in range(2):
                        mm = nc.tensor.matmul(out[h], qt[rows, c, p, 1:L + 1, :].rearrange("p k c -> p (k c)"),
                                              hb[rows, c, qq, 0:K], start=False, stop=(c == 1))
            mm.then_inc(y_mm, 1)

        DVE_PER = 82

        def dve_mix(dve):
            tt, stt, cp = nc.vector.tensor_tensor, nc.vector.scalar_tensor_tensor, nc.vector.tensor_copy
            dve.wait_ge(h_spilled, 48)
            dve.sem_inc(m_scaled, 3)
            dve.sem_inc(e_read, 1)
            dve.sem_inc(y_ev, 1)
            pre = Steps(dve, own["dve_mix"])
            pre.do(nc.vector.memset(taps[:, 0:P], 0.0))
            pre.do(nc.vector.memset(hb[:, :, :, 0:1], 0.0))
            pre.sync()
            with dve.Fori(0, 4) as i:
                st = Steps(dve, own["dve_mix"], i, DVE_PER, 2)
                st.sync()
                pairs = lambda tab, c: tab[:, c, ds(i * 4, 4)]

                def evac(q):
                    for b in range(NB):
                        dve.wait_ge(pe_block, mix_block(i, q, b))
                        dve.wait_ge(m_out, i * 18 + (3 * q + b + 1))
                        tt(mt[b], PA[b][:, 0:BW], rstd[:, cols(b)], ALU.mult).then_inc(m_scaled, 1)

                split_lo(dve, mix_unit(i, 2))
                dve.wait_ge(y_mm, i * 2 + 1)
                shp = lambda k: [P, 4, k, GC]
                tmp = lambda k: [mtmp[:, c, :, 0:k * GC].rearrange("p j (k c) -> p j k c", c=GC) for c in range(2)]
                per_k = lambda tab, c, k: pairs(tab, c).unsqueeze(3).broadcast_to(shp(k))
                per_c = lambda tab, c, k: pairs(tab, c).unsqueeze(2).broadcast_to(shp(k))
                cmul(st, (pt[:, 0], pt[:, 1]), [per_k(arev, c, L) for c in range(2)], [per_c(bb, c, L) for c in range(2)], tmp(L))
                st.sync()
                cmul(st, (qt[:, 0], qt[:, 1]), [per_k(apw, c, L + 1) for c in range(2)], [per_c(cc, c, L + 1) for c in range(2)],
                     tmp(L + 1), neg_im=True)
                for c in range(2):
                    st.do(nc.vector.memset(bbst[:, c], 0.0))
                st.do(take(dst_[:, :], vecs[:, ds(i * 8 + V_D, 8)]))
                st.do(take(bst[:, 0:1], vecs[:, ds(i * 1 + V_BIN, 1)]))
                st.do(take(bst[:, 1:2], vecs[:, ds(i * 1 + (V_BIN + 4), 1)]))
                st.do(take(bst[:, 2:6], vecs[:, ds(i * 4 + (V_BIN + 8), 4)]))
                st.sync()
                for c in range(2):
                    for h in range(2):
                        rows = slice(64 * h, 64 * h + 64)
                        st.do(take(bbst[rows, c, :, h, :], bb[rows, c, ds(i * 4, 4)]))
                st.sync()
                dve.sem_inc(pq_ready, 1)
                evac(0)
                for c in range(2):
                    dve.wait_ge(prep_mm, i * 3 + (c + 1))
                    cp(bint[:, c].rearrange("p j s -> p (j s)"), PB[c][:, :]).then_inc(prep_ev, 1)
                dve.wait_ge(prep_mm, i * 3 + 3)
                cp(taps[:, P:2 * P], PB[2][:, 0:P]).then_inc(prep_ev, 1)
                split_lo(dve, mix_unit(i, 3))
                w4 = [P, 4, L, 16]
                wtv = [wt[:, c, :, 0:KP].rearrange("p j (a b) -> p j a b", b=16) for c in range(2)]
                tw = [mtmp[:, c, :, 0:KP].rearrange("p j (a b) -> p j a b", b=16) for c in range(2)]
                cmul(st, wtv, [pairs(whi, c).unsqueeze(3).broadcast_to(w4) for c in range(2)],
                     [pairs(wlo, c).unsqueeze(2).broadcast_to(w4) for c in range(2)], tw)
                st.sync()
                st.do(cp(wt[:, :, :, KP:K], wt[:, :, :, 0:KS]))
                st.do(tt(dec[:, :, :], sm[:, S["m8"], ds(i * 4, 4)].unsqueeze(2).broadcast_to([P, 4, K]),
                         mask[:, :].unsqueeze(1).broadcast_to([P, 4, K]), ALU.mult))
                st.sync()
                evac(1)
                split_lo(dve, mix_unit(i, 4))
                evac(2)
                split_lo(dve, mix_unit(i, 5))
                dve_states(dve, st, i, 0)
                evac(3)
                split_lo(dve, mix_unit(i, 6))
                dve_y(dve, st, i, 0)
                evac(4)
                split_lo(dve, mix_unit(i, 7))
                dve_states(dve, st, i, 1)
                evac(5)
                dve_y(dve, st, i, 1)
                assert st.n == DVE_PER, st.n

        def dve_states(dve, st, i, hf):
            tt, stt, cp = nc.vector.tensor_tensor, nc.vector.scalar_tensor_tensor, nc.vector.tensor_copy
            dve.wait_ge(e_mm, i * 2 + (hf + 1))
            E = [PB[c][:, 0:2 * K].rearrange("p (q k) -> p q k", k=K) for c in range(2)]
            w = [wt[:, c, 2 * hf:2 * hf + 2, :] for c in range(2)]
            st.do(tt(r1[:, :, :], E[0], w[0], ALU.mult))
            st.do(tt(r2[:, :, :], E[1], w[1], ALU.mult))
            st.do(tt(r3[:, :, :], E[1], w[0], ALU.mult))
            tt(r4[:, :, :], E[0], w[1], ALU.mult).then_inc(e_read, 1)
            dve.wait_ge(e_read, i * 2 + (hf + 2))
            st.sync()
            st.do(tt(vr[:, :, :], r1[:, :, :], r2[:, :, :], ALU.add))
            st.do(tt(vi[:, :, :], r3[:, :, :], r4[:, :, :], ALU.subtract))
            st.sync()
            pr = lambda n: sm[:, S[n], ds(i * 4 + 2 * hf, 2)].unsqueeze(2)
            st.do(tt(vr[:, :, KP:KP + 1], vr[:, :, KP:KP + 1], pr("rhr"), ALU.add))
            st.do(tt(vi[:, :, KP:KP + 1], vi[:, :, KP:KP + 1], pr("rhi"), ALU.add))
            st.sync()
            flat = lambda x: x.rearrange("p q k -> p (q k)")
            dd = flat(dec[:, 2 * hf:2 * hf + 2, :])
            st.do(nc.vector.tensor_tensor_scan(flat(r1[:, :, :]), dd, flat(vr[:, :, :]), 0.0, ALU.mult, ALU.add))
            st.do(nc.vector.tensor_tensor_scan(flat(r2[:, :, :]), dd, flat(vi[:, :, :]), 0.0, ALU.mult, ALU.add))
            st.sync()
            cmul(st, [hb[:, c, :, 1:K + 1] for c in range(2)], w, (r1[:, :, :], r2[:, :, :]), (r3[:, :, :], r4[:, :, :]))
            st.sync()
            for c in range(2):
                st.do(take(hfin[:, c, ds(i * 4 + 2 * hf, 2)].unsqueeze(2), hb[:, c, :, KP:KP + 1]))
                st.do(take(hfin[:, 2 + c, ds(i * 4 + 2 * hf, 2)].unsqueeze(2), hb[:, c, :, K:K + 1]))
            st.sync()
            for c in range(2):
                st.do(take(hb[:, c, :, KP:KP + 1], sp_[:, ds(i * 4 + (2 * hf + (H0R, H0I)[c]), 2)].unsqueeze(2)))
            st.sync()
            dve.sem_inc(hb_ready, 1)

        def dve_y(dve, st, i, hf):
            tt, stt = nc.vector.tensor_tensor, nc.vector.scalar_tensor_tensor
            dve.wait_ge(y_mm, i * 2 + (hf + 2))
            for j in range(4):
                qq, h = j // 2, j % 2
                g = 4 * hf + j
                ins = stt(yv[:, j, :], ur[:, g, :], dst_[:, g:g + 1], PC[h][:, qq * K:(qq + 1) * K], ALU.mult, ALU.add)
                if j < 3:
                    st.do(ins)
            ins.then_inc(y_ev, 1)
            dve.wait_ge(y_ev, i * 2 + (hf + 2))
            st.sync()
            st.do(tt(ya[:, :, :], yv[:, :, :], yv[:, :, :], ALU.mult))
            st.sync()
            st.do(nc.vector.tensor_scalar(ya[:, :, :], ya[:, :, :], 0.044715, 1.0, ALU.mult, ALU.add))
            st.sync()
            tt(ya[:, :, :], ya[:, :, :], yv[:, :, :], ALU.mult).then_inc(gelu_in, 1)
            dve.wait_ge(sig_done, i * 2 + (hf + 1))
            tt(yv[:, :, :], yv[:, :, :], ya[:, :, :], ALU.mult).then_inc(y_full, 1)
            dve.wait_ge(yhs_done, i * 2 + (hf + 1))
            tt(yls[:, :, :], yv[:, :, :], yhs[:, :, :].bitcast(F32), ALU.subtract).then_inc(yls_done, 1)

        def act_mix(act):
            act.wait_ge(h_spilled, 48)
            act.sem_inc(m_out, 3)
            for b in range(NB):
                act.sem_inc(m_stored[b], 16)
            act.sem_inc(y_stored, 256)
            with act.Fori(0, 4) as i:
                def evac(q):
                    for b in range(NB):
                        act.wait_ge(m_scaled, i * 18 + (3 * q + b + 1 + 3))
                        fn = ACT.Sigmoid if q > 1 else ACT.Identity
                        if q == 1:
                            nc.scalar.activation(up[:, ds(i * T + b * BW, BW)], mt[b], fn, bias=bst[:, 1:2]).then_inc(m_out, 1)
                            continue
                        n = (0, None, 1, 2, 3, 4)[q]
                        act.wait_ge(m_stored[b], i * 80 + 16 * (n + 1))
                        nc.scalar.activation(og[b], mt[b], fn, bias=bst[:, q:q + 1]).then_inc(m_out, 1)
                    for b in range(NB):
                        if q == 1:
                            continue
                        act.wait_ge(m_out, i * 18 + (3 * q + b + 1 + 3))
                        if q == 0:
                            act.dma_start(u_dram[ds(i, 1), :, cols(b)].rearrange("o p t -> p (o t)"), og[b]).then_inc(m_stored[b], 16)
                        else:
                            act.dma_start(gate_dram[ds(i * 4 + q - 2, 1), :, cols(b)].rearrange("o p t -> p (o t)"),
                                          og[b]).then_inc(m_stored[b], 16)

                def gelu(hf):
                    act.wait_ge(gelu_in, i * 2 + (hf + 1))
                    nc.scalar.activation(ya[:, :, :], ya[:, :, :], ACT.Sigmoid, scale=2 * sqrt(2 / pi)).then_inc(sig_done, 1)
                    act.wait_ge(y_full, i * 2 + (hf + 1))
                    act.wait_ge(y_stored, i * 512 + 256 * (hf + 1))
                    nc.scalar.activation(yhs[:, :, :], yv[:, :, :], ACT.Copy).then_inc(yhs_done, 1)
                    act.wait_ge(yls_done, i * 2 + (hf + 1))
                    act.wait_ge(yhs_done, i * 2 + (hf + 1))
                    for dram, src in ((yhi_dram, yhs), (ylo_dram, yls)):
                        for t in range(L):
                            act.dma_start(dram.rearrange("(g c) t k -> c g t k", c=GC)[:, ds(i * 8 + 4 * hf, 4), t, :],
                                          src[GC * t:GC * t + GC, :, :].bitcast(F32)).then_inc(y_stored, 16)

                for q in range(6):
                    if q < 4:
                        split_hi(act, mix_unit(i, q + 2))
                    evac(q)
                    if q in (3, 4):
                        split_hi(act, mix_unit(i, q + 3))
                    if q in (3, 5):
                        gelu(q // 2 - 1)

        def sp_mix(sp):
            sp.wait_ge(h_spilled, 48)

            def side(i):
                sp.wait_ge(prep_ev, i * 3 + 3)
                sp.dma_start(taps_dram, taps[:, :]).then_inc(taps_stored, 16)
                for b in range(NB):
                    sp.wait_ge(m_stored[b], i * 80 + 32)
                sp.wait_ge(y_mm, i * 2 + 1)
                sp.wait_ge(y_ev, i * 2 + 1)
                for s in range(L):
                    sp.dma_start(ur[GC * s:GC * s + GC, :, :],
                                 u_dram.rearrange("j (g c) (s k) -> j s c g k", c=GC, s=L)[ds(i, 1), s]
                                 .rearrange("o c g k -> (o c) g k")).then_inc(ur_loaded, 16)
                sp.wait_ge(taps_stored, i * 16 + 16)
                for s in range(L):
                    sp.dma_start(toep[GC * s:GC * s + GC, :, :],
                                 taps_dram.rearrange("(g c) x -> c g x", c=GC)[:, :, P - GC * s:2 * P - GC * s]).then_inc(toep_loaded, 16)
            for q in range(3, 6):
                load_unit(sp, "mix", 0, q)
            with sp.Fori(0, 3) as j:
                load_unit(sp, "mix", Along(j, 3, 1, 1), 0)
                side(j)
                for q in range(1, 6):
                    load_unit(sp, "mix", Along(j, 3, 1, 1), q)
            side(3)

        def pool_windows(pool):
            pool.wait_ge(h_spilled, 48)
            st = Steps(pool, own["pool_prep"])
            tt, cp, ts = nc.gpsimd.tensor_tensor, nc.gpsimd.tensor_copy, nc.gpsimd.tensor_scalar
            for g in range(4):
                w = 2 << g
                pool.wait_ge(m_out, 18 * g + 6 + 3)
                if g == 0:
                    pool.wait_ge(own["dve_prep"], 2)
                u = up[:, g * T:(g + 1) * T].rearrange("p (s k) -> p s k", s=L)
                st.sync()
                st.do(nc.gpsimd.memset(ext[:, :, 0:2], 0.0))
                st.do(cp(ext[:, :, 2:2 + KP], u[:, :, 0:KP]))
                st.do(cp(ext[:, :, 2 + KP:4 + KP], hcol[:, g, :].rearrange("p (k s) -> p s k", s=L)))
                st.do(cp(ext[:, :, 4 + KP:4 + K], u[:, :, KP:K]))
                st.do(cp(tail[:, g, 0, :].rearrange("p (k s) -> p s k", s=L), u[:, :, KP - 2:KP]))
                st.do(cp(tail[:, g, 1, :].rearrange("p (k s) -> p s k", s=L), u[:, :, K - 2:K]))
                src, dst = ext, sum_a
                for level in range(g + 1):
                    d = 1 << level
                    st.sync()
                    if d < L:
                        st.do(tt(dst[:, d:L, :], src[:, d:L, :], src[:, 0:L - d, :], ALU.add))
                    st.do(tt(dst[:, 0:d, 1:], src[:, 0:d, 1:], src[:, L - d:L, 0:K + 3], ALU.add))
                    st.do(cp(dst[:, 0:d, 0:1], src[:, 0:d, 0:1]))
                    src, dst = dst, src
                st.sync()
                st.do(tt(src[:, :, 2:4], src[:, :, 2:4], cnt[:, g, :].rearrange("p (s k) -> p s k", s=L), ALU.mult))
                st.sync()
                st.do(ts(src[:, :, 2:4 + K], src[:, :, 2:4 + K], 1.0 / w, 1.0, ALU.mult, ALU.mult))
                st.sync()
                st.do(tt(u[:, :, 0:KP], src[:, :, 2:2 + KP], u[:, :, 0:KP], ALU.subtract))
                st.do(tt(u[:, :, KP:K], src[:, :, 4 + KP:4 + K], u[:, :, KP:K], ALU.subtract))
                st.sync()
                pool.sem_inc(pooled, 1)

        MIX_END = plan.block["pool"]

        def pe_after(pe):
            pe.wait_ge(tail_ready, 1)
            nc.tensor.transpose(PB[0][0:64, 0:P], hfin[:, :, :].rearrange("p a j -> p (a j)"), ident[:, :])
            for w in range(2):
                for g in range(4):
                    mm = nc.tensor.transpose(PB[1 + w][0:16, g * P:(g + 1) * P], tail[:, g, w, :], ident[:, :])
            mm.then_inc(last_mm, 1)
            pe.wait_ge(pl_ready, 4)
            u = plan.unit["pool"]
            pe.wait_ge(w_ready, u + 1)
            for m in range(DT):
                for b in range(NB):
                    n = NB * m + b
                    if n >= 2:
                        pe.wait_ge(gp_done, n - 1)
                    three(PC[n % 2][:, 0:BW], wslices(u % SPLIT_SLOTS, m * P, m * P + P),
                          (pl_hi[:, m // 2, cols(b)], pl_lo[:, m // 2, cols(b)]), True, True).then_inc(pe_block, 1)

        def dve_after(dve):
            dve.wait_ge(pooled, 4)
            dve.wait_ge(yls_done, 8)
            dve.sem_inc(tail_ready, 1)
            for g in range(4):
                dve.wait_ge(pl_hi_done, g + 1)
                nc.vector.tensor_tensor(pl_lo[:, g, :], up[:, g * T:(g + 1) * T], pl_hi[:, g, :].bitcast(F32),
                                        ALU.subtract).then_inc(pl_ready, 1)
            split_lo(dve, plan.unit["pool"] + 2)
            for m in range(DT):
                dve.wait_ge(gp_loaded[m % 2], 16 * (m // 2 + 1))
                if m >= 2:
                    dve.wait_ge(gp_stored[m % 2], 16 * (m // 2))
                for b in range(NB):
                    n = NB * m + b
                    dve.wait_ge(pe_block, MIX_END + n + 1)
                    nc.vector.scalar_tensor_tensor(gp_out[:, m % 2, cols(b)], PC[n % 2][:, 0:BW], vecs[:, V_PSC + m:V_PSC + m + 1],
                                                   gp_in[:, m % 2, cols(b)], ALU.mult, ALU.mult).then_inc(gp_done, 1)

        def act_after(act):
            act.wait_ge(pe_block, MIX_END)
            for g in range(4):
                act.wait_ge(pooled, g + 1)
                nc.scalar.activation(pl_hi[:, g, :], up[:, g * T:(g + 1) * T], ACT.Copy).then_inc(pl_hi_done, 1)
            act.wait_ge(last_mm, 1)
            nc.scalar.activation(hfrow[:, :], PB[0][0:64, 0:P], ACT.Copy).then_inc(last_ev, 1)
            for w in range(2):
                nc.scalar.activation(prow[:, w, :], PB[1 + w][0:16, :], ACT.Copy).then_inc(last_ev, 1)
            split_hi(act, plan.unit["pool"] + 2)
            act.wait_ge(last_ev, 3)
            for n, out in enumerate((re_prompt, im_prompt, re_sample, im_sample)):
                act.dma_start(out.rearrange("(j g) s -> j (g s)", g=2), hfrow[16 * n:16 * n + 16, :]).then_inc(state_out, 16)
            for w, out in enumerate((pool_prompt, pool_sample)):
                act.dma_start(out, prow[1:16, w, :]).then_inc(state_out, 16)
            act.wait_ge(state_out, 96)

        def sp_after(sp):
            load_unit(sp, "pool", 0, 0)
            load_unit(sp, "glu", 0, 0)
            load_unit(sp, "glu", 0, 1)
            sp.wait_ge(pe_block, MIX_END)
            sp.wait_ge(y_stored, 256 * 9)
            sp.dma_start(y_hi.bitcast(F32), yhi_dram.rearrange("(j p) t k -> p j (t k)", p=P)).then_inc(y_loaded, 16)
            sp.dma_start(y_lo.bitcast(F32), ylo_dram.rearrange("(j p) t k -> p j (t k)", p=P)).then_inc(y_loaded, 16)
            sp.wait_ge(tail_ready, 1)
            for b in range(NB):
                sp.wait_ge(m_stored[b], 16 * 21)
            for m in range(DT + 1):
                if m < DT:
                    if m >= 2:
                        sp.wait_ge(gp_done, NB * (m - 1))
                    sp.dma_start(gp_in[:, m % 2, :], gate_dram[DT + m]).then_inc(gp_loaded[m % 2], 16)
                if m:
                    sp.wait_ge(gp_done, NB * m)
                    sp.dma_start(prod_dram[m - 1], gp_out[:, (m - 1) % 2, :]).then_inc(gp_stored[(m - 1) % 2], 16)
            sp.wait_ge(pl_ready, 4)
            sp.wait_ge(last_mm, 1)
            sp.wait_ge(state_out, 96)
            for b in range(NB):
                sp.dma_start(xres[:, :, cols(b)], h_dram[:, :, cols(b)]).then_inc(h_back, 16)

        side_slot = [(std[:, :], rpost[:, :]), (rstd[:, 0:BW], rstd[:, BW:2 * BW])]

        def pool_side(pool):
            for i in range(2):
                pool.wait_ge(gp_stored[i], 64)
            for n in range(NB * DT):
                if n >= 2:
                    pool.wait_ge(h_mul[3], n - 1)
                m, b = divmod(n, NB)
                gs, pr = side_slot[n % 2]
                pool.dma_start(gs, gate_dram[m, :, cols(b)]).then_inc(side_loaded[n % 2], 16)
                pool.dma_start(pr, prod_dram[m, :, cols(b)]).then_inc(side_loaded[n % 2], 16)

        def pe_glu(pe, g):
            for q in range(2):
                u = plan.unit[("glu", g)] + q
                m = 2 * g + q
                pe.wait_ge(w_ready, u + 1)
                for b in range(NB):
                    pe.wait_ge(in_free[3], 3 * m + b + 1)
                    for h, out in ((0, PA), (1, PB)):
                        for k in range(4):
                            c0 = (2 * k + h) * P
                            mm = three(out[b][:, 0:BW], wslices(u % SPLIT_SLOTS, c0, c0 + P),
                                       (y_hi[:, k, cols(b)], y_lo[:, k, cols(b)]), k == 0, k == 3)
                    mm.then_inc(pe_block, 1)

        def pe_merge(pe):
            pe.wait_ge(y_loaded, 32)
            pe.wait_ge(last_ev, 3)
            pe_glu(pe, 0)
            for g in range(1, MG):
                pe_glu(pe, g)
                pe_out(pe, 3, g - 1)
            pe_last(pe, 3)

        def dve_glu(dve, g):
            stt, tt = nc.vector.scalar_tensor_tensor, nc.vector.tensor_tensor
            for q in range(2):
                m = 2 * g + q
                split_lo(dve, plan.unit[("glu", g)] + q + 2)
                for b in range(NB):
                    n = NB * m + b
                    s = n % 2
                    gs, pr = side_slot[s]
                    dve.wait_ge(sig_m, n + 1)
                    stt(ta[:, s, :], PA[b][:, 0:BW], vecs[:, V_BGLU + m:V_BGLU + m + 1], tb[:, s, :], ALU.add, ALU.mult).then_inc(in_free[3], 1)
                    dve.wait_ge(in_free[3], n + 1 + 3)
                    dve.wait_ge(side_loaded[s], 32 * (n // 2 + 1))
                    tt(ta[:, s, :], ta[:, s, :], gs, ALU.mult).then_inc(merge_a, 1)
                    dve.wait_ge(merge_a, n + 1)
                    tt(tb[:, s, :], ta[:, s, :], pr, ALU.add).then_inc(h_mul[3], 1)
                    dve.wait_ge(hid_hi_done[3], n + 1)
                    hs = m % 4
                    tt(hid_lo[:, hs, cols(b)], tb[:, s, :], hid_hi[:, hs, cols(b)].bitcast(F32), ALU.subtract).then_inc(hid_ready[3], 1)

        def act_glu(act, g):
            for q in range(2):
                m = 2 * g + q
                split_hi(act, plan.unit[("glu", g)] + q + 2)
                for b in range(NB):
                    n = NB * m + b
                    s = n % 2
                    act.wait_ge(pe_block, plan.block[("glu", g)] + 3 * q + b + 1)
                    if n >= 2:
                        act.wait_ge(hid_ready[3], n - 1)
                    nc.scalar.activation(tb[:, s, :], PB[b][:, 0:BW], ACT.Sigmoid,
                                         bias=vecs[:, V_BGLU + 8 + m:V_BGLU + 9 + m]).then_inc(sig_m, 1)
                    act.wait_ge(h_mul[3], n + 1)
                    if q == 0 and b == 0:
                        if g >= 2:
                            act.wait_ge(pe_block, plan.block[("merge", g - 2)] + 24)
                        else:
                            act.wait_ge(gp_stored[0], 64)
                            act.wait_ge(gp_stored[1], 64)
                    hs = m % 4
                    nc.scalar.activation(hid_hi[:, hs, cols(b)], tb[:, s, :], ACT.Copy).then_inc(hid_hi_done[3], 1)

        def dve_merge(dve, next_units):
            dve.wait_ge(acc_zero, 2)
            dve.sem_inc(in_free[3], 3)
            dve.sem_inc(out_free[3], 26)
            dve_glu(dve, 0)
            for g in range(1, MG):
                dve_glu(dve, g)
                dve_outs(dve, 3, g - 1)
            dve_last(dve, 3, next_units)

        def act_merge(act, next_units):
            act_glu(act, 0)
            for g in range(1, MG):
                act_glu(act, g)
                act_outs(act, 3, g - 1)
            act_last(act, 3, next_units)

        def sp_merge(sp):
            for g in range(1, MG):
                for q in range(2):
                    load_unit(sp, "glu", g, q)
                for q in range(2):
                    load_unit(sp, "merge", g - 1, q)
            for q in range(2):
                load_unit(sp, "merge", MG - 1, q)

        TILES = list(range(9))
        dcol = ta.rearrange("p a b -> p (a b)")[:, 0:DT * DEC].rearrange("p (m t) -> p m t", m=DT)

        def dve_end(dve):
            dve.wait_ge(h_done, 72)
            nc.vector.tensor_copy(dcol.rearrange("p m (k s) -> p m k s", s=L),
                                  xres.rearrange("p m (s k) -> p m k s", s=L)[:, :, KP:K, :]).then_inc(dcol_done, 1)

        def pe_end(pe):
            F = 0
            for tile in TILES:
                b = 2 if tile == 8 else (tile * K + KP - 1) // BW
                pe.wait_ge(h_done, 48 + 8 * b + 8)
                if tile == 8:
                    pe.wait_ge(dcol_done, 1)
                for half in range(2):
                    if F >= 3:
                        pe.wait_ge(yrow_ready, F - 2)
                    rows = DEC if tile == 8 else P
                    for j in range(4):
                        m = 4 * half + j
                        src = xres[:, m, :]
                        if tile == 8:
                            src = dcol[:, m, :]
                        else:
                            src = src[:, tile * K:tile * K + KP]
                        mm = nc.tensor.transpose(PB[F % 3][0:rows, j * P:(j + 1) * P], src, ident[:, :])
                    mm.then_inc(y_turned, 1)
                    F += 1

        def act_end(act):
            F = 0
            for tile in TILES:
                rows = DEC if tile == 8 else P
                for half in range(2):
                    act.wait_ge(y_turned, F + 1)
                    if half == 0 and tile >= 4:
                        act.wait_ge(y_out[tile % 4], 16 * (tile // 4))
                    nc.scalar.activation(yrow[0:rows, tile % 4, 512 * half:512 * half + 512], PB[F % 3][0:rows, :],
                                         ACT.Copy).then_inc(yrow_ready, 1)
                    F += 1

        def sp_end(sp):
            yp = y_prompt.rearrange("(k s) d -> s k d", s=L)
            for tile in TILES:
                sp.wait_ge(yrow_ready, 2 * tile + 2)
                if tile == 8:
                    sp.dma_start(y_sample, yrow[0:DEC, 0, :]).then_inc(y_out[0], 16)
                else:
                    sp.dma_start(yp[tile], yrow[:, tile % 4, :]).then_inc(y_out[tile % 4], 16)
            for i, n in enumerate((3, 2, 2, 2)):
                sp.wait_ge(y_out[i], 16 * n)

        FIRST_MIX, FIRST_F2 = plan.unit[("mix", 0)], plan.unit[(2, "in", 0)]

        @block.sync
        def _(sp):
            sp_start(sp)
            sp_ffn(sp, 1, skip=3)
            for q in range(3):
                load_unit(sp, "mix", 0, q)
            for b in range(NB):
                sp.wait_ge(h_done, 8 * b + 8)
                sp.dma_start(h_dram[:, :, cols(b)], xres[:, :, cols(b)]).then_inc(h_spilled, 16)
                if b == 0:
                    sp_prep(sp)
            sp_mix(sp)
            sp_after(sp)
            sp_merge(sp)
            sp_ffn(sp, 2)
            sp_end(sp)

        @block.gpsimd
        def _(pool):
            nc.gpsimd.memset(ident[:, :], 0.0).then_inc(const_ready, 1)
            nc.gpsimd.memset(ones[:, :], 1.0).then_inc(const_ready, 1)
            nc.gpsimd.memset(epsc[:, :], EPS).then_inc(const_ready, 1)
            pool.wait_ge(const_ready, 3)
            nc.gpsimd.affine_select(out=ident[:, :], in_=ident[:, :], compare_op=ALU.not_equal, fill=1.0, base=0,
                                    pattern=[[-1, P]], channel_multiplier=1).then_inc(const_ready, 2)
            pool.wait_ge(x_turned, 18)
            nc.gpsimd.memset(acc[:, :, :], 0.0).then_inc(acc_zero, 1)
            for b in range(NB):
                add_squares(pool, job(0, "x", b))
            pool_stage(pool, 1)
            pool_windows(pool)
            pool.wait_ge(pl_ready, 4)
            pool.wait_ge(last_mm, 1)
            pool.wait_ge(state_out, 96)
            nc.gpsimd.memset(acc[:, :, :], 0.0).then_inc(acc_zero, 1)
            pool_side(pool)
            pool_stage(pool, 2)
            pool.wait_ge(h_done, 48)
            nc.gpsimd.memset(acc[:, :, :], 0.0).then_inc(acc_zero, 1)
            pool_stage(pool, 3)

        @block.scalar
        def _(act):
            split_hi(act, 0)
            split_hi(act, 1)
            act.wait_ge(const_ready, 5)
            empty_x(act, lambda d, s: nc.scalar.activation(d, s, ACT.Copy), 1, x_act)
            act.wait_ge(x_dve, 9)
            act.wait_ge(vec_ready, 1)
            act.wait_ge(x_act, 9)
            for b in range(NB):
                for m in range(DT):
                    z_hi_part(act, 0, b, m, V_PRE1)
                    square(act, job(0, "x", b), m, xres[:, m, cols(b)])
            act_ffn(act, 1, [FIRST_MIX + 1])
            act_prep(act)
            act_mix(act)
            act_after(act)
            act_merge(act, [FIRST_F2 + 1])
            act_ffn(act, 2, [])
            act_end(act)

        @block.vector
        def _(dve):
            dve.wait_ge(vec_mm, 1)
            nc.vector.tensor_copy(vecs[:, :], PC[0][:, 0:P]).then_inc(vec_ready, 1)
            empty_x(dve, nc.vector.tensor_copy, 0, x_dve)
            split_lo(dve, 0)
            split_lo(dve, 1)
            dve.wait_ge(vec_ready, 1)
            dve.wait_ge(x_dve, 9)
            dve.wait_ge(x_act, 9)
            dve.sem_inc(in_free[1], 3)
            for b in range(NB):
                for m in range(DT):
                    z_lo_part(dve, 0, b, m, V_PRE1)
            before = lambda st: (lambda b: recip_row(dve, st, b))

            def recip_row(dve, st, b):
                recip(dve, job(st, "h", b), rstd[:, cols(b)])
                dve.wait_ge(recip_done, job(st, "h", b) + 1)
            dve_ffn(dve, 1, before(0), [FIRST_MIX + 1])
            steps = dve_prep_a(dve)
            for b in range(NB):
                recip_row(dve, 1, b)
            dve_prep_b(dve, steps)
            dve_mix(dve)
            dve_after(dve)
            dve_merge(dve, [FIRST_F2 + 1])
            dve_ffn(dve, 2, before(2), [])
            dve_end(dve)

        @block.tensor
        def _(pe):
            pe_start(pe)
            pe_ffn(pe, 1)
            pe.sem_inc(y_mm, 1)
            pe_prep(pe)
            pe_mix(pe)
            pe_after(pe)
            pe_merge(pe)
            pe_ffn(pe, 2)
            pe_end(pe)


_INS = ["x_prompt", "x_sample", "state_ssm_re", "state_ssm_im", "cache_pool", "ffn1_pre_g", "ffn1_w_in", "ffn1_w_out",
        "ffn1_post_g", "mix_pre_g", "w_in", "b_in", "ssm_lambda_re", "ssm_lambda_im", "ssm_log_step", "ssm_b_re", "ssm_b_im",
        "ssm_c_re", "ssm_c_im", "ssm_d", "ssm_w_glu", "ssm_b_glu", "pool_w", "pool_scale", "w_out", "mix_post_g",
        "ffn2_pre_g", "ffn2_w_in", "ffn2_w_out", "ffn2_post_g"]
_OUTS = [((1, SEQ, D), (SEQ, D)), ((1, DEC, D), (DEC, D)), ((1, 1, G, NS), (G, NS)), ((1, 1, G, NS), (G, NS)),
         ((1, 1, HIST, DS), (HIST, DS)), ((1, 1, G, NS), (G, NS)), ((1, 1, G, NS), (G, NS)), ((1, 1, HIST, DS), (HIST, DS))]


def constants():
    counts = np.ones((P, 4, L, 2), np.float32)
    for g in range(4):
        w = 2 << g
        for t in range(w - 1):
            counts[:, g, t % L, t // L] = w / (t + 1)
    mask = np.ones((P, K), np.float32)
    mask[:, [0, KP]] = 0.0
    return {"window_counts": counts.reshape(P, 4, 2 * L), "scan_mask": mask}


def kernel(**inputs):
    import concourse.bacc as bacc
    from concourse.bass_utils import run_bass_kernel_spmd

    nc = bacc.Bacc("TRN2", target_bir_lowering=False, num_devices=1, dynamic_dma_scratch_size=1024)
    arrays, args = {}, {}
    for name in _INS:
        x = np.ascontiguousarray(inputs[name])
        x = x[0] if x.shape[0] == 1 else x
        if name in ("state_ssm_re", "state_ssm_im", "cache_pool"):
            x = x[0]
        arrays[name] = np.ascontiguousarray(x)
    arrays.update(constants())
    for name, x in arrays.items():
        args[name] = nc.dram_tensor(name, x.shape, mybir.dt.from_np(x.dtype), kind="ExternalInput").ap()
    outs = [nc.dram_tensor(f"out_{n}", flat, F32, kind="ExternalOutput").ap() for n, (_, flat) in enumerate(_OUTS)]
    layer(nc, args, outs)
    r = run_bass_kernel_spmd(nc, [arrays], core_ids=[0])
    return tuple(r.results[0][f"out_{n}"].reshape(shape) for n, (shape, _) in enumerate(_OUTS))
```

```python
from contextlib import ExitStack
from math import pi, sqrt

import numpy as np

import concourse.bass as bass
from concourse import mybir

F32 = mybir.dt.float32
F32R = mybir.dt.float32r
I32 = mybir.dt.int32
ACT = mybir.ActivationFunctionType
ALU = mybir.AluOpType
ds = bass.ds

P = 128
D = 1024
DT = D // P
DFF = 2816
HT = DFF // P
SEQ, DEC = 1024, 32
L = 8
KP, KS = SEQ // L, DEC // L
K = KP + KS
T = L * K
NB = 3
BW = T // NB
G, GC, NS = 32, 16, 64
NPAIR = G // 2
DS = 512
HIST = 15
EPS = 1e-6
RAW_SLOTS, SPLIT_SLOTS = 3, 3
WU = D

V_PRE1, V_POST1, V_PREM, V_POSTM, V_PRE2, V_POST2, V_PSC, V_BIN, V_BGLU, V_D = 0, 8, 16, 24, 32, 40, 48, 56, 80, 96


class Along:

    def __init__(self, i, n, a, b):
        self.i, self.n, self.a, self.b = i, n, a, b

    def __add__(self, k):
        return Along(self.i, self.n, self.a, self.b + k)


def of(f, x):
    if not isinstance(x, Along):
        return f(x)
    v = [f(x.a * k + x.b) for k in range(x.n)]
    step = v[1] - v[0]
    assert all(q - p == step for p, q in zip(v, v[1:])), v
    return v[0] if step == 0 else x.i * step + v[0]


class Plan:

    def __init__(self):
        self.unit, self.block, self.last = {}, {}, []
        self.n = 0

    def add(self, key, units, blocks_of_unit, together=False):
        self.unit[key], self.block[key] = len(self.last), self.n
        for _ in range(units):
            self.n += 0 if together else blocks_of_unit
            self.last.append(self.n)
        if together:
            self.n += blocks_of_unit
            for u in range(units):
                self.last[-1 - u] = self.n


def groups(n):
    order = [("in", 0), ("in", 1)]
    for g in range(2, n):
        order += [("out", g - 2), ("in", g)]
    return order + [("fin", n - 2)]


FG = HT // 2
MG = DT // 2
plan = Plan()
for f in (1, 2):
    if f == 2:
        for t in range(4):
            plan.add(("mix", t), 6, NB)
        plan.add("pool", 1, NB * DT)
        for what, g in groups(MG):
            if what == "fin":
                plan.add(("fin", 3), 4, NB * DT, True)
            else:
                plan.add(("glu" if what == "in" else "merge", g), 2, *((NB,) if what == "in" else (NB * DT, True)))
    for what, g in groups(FG):
        if what == "fin":
            plan.add(("fin", f), 4, NB * DT, True)
            continue
        plan.add((f, what, g), *((4, NB) if what == "in" else (2, NB * DT, True)))
        if (what, g) == ("in", 0):
            first = plan.block[(f, "in", 0)]
            plan.last[-4:-2] = first + 2 * NB - 1, first + 2 * NB
UNITS = len(plan.last)


def layer(nc, a, outs):
    (y_prompt, y_sample, re_prompt, im_prompt, pool_prompt, re_sample, im_sample, pool_sample) = outs
    ctx = ExitStack()
    with ctx:
        def sb(name, shape, dt=F32, on=ctx):
            return on.enter_context(nc.sbuf_tensor(name, shape, dt))

        def sem(name):
            return ctx.enter_context(nc.semaphore(name))

        def scratch(name, shape):
            return nc.dram_tensor(name, shape, F32, kind="Internal").ap()

        h_dram = scratch("h_dram", (P, DT, T))
        u_dram = scratch("u_dram", (4, P, T))
        gate_dram = scratch("gate_dram", (2 * DT, P, T))
        prod_dram = scratch("prod_dram", (DT, P, T))
        taps_dram = scratch("taps_dram", (P, 2 * P))
        y_dram = scratch("y_dram", (DS, L, K))

        w_raw = sb("w_raw", [P, RAW_SLOTS, WU])
        w_hi = sb("w_hi", [P, SPLIT_SLOTS, WU], F32R)
        w_lo = sb("w_lo", [P, SPLIT_SLOTS, WU], F32R)
        rstd = sb("rstd", [P, T])
        ident = sb("ident", [P, P])
        ones = sb("ones", [P, P])
        vecs = sb("vecs", [P, P])
        ta = sb("ta", [P, 2, BW])
        tb = sb("tb", [P, 2, BW])
        std = sb("std", [P, BW])
        rpost = sb("rpost", [P, BW])
        sq = sb("sq", [P, 2, BW])
        ssum = sb("ssum", [P, 2, BW])
        epsc = sb("epsc", [P, 1])

        with ExitStack() as s:
            yrow = sb("yrow", [P, 4, D], F32, s)
        z_hi = sb("z_hi", [P, DT, T], F32R)
        z_lo = sb("z_lo", [P, DT, T], F32R)
        y_hi, y_lo, pl_hi, pl_lo = z_hi[:, 0:4], z_lo[:, 0:4], z_hi[:, 4:8], z_lo[:, 4:8]

        with ExitStack() as s:
            hid_hi = sb("hid_hi", [P, 4, T], F32R, s)
            hid_lo = sb("hid_lo", [P, 4, T], F32R, s)
            acc = sb("acc", [P, DT, T], F32, s)
            xres = sb("xres", [P, DT, T], F32, s)
        with ExitStack() as s:
            xrow = sb("xrow", [P, 9, D], F32, s)
            vrow = sb("vrow", [P, P], F32, s)
        with ExitStack() as s:
            gp_in = sb("gp_in", [P, 2, T], F32, s)
            gp_out = sb("gp_out", [P, 2, T], F32, s)
        with ExitStack() as s:
            srow = sb("srow", [P, P], F32, s)
            crow = sb("crow", [P, 2, 4, 2, NS], F32, s)
            lsrow = sb("lsrow", [P, 2], F32, s)
            sp_ = sb("sp_", [P, 80], F32, s)
            sm = sb("sm", [P, 34, NPAIR], F32, s)
            smi = sb("smi", [P, NPAIR], I32, s)
            apw = sb("apw", [P, 2, NPAIR, 9], F32, s)
            arev = sb("arev", [P, 2, NPAIR, 8], F32, s)
            braw = sb("braw", [P, 2, NPAIR, GC], F32, s)
            bb = sb("bb", [P, 2, NPAIR, GC], F32, s)
            cc = sb("cc", [P, 2, NPAIR, GC], F32, s)
            wlo = sb("wlo", [P, 2, NPAIR, 16], F32, s)
            whi = sb("whi", [P, 2, NPAIR, 8], F32, s)
            ctmp = sb("ctmp", [P, 2, NPAIR * GC], F32, s)
            hfin = sb("hfin", [P, 4, NPAIR], F32, s)
            hfrow = sb("hfrow", [64, P], F32, s)
            mask = sb("mask", [P, K], F32, s)
            hrow = sb("hrow", [16, DS], F32, s)
            hcol = sb("hcol", [P, 4, 16], F32, s)
            cnt = sb("cnt", [P, 4, 16], F32, s)
            pt = sb("pt", [P, 2, 4, L, GC], F32, s)
            qt = sb("qt", [P, 2, 4, L + 1, GC], F32, s)
            mtmp = sb("mtmp", [P, 2, 4, (L + 1) * GC], F32, s)
            bbst = sb("bbst", [P, 2, 4, 2, GC], F32, s)
            bint = sb("bint", [P, 2, 4, P], F32, s)
            taps = sb("taps", [P, 2 * P], F32, s)
            toep = sb("toep", [P, 8, P], F32, s)
            ur = sb("ur", [P, 8, K], F32, s)
            wt = sb("wt", [P, 2, 4, K], F32, s)
            dec = sb("dec", [P, 4, K], F32, s)
            dst_ = sb("dst_", [P, 8], F32, s)
            bst = sb("bst", [P, 6], F32, s)
            r1 = sb("r1", [P, 2, K], F32, s)
            r2 = sb("r2", [P, 2, K], F32, s)
            r3 = sb("r3", [P, 2, K], F32, s)
            r4 = sb("r4", [P, 2, K], F32, s)
            vr = sb("vr", [P, 2, K], F32, s)
            vi = sb("vi", [P, 2, K], F32, s)
            hb = sb("hb", [P, 2, 2, K + 1], F32, s)
            yv = sb("yv", [P, 4, K], F32, s)
            ya = sb("ya", [P, 4, K], F32, s)
            up = sb("up", [P, 4 * T], F32, s)
            ext = sb("ext", [P, L, K + 4], F32, s)
            sum_a = sb("sum_a", [P, L, K + 4], F32, s)
            tail = sb("tail", [P, 4, 2, 16], F32, s)
        mt = [ta[:, 0, :], ta[:, 1, :], tb[:, 0, :]]
        og = [tb[:, 1, :], std[:, :], rpost[:, :]]
        prow = mtmp[0:16].rearrange("p a b c -> p (a b c)")[:, 0:2 * DS].rearrange("p (w d) -> p w d", w=2)

        bank = [ctx.enter_context(nc.psum_tensor(f"bank{i}", [P, 512], F32)) for i in range(8)]
        PA, PB, PC = bank[0:3], bank[3:6], bank[6:8]

        w_loaded = [sem(f"w_loaded{i}") for i in range(RAW_SLOTS)]
        glu_value_loaded = sem("glu_value_loaded")
        w_hi_done, w_ready, pe_block = sem("w_hi_done"), sem("w_ready"), sem("pe_block")
        const_ready, vec_loaded = sem("const_ready"), sem("vec_loaded")
        vec_mm, vec_ready = sem("vec_mm"), sem("vec_ready")
        x_loaded = [sem(f"x_loaded{i}") for i in range(9)]
        x_turned, x_dve, x_act = sem("x_turned"), sem("x_dve"), sem("x_act")
        sq_done, sum_done, stat_done, std_done, recip_done = (sem(n) for n in ("sq_done", "sum_done", "stat_done", "std_done", "recip_done"))
        zhi_done, z_ready, h_done, t_done = sem("zhi_done"), sem("z_ready"), sem("h_done"), sem("t_done")
        acc_zero, acc_done = sem("acc_zero"), sem("acc_done")
        in_free, ta_done, silu_done, h_mul, hid_hi_done, hid_ready, out_free = (
            {f: sem(f"{n}{f}") for f in (1, 2, 3)} for n in ("in_free", "ta_done", "silu_done", "h_mul", "hid_hi_done", "hid_ready", "out_free"))
        h_spilled, h_back = sem("h_spilled"), sem("h_back")
        own = {n: sem(f"{n}_step") for n in ("dve_prep", "dve_mix", "dve_pool", "act_prep", "pool_prep")}
        sp_loaded, sp_mm, sp_ev = sem("sp_loaded"), sem("sp_mm"), sem("sp_ev")
        prep_act, prep_dve = sem("prep_act"), sem("prep_dve")
        m_scaled, m_out = sem("m_scaled"), sem("m_out")
        m_stored = [sem(f"m_stored{b}") for b in range(NB)]
        pq_ready, prep_mm, prep_ev = sem("pq_ready"), sem("prep_mm"), sem("prep_ev")
        taps_stored, toep_loaded, ur_loaded = sem("taps_stored"), sem("toep_loaded"), sem("ur_loaded")
        e_mm, e_read, hb_ready, y_mm, y_ev, gelu_in, sig_done, y_full, y_stored = (
            sem(n) for n in ("e_mm", "e_read", "hb_ready", "y_mm", "y_ev", "gelu_in", "sig_done", "y_full", "y_stored"))
        y_loaded = [sem(f"y_loaded{j}") for j in range(4)]
        y_hi_done, y_ready, pooled, pl_hi_done, pl_ready = sem("y_hi_done"), sem("y_ready"), sem("pooled"), sem("pl_hi_done"), sem("pl_ready")
        hist_mm, hist_ev, tail_ready, last_mm, last_ev = sem("hist_mm"), sem("hist_ev"), sem("tail_ready"), sem("last_mm"), sem("last_ev")
        gp_loaded = [sem(f"gp_loaded{i}") for i in range(2)]
        gp_stored = [sem(f"gp_stored{i}") for i in range(2)]
        pool_free, gp_done = sem("pool_free"), sem("gp_done")
        side_loaded = [sem(f"side_loaded{i}") for i in range(2)]
        sig_m, merge_a, merge_t, merge_read = sem("sig_m"), sem("merge_a"), sem("merge_t"), sem("merge_read")
        dcol_done, y_turned, yrow_ready = sem("dcol_done"), sem("y_turned"), sem("yrow_ready")
        y_out = [sem(f"y_out{i}") for i in range(4)]
        state_out = sem("state_out")

        block = ctx.enter_context(nc.Block())
        cols = lambda b: slice(b * BW, (b + 1) * BW)

        def fin_group(ph):
            return (MG if ph == 3 else FG) - 2

        def unit_source(key, g, q):
            if isinstance(key, tuple) and key[0] in (1, 2):
                f, what = key
                if what == "in":
                    c = of(lambda x: (2 * x + q // 2) * P + (q % 2) * DFF, g)
                    return a[f"ffn{f}_w_in"].rearrange("(k p) n -> p k n", p=P)[:, :, ds(c, P)], "k"
                return a[f"ffn{f}_w_out"][ds(of(lambda x: (2 * x + q) * P, g), P), :], None
            if key == "fin":
                t = 2 * (fin_group(g)) + q
                return (a["w_out"] if g == 3 else a[f"ffn{g}_w_out"])[t * P:(t + 1) * P, :], None
            if key == "mix":
                c = of(lambda x: (x * P, 4 * P + x * P)[q] if q < 2 else 8 * P + (4 * x + q - 2) * P, g)
                return a["w_in"].rearrange("(k p) n -> p k n", p=P)[:, :, ds(c, P)], "k"
            if key == "pool":
                return a["pool_w"].rearrange("g c o -> c g o"), "g"
            if key == "glu":
                c = (2 * g + q) * P
                return a["ssm_w_glu"].rearrange("(k p) (h n) -> p k h n", p=P, h=2)[:, :, :, c:c + P], "kh"
            return a["w_out"][(2 * g + q) * P:(2 * g + q + 1) * P, :], None

        def load_unit(sp, key, g, q):
            name = key if isinstance(key, tuple) else (key,)
            u_of = lambda x: plan.unit[(*name, x) if key != "pool" else "pool"] + q
            slot = of(lambda x: u_of(x) % RAW_SLOTS, g)
            if isinstance(g, Along) or u_of(g) >= RAW_SLOTS:
                sp.wait_ge(w_ready, of(lambda x: u_of(x) - RAW_SLOTS + 1, g))
            src, form = unit_source(key, g, q)
            dst = w_raw[:, slot, :]
            if form == "k":
                dst = dst.rearrange("p (k n) -> p k n", k=DT)
            elif form == "g":
                dst = dst.rearrange("p (g o) -> p g o", g=4)
            elif form == "kh":
                dst = dst.rearrange("p (k h n) -> p k h n", k=4, h=2)
                sp.dma_start(dst[:, :, 0, :], src[:, :, 0, :]).then_inc(glu_value_loaded, 16)
                sp.wait_ge(glu_value_loaded, 16 * (2 * g + q + 1))
                sp.dma_start(dst[:, :, 1, :], src[:, :, 1, :]).then_inc(w_loaded[slot], 16)
                return
            sp.dma_start(dst, src).then_inc(w_loaded[slot], 16)

        def loaded_value(u):
            return 16 * (u // RAW_SLOTS + 1)

        IN_Z = {plan.unit[("fin", ph)] + k: (plan.block[("fin", ph)], 2 * BW + P * (k - 2)) for ph in (1, 2, 3) for k in (2, 3)}

        def split_place(u):
            raw = w_raw[:, of(lambda x: x % RAW_SLOTS, u), :]
            if not isinstance(u, Along) and u in IN_Z:
                free, c = IN_Z[u]
                return z_hi[:, :, c:c + P], z_lo[:, :, c:c + P], raw.rearrange("p (m n) -> p m n", m=DT), free
            slot = of(lambda x: x % SPLIT_SLOTS, u)
            free = of(lambda x: plan.last[x - SPLIT_SLOTS], u) if isinstance(u, Along) or u >= SPLIT_SLOTS else 0
            return w_hi[:, slot, :], w_lo[:, slot, :], raw, free

        def split_hi(act, u):
            hi, _, raw, free = split_place(u)
            act.wait_ge(w_loaded[of(lambda x: x % RAW_SLOTS, u)], of(loaded_value, u))
            if isinstance(u, Along) or u >= SPLIT_SLOTS:
                act.wait_ge(pe_block, free)
            nc.scalar.activation(hi, raw, ACT.Copy).then_inc(w_hi_done, 1)

        def split_lo(dve, u):
            hi, lo, raw, _ = split_place(u)
            dve.wait_ge(w_hi_done, of(lambda x: x + 1, u))
            nc.vector.tensor_tensor(lo, raw, hi.bitcast(F32), ALU.subtract).then_inc(w_ready, 1)

        def three(out, lhs, rhs, first, last):
            (lh, ll), (rh, rl) = lhs, rhs
            nc.tensor.matmul(out, lh, rh, start=first, stop=False)
            nc.tensor.matmul(out, lh, rl, start=False, stop=False)
            return nc.tensor.matmul(out, ll, rh, start=False, stop=last)

        def wslices(slot, lo, hi):
            return w_hi[:, slot, lo:hi], w_lo[:, slot, lo:hi]

        def job(stage, kind, b):
            return {0: 0, 1: 3, 2: 9, 3: 15}[stage] + (3 if kind == "h" and stage else 0) + b

        def square(act, J, m, src):
            need = {0: 7 * (J - 1) + 6, 1: 7 * (J - 1) + 7, 2: 7 * J + 1}.get(m, 7 * J + m - 2)
            if need > 0:
                act.wait_ge(sum_done, need)
            nc.scalar.activation(sq[:, m % 2, :], src, ACT.Square).then_inc(sq_done, 1)

        def add_squares(pool, J):
            for m in range(1, DT):
                pool.wait_ge(sq_done, DT * J + m + 1)
                if m == 1 and J >= 2:
                    pool.wait_ge(stat_done, J - 1)
                if m > 1:
                    pool.wait_ge(sum_done, 7 * J + m - 1)
                nc.gpsimd.tensor_tensor(ssum[:, J % 2, :], sq[:, 0, :] if m == 1 else ssum[:, J % 2, :],
                                        sq[:, m % 2, :], ALU.add).then_inc(sum_done, 1)

        def stat(pe, J, out, free=None):
            pe.wait_ge(sum_done, 7 * J + 7)
            if free is not None:
                pe.wait_ge(*free)
            nc.tensor.matmul(out[:, 0:BW], ones[:, :], ssum[:, J % 2, :], start=True, stop=True).then_inc(stat_done, 1)

        def root(act, J, src):
            act.wait_ge(stat_done, J + 1)
            if J:
                act.wait_ge(recip_done, J)
            nc.scalar.activation(std[:, :], src[:, 0:BW], ACT.Sqrt, bias=epsc[:, 0:1], scale=1.0 / D).then_inc(std_done, 1)

        def recip(dve, J, dst):
            dve.wait_ge(std_done, J + 1)
            nc.vector.reciprocal(dst, std[:, :]).then_inc(recip_done, 1)

        STAT_H = [PC[0], PC[1], PC[0]]

        def z_hi_part(act, stage, b, m, gain):
            if stage:
                act.wait_ge(h_done, 24 * (stage - 1) + 8 * b + m + 1)
            nc.scalar.activation(z_hi[:, m, cols(b)], xres[:, m, cols(b)], ACT.Copy,
                                 scale=vecs[:, gain + m:gain + m + 1]).then_inc(zhi_done, 1)

        def z_lo_part(dve, stage, b, m, gain):
            dve.wait_ge(zhi_done, 24 * stage + 8 * b + m + 1)
            nc.vector.scalar_tensor_tensor(z_lo[:, m, cols(b)], xres[:, m, cols(b)], vecs[:, gain + m:gain + m + 1],
                                           z_hi[:, m, cols(b)].bitcast(F32), ALU.mult, ALU.subtract).then_inc(z_ready, 1)

        GAIN = {0: V_PRE1, 1: V_PREM, 2: V_PRE2}
        POST = {1: V_POST1, 2: V_POSTM, 3: V_POST2}
        tcount = [0]

        def residual(dve, stage, b):
            for m in range(DT + 1):
                if m < DT:
                    yield ("h", m)
                if m and stage < 3:
                    yield ("z", m - 1)

        def residual_step(dve, stage, b, what, m):
            if what == "z":
                z_lo_part(dve, stage, b, m, GAIN[stage])
                return
            g = POST[stage] + m
            slot = tcount[0] % 2
            nc.vector.scalar_tensor_tensor(ta[:, slot, :], acc[:, m, cols(b)], vecs[:, g:g + 1], rpost[:, :],
                                           ALU.mult, ALU.mult).then_inc(t_done, 1)
            tcount[0] += 1
            dve.wait_ge(t_done, tcount[0])
            if stage == 2 and m == 0:
                dve.wait_ge(h_back, 16 * (b + 1))
            nc.vector.scalar_tensor_tensor(xres[:, m, cols(b)], ta[:, slot, :], 0.5 if stage != 2 else 1.0,
                                           xres[:, m, cols(b)], ALU.mult, ALU.add).then_inc(h_done, 1)

        def out_key(ph, g):
            return (ph, "out", g) if ph != 3 else ("merge", g)

        def in_key(ph, g):
            return (ph, "in", g) if ph != 3 else ("glu", g)

        AROUND = [PC[0], PC[1], PA[0], PB[0], PA[1], PB[1], PA[2], PB[2]]

        def out_bank(n):
            index = lambda k: k % 8 if k < 16 else k % 2
            before = [k for k in range(n) if index(k) == index(n)]
            return AROUND[index(n)], before[-1] if before else None

        def pe_out(pe, ph, g):
            u = of(lambda x: plan.unit[out_key(ph, x)], g)
            s0 = of(lambda x: plan.unit[out_key(ph, x)] % SPLIT_SLOTS, g)
            hs = of(lambda x: 2 * (x % 2), g)
            pe.wait_ge(w_ready, u + 2)
            for b in range(NB):
                pe.wait_ge(hid_ready[ph], of(lambda x: 6 * x + 3 + b + 1, g))
                for m in range(DT):
                    n = 8 * b + m
                    out, before = out_bank(n)
                    out = out[:, 0:BW]
                    if before is not None:
                        pe.wait_ge(out_free[ph], of(lambda x: 24 * x + before + 27, g))
                    elif n < 2:
                        pe.wait_ge(out_free[ph], of(lambda x: 24 * x + n + 25, g))
                    else:
                        pe.wait_ge(in_free[ph], of(lambda x: 3 * (2 * min(x + 1, last_group(ph)) + 1) + (n - 2) // 2 + 4, g))
                    for k in range(2):
                        mm = three(out, wslices((s0 + k) % SPLIT_SLOTS, m * P, m * P + P),
                                   (hid_hi[:, hs + k, cols(b)], hid_lo[:, hs + k, cols(b)]), k == 0, k == 1)
                    mm.then_inc(pe_block, 1)

        def dve_out(dve, ph, g, b, m, bank=None):
            key = out_key(ph, g) if bank is None else ("fin", ph)
            dve.wait_ge(pe_block, of(lambda x: plan.block[out_key(ph, x) if bank is None else ("fin", ph)] + 8 * b + m + 1, g))
            dst = acc[:, m, cols(b)]
            dve.wait_ge(out_free[ph], of(lambda x: 24 * x + 8 * b + m + 3, g))
            nc.vector.tensor_tensor(dst, dst, (bank or out_bank(8 * b + m)[0])[:, 0:BW], ALU.add).then_inc(out_free[ph], 1)

        def last_group(ph):
            return (FG if ph != 3 else MG) - 1

        def stage_of(ph):
            return {1: 1, 3: 2, 2: 3}[ph]

        FIN_ROUND, FIN_BEFORE = [PB[0], PB[1], PB[2], PC[0]], [3, 5, 7, 0]
        STAT_ACC = [PA[0], PA[1], PC[1]]

        def fin_bank(n):
            return AROUND[n] if n < DT else FIN_ROUND[(n - DT) % 4]

        def pe_fin(pe, ph):
            g, st = fin_group(ph), stage_of(ph)
            u0 = plan.unit[("fin", ph)]

            def lhs(k, m):
                if u0 + k in IN_Z:
                    c = IN_Z[u0 + k][1]
                    return z_hi[:, m, c:c + P], z_lo[:, m, c:c + P]
                return wslices((u0 + k) % SPLIT_SLOTS, m * P, m * P + P)

            def part(b, m, ks):
                for k in ks:
                    h = (2 * g + k) % 4
                    mm = three(fin_bank(8 * b + m)[:, 0:BW], lhs(k, m), (hid_hi[:, h, cols(b)], hid_lo[:, h, cols(b)]),
                               k == 0, k == 3)
                return mm
            pe.wait_ge(w_ready, u0 + 2)
            pe.wait_ge(hid_ready[ph], 6 * (g + 1) + 3 + 1)
            for m in range(DT):
                if m < 2:
                    pe.wait_ge(out_free[ph], 24 * g + m + 25)
                else:
                    pe.wait_ge(in_free[ph], 3 * (2 * (g + 1) + 1) + (m - 2) // 2 + 4)
                part(0, m, (0, 1))
            pe.wait_ge(w_ready, u0 + 4)
            for m in range(DT):
                part(0, m, (2, 3)).then_inc(pe_block, 1)
            for b in (1, 2):
                pe.wait_ge(hid_ready[ph], 6 * (g + 1) + 3 + b + 1)
                for m in range(DT):
                    r = 8 * (b - 1) + m
                    before = FIN_BEFORE[r] if r < 4 else 8 + r - 4
                    pe.wait_ge(out_free[ph], 24 * g + 26 + before + 1)
                    part(b, m, range(4)).then_inc(pe_block, 1)
                    if m == 2:
                        stat(pe, job(st, "acc", b - 1), STAT_ACC[b - 1])

        def stat_fin(pe, ph):
            stat(pe, job(stage_of(ph), "acc", 2), STAT_ACC[2], (out_free[ph], 24 * fin_group(ph) + 26 + 24))

        def dve_last(dve, ph, next_units):
            st, g = stage_of(ph), fin_group(ph)
            last = plan.unit[("fin", ph)] + 2
            split_lo(dve, last)
            split_lo(dve, last + 1)

            def take(steps, n):
                for _ in range(n):
                    for what in [next(steps, None)]:
                        if what:
                            residual_step(dve, st, b_of[0], *what)
            b_of = [0]
            per = 2 if st < 3 else 1
            steps = iter(())
            for b in range(NB):
                for m in range(DT):
                    dve_out(dve, ph, g, b, m, fin_bank(8 * b + m))
                    if b and m == 3:
                        take(steps, per + 1)
                        b_of[0] = b - 1
                        recip(dve, job(st, "acc", b - 1), rpost[:, :])
                        dve.wait_ge(recip_done, job(st, "acc", b - 1) + 1)
                        steps = residual(dve, st, b - 1)
                    elif b:
                        take(steps, per)
            if ph == 3:
                dve.sem_inc(in_free[2], 3)
            for u in next_units:
                split_lo(dve, u)
            take(steps, 2 * DT)
            b_of[0] = 2
            recip(dve, job(st, "acc", 2), rpost[:, :])
            dve.wait_ge(recip_done, job(st, "acc", 2) + 1)
            take(residual(dve, st, 2), 2 * DT)

        def act_last(act, ph, next_units):
            st, g = stage_of(ph), fin_group(ph)
            last = plan.unit[("fin", ph)] + 2
            split_hi(act, last)
            split_hi(act, last + 1)

            def sqa(b, m):
                act.wait_ge(out_free[ph], 24 * g + 8 * b + m + 1 + 26)
                square(act, job(st, "acc", b), m, acc[:, m, cols(b)])

            def zh(b, m):
                if st < 3:
                    z_hi_part(act, st, b, m, GAIN[st])

            def sqh(b, m):
                if st < 3:
                    square(act, job(st, "h", b), m, xres[:, m, cols(b)])
            for m in range(DT):
                sqa(0, m)
            for b in (1, 2):
                for m in range(DT):
                    sqa(b, m)
                    if m < 4 and b == 2:
                        zh(0, m + 4)
                    if m == 3:
                        root(act, job(st, "acc", b - 1), STAT_ACC[b - 1])
                    if m >= 4:
                        zh(b - 1, m - 4)
            for u in next_units:
                split_hi(act, u)
            for m in range(4):
                zh(1, m + 4)
                sqh(0, 2 * m)
                sqh(0, 2 * m + 1)
            root(act, job(st, "acc", 2), STAT_ACC[2])
            for m in range(DT):
                zh(2, m)
                sqh(1, m)
            if st == 1:
                root(act, job(st, "h", 0), STAT_H[0])
            for m in range(DT):
                sqh(2, m)
            if st == 1:
                root(act, job(st, "h", 1), STAT_H[1])
                root(act, job(st, "h", 2), STAT_H[2])

        def pool_stage(pool, st):
            for b in range(NB):
                add_squares(pool, job(st, "acc", b))
            if st == 1:
                pool.wait_ge(pe_block, plan.block[("mix", 0)])
                nc.gpsimd.memset(hrow[:, :], 0.0).then_inc(const_ready, 1)
            if st < 3:
                for b in range(NB):
                    add_squares(pool, job(st, "h", b))

        def stats_h(pe, stage, b):
            J = job(stage, "h", b)
            stat(pe, J, STAT_H[b], (std_done, J - 1) if b == 2 else None)

        def pe_in(pe, f, g, hooks=None):
            z_before = 24 * (0 if f == 1 else 2)
            turns = [(q, b) for q in range(4) for b in range(NB)]
            if hooks:
                turns[:6] = [(q, b) for b in range(NB) for q in range(2)]
            for q, b in turns:
                u = of(lambda x: plan.unit[(f, "in", x)] + q, g)
                slot = of(lambda x: (plan.unit[(f, "in", x)] + q) % SPLIT_SLOTS, g)
                out = (PA, PB)[q % 2][b][:, 0:BW]
                if b == 0:
                    pe.wait_ge(w_ready, u + 1)
                if q % 2 == 0:
                    pe.wait_ge(in_free[f], of(lambda x: 3 * (2 * x + q // 2) + b + 1, g))
                if hooks and q == 0:
                    pe.wait_ge(z_ready, z_before + 8 * b + 8)
                for k in range(DT):
                    mm = three(out, wslices(slot, k * P, k * P + P), (z_hi[:, k, cols(b)], z_lo[:, k, cols(b)]),
                               k == 0, k == DT - 1)
                mm.then_inc(pe_block, 1)
                if hooks and (q, b) in hooks:
                    hooks[q, b]()

        def pe_ffn(pe, f):
            st = 0 if f == 1 else 2
            pe_in(pe, f, 0, {(0, 0): (lambda: stat_fin(pe, 3)) if f == 2 else (lambda: None),
                             (0, 1): lambda: stats_h(pe, st, 0), (0, 2): lambda: stats_h(pe, st, 1),
                             (1, 2): lambda: stats_h(pe, st, 2)})
            pe_in(pe, f, 1)
            with pe.Fori(0, 4) as i:
                g = Along(i, 4, 2, 0)
                pe_out(pe, f, g)
                pe_in(pe, f, g + 2)
                pe_out(pe, f, g + 1)
                pe_in(pe, f, g + 3)
            pe_out(pe, f, 8)
            pe_in(pe, f, 10)
            pe_fin(pe, f)
            if f == 2:
                stat_fin(pe, 2)

        def tile_blocks(g):
            return [(j, b, of(lambda x: 3 * (2 * x + j) + b, g)) for j in range(2) for b in range(NB)]

        def dve_ffn_in(dve, f, g, before=None):
            for j, b, n in tile_blocks(g):
                if b == 0:
                    for q in (0, 1):
                        split_lo(dve, unit_along(f, g, 2 * j + q + 2))
                if before and j == 0:
                    before(b)
                if before and j == 0:
                    dve.wait_ge(pe_block, plan.block[(f, "in", 0)] + 2 * b + 2)
                else:
                    dve.wait_ge(pe_block, of(lambda x: plan.block[(f, "in", x)] + 6 * j + 3 + b + 1, g))
                s = (3 * j + b) % 2
                nc.vector.tensor_tensor(ta[:, s, :], PA[b][:, 0:BW], rstd[:, cols(b)], ALU.mult).then_inc(ta_done[f], 1)
                nc.vector.tensor_tensor(tb[:, s, :], PB[b][:, 0:BW], rstd[:, cols(b)], ALU.mult).then_inc(in_free[f], 1)
                dve.wait_ge(silu_done[f], n + 1)
                dve.wait_ge(in_free[f], n + 1 + 3)
                nc.vector.tensor_tensor(tb[:, s, :], tb[:, s, :], ta[:, s, :], ALU.mult).then_inc(h_mul[f], 1)
                dve.wait_ge(hid_hi_done[f], n + 1)
                hs = of(lambda x: 2 * (x % 2) + j, g)
                nc.vector.tensor_tensor(hid_lo[:, hs, cols(b)], tb[:, s, :], hid_hi[:, hs, cols(b)].bitcast(F32),
                                        ALU.subtract).then_inc(hid_ready[f], 1)

        def unit_along(f, g, ahead):
            if isinstance(g, Along):
                v = [plan.unit[(f, "in", g.a * k + g.b)] + ahead for k in range(g.n)]
                return Along(g.i, g.n, v[1] - v[0], v[0])
            return plan.unit[(f, "in", g)] + ahead

        def act_ffn_in(act, f, g, first=False, before=None):
            for j, b, n in tile_blocks(g):
                if b == 0:
                    for q in (0, 1):
                        split_hi(act, unit_along(f, g, 2 * j + q + 2))
                s = (3 * j + b) % 2
                if before and j == 0:
                    before(b)
                act.wait_ge(ta_done[f], n + 1)
                nc.scalar.activation(ta[:, s, :], ta[:, s, :], ACT.Silu).then_inc(silu_done[f], 1)
                act.wait_ge(h_mul[f], n + 1)
                if not first and j == 0 and b == 0:
                    act.wait_ge(pe_block, of(lambda x: plan.block[(f, "out", x - 2)] + 24, g))
                hs = of(lambda x: 2 * (x % 2) + j, g)
                nc.scalar.activation(hid_hi[:, hs, cols(b)], tb[:, s, :], ACT.Copy).then_inc(hid_hi_done[f], 1)

        def out_unit(ph, g):
            if isinstance(g, Along):
                v = [plan.unit[out_key(ph, g.a * k + g.b)] for k in range(g.n)]
                return Along(g.i, g.n, v[1] - v[0], v[0])
            return plan.unit[out_key(ph, g)]

        def dve_outs(dve, ph, g):
            split_lo(dve, out_unit(ph, g) + 2)
            for b in range(NB):
                for m in range(DT):
                    dve_out(dve, ph, g, b, m)
            split_lo(dve, out_unit(ph, g) + 3)

        def act_outs(act, ph, g):
            split_hi(act, out_unit(ph, g) + 2)
            split_hi(act, out_unit(ph, g) + 3)

        def dve_ffn(dve, f, before, next_units):
            dve_ffn_in(dve, f, 0, before)
            dve_ffn_in(dve, f, 1)
            dve.wait_ge(acc_zero, 1 if f == 1 else 3)
            dve.sem_inc(out_free[f], 26)
            with dve.Fori(0, 4) as i:
                g = Along(i, 4, 2, 0)
                dve_outs(dve, f, g)
                dve_ffn_in(dve, f, g + 2)
                dve_outs(dve, f, g + 1)
                dve_ffn_in(dve, f, g + 3)
            dve_outs(dve, f, 8)
            dve_ffn_in(dve, f, 10)
            dve_last(dve, f, next_units)

        def act_ffn(act, f, next_units):
            st = 0 if f == 1 else 2
            act_ffn_in(act, f, 0, True, lambda b: root(act, job(st, "h", b), STAT_H[b]))
            act_ffn_in(act, f, 1, True)
            with act.Fori(0, 4) as i:
                g = Along(i, 4, 2, 0)
                act_outs(act, f, g)
                act_ffn_in(act, f, g + 2)
                act_outs(act, f, g + 1)
                act_ffn_in(act, f, g + 3)
            act_outs(act, f, 8)
            act_ffn_in(act, f, 10)
            act_last(act, f, next_units)

        def sp_ffn(sp, f, skip=0):
            def ins(g, start=0):
                for q in range(start, 4):
                    load_unit(sp, (f, "in"), g, q)

            def outs(g):
                for q in range(2):
                    load_unit(sp, (f, "out"), g, q)
            ins(0, skip)
            ins(1)
            with sp.Fori(0, 4) as i:
                g = Along(i, 4, 2, 0)
                outs(g)
                ins(g + 2)
                outs(g + 1)
                ins(g + 3)
            outs(8)
            ins(10)
            for q in range(4):
                load_unit(sp, "fin", f, q)

        def vec_rows(sp):
            names = [("ffn1_pre_g", V_PRE1), ("ffn1_post_g", V_POST1), ("mix_pre_g", V_PREM), ("mix_post_g", V_POSTM),
                     ("ffn2_pre_g", V_PRE2), ("ffn2_post_g", V_POST2), ("pool_scale", V_PSC), ("b_in", V_BIN),
                     ("ssm_b_glu", V_BGLU)]
            for name, r in names:
                n = a[name].shape[0] // P
                sp.dma_start(vrow[r:r + n, :], a[name].rearrange("(n p) -> n p", p=P)).then_inc(vec_loaded, 16)
            for t in range(L):
                sp.dma_start(vrow[V_D:V_D + G, t * GC:(t + 1) * GC],
                             a["ssm_d"].rearrange("(g c) -> g c", c=GC)).then_inc(vec_loaded, 16)
            return 16 * (len(names) + L)
        VEC_DMAS = 16 * 17
        ORDER = [8, 0, 1, 2, 3, 4, 5, 6, 7]

        def sp_start(sp):
            xp = a["x_prompt"].rearrange("(k s) d -> s k d", s=L)
            for n, tile in enumerate(ORDER):
                if tile == 8:
                    sp.dma_start(xrow[0:DEC, 8, :], a["x_sample"]).then_inc(x_loaded[8], 16)
                else:
                    sp.dma_start(xrow[:, tile, :], xp[tile]).then_inc(x_loaded[tile], 16)
                if n == 1:
                    vec_rows(sp)
                if n == 3:
                    for q in range(3):
                        load_unit(sp, (1, "in"), 0, q)

        def pe_start(pe):
            pe.wait_ge(const_ready, 5)
            pe.wait_ge(vec_loaded, VEC_DMAS)
            nc.tensor.transpose(PC[0][:, 0:P], vrow[:, :], ident[:, :]).then_inc(vec_mm, 1)
            F = 0
            for tile in ORDER:
                rows = DEC if tile == 8 else P
                pe.wait_ge(x_loaded[tile], 16)
                for half in range(2):
                    if F >= 6:
                        pe.wait_ge(x_dve if F % 2 == 0 else x_act, (F - 6) // 2 + 1)
                    for j in range(4):
                        m = 4 * half + j
                        mm = nc.tensor.transpose(bank[F % 6][:, j * P:j * P + rows], xrow[0:rows, tile, m * P:(m + 1) * P],
                                                 ident[0:rows, 0:rows])
                    mm.then_inc(x_turned, 1)
                    F += 1

        def empty_x(eng, copy, which, done):
            F = 0
            for tile in ORDER:
                for half in range(2):
                    if F % 2 == which:
                        eng.wait_ge(x_turned, F + 1)
                        src = bank[F % 6][:, :].rearrange("p (j t) -> p j t", j=4)
                        dst = xres[:, 4 * half:4 * half + 4, :]
                        if tile < 8:
                            copy(dst[:, :, tile * K:tile * K + KP], src[:, :, 0:P]).then_inc(done, 1)
                        else:
                            for j in range(4):
                                ins = copy(dst[:, j, :].rearrange("p (s k) -> p s k", s=L)[:, :, KP:K],
                                           src[:, j, 0:DEC].rearrange("p (k s) -> p s k", s=L))
                            ins.then_inc(done, 1)
                    F += 1

        S = {n: k for k, n in enumerate("dt mag th n r sn sh cs ar ai den rden nr fr fi t0 t1 p x w2r w2i w4r w4i w8r w8i m2 m4 m8 rhr rhi un lrdt e0 e1".split())}
        LRE, LIM, H0R, H0I, LST = range(0, 80, 16)
        PREP_DMAS = 16 * 14

        def sp_prep(sp):
            sp.wait_ge(pe_block, plan.block[("mix", 0)])
            rows = lambda n: a[n].rearrange("(j g) s -> j (g s)", g=2)
            for r, n in ((LRE, "ssm_lambda_re"), (LIM, "ssm_lambda_im"), (H0R, "state_ssm_re"), (H0I, "state_ssm_im")):
                sp.dma_start(srow[r:r + 16, :], rows(n)).then_inc(sp_loaded, 16)
            sp.dma_start(lsrow[LST:LST + 16, :], a["ssm_log_step"].rearrange("(j g) -> j g", g=2)).then_inc(sp_loaded, 16)
            for c, n in enumerate(("ssm_b_re", "ssm_b_im")):
                sp.dma_start(braw[:, c], a[n].rearrange("(j g) s c -> g s j c", g=2).rearrange("g s j c -> (g s) j c")
                             ).then_inc(sp_loaded, 16)
            for c, n in enumerate(("ssm_c_re", "ssm_c_im")):
                for twice in range(2):
                    sp.dma_start(crow[:, c, :, twice, :], a[n].rearrange("g c s -> (g c) s").rearrange("(t p) s -> p t s", p=P)
                                 ).then_inc(sp_loaded, 16)
            sp.wait_ge(const_ready, 6)
            sp.dma_start(hrow[1:16, :], a["cache_pool"]).then_inc(sp_loaded, 16)
            sp.dma_start(cnt[:, :, :], a["window_counts"]).then_inc(sp_loaded, 16)
            sp.dma_start(mask[:, :], a["scan_mask"]).then_inc(sp_loaded, 16)

        def pe_prep(pe):
            pe.wait_ge(sp_loaded, PREP_DMAS)
            pe.wait_ge(prep_dve, 1)
            nc.tensor.transpose(PB[0][:, 0:80], srow[0:80, :], ident[0:80, 0:80])
            for g in range(4):
                nc.tensor.transpose(PB[0][:, P + 16 * g:P + 16 * g + 16], hrow[:, g * P:(g + 1) * P], ident[0:16, 0:16])
            for c in range(2):
                for t in range(4):
                    mm = nc.tensor.transpose(PB[1 + c][:, t * P:(t + 1) * P],
                                             crow[:, c, t].rearrange("p a s -> p (a s)"), ident[:, :])
            mm.then_inc(sp_mm, 1)

        class Steps:

            def __init__(self, eng, s, i=None, per=0, base=0):
                self.eng, self.s, self.i, self.per, self.base, self.n = eng, s, i, per, base, 0

            def do(self, ins):
                self.n += 1
                ins.then_inc(self.s, 1)

            def sync(self):
                if self.base + self.n > 0 or self.i is not None:
                    v = self.base + self.n
                    self.eng.wait_ge(self.s, v if self.i is None else self.i * self.per + v)

        def take(dst, src):
            return nc.vector.tensor_scalar(dst, src, 1.0, None, ALU.mult)

        def cmul(st, out, x, y, tmp, conj_x=False, neg_im=False):
            tt = nc.vector.tensor_tensor
            (xr, xi), (yr, yi), (t0, t1) = x, y, tmp
            st.do(tt(t0, xr, yr, ALU.mult))
            st.do(tt(t1, xi, yi, ALU.mult))
            st.sync()
            st.do(tt(out[0], t0, t1, ALU.add if conj_x else ALU.subtract))
            st.sync()
            st.do(tt(t0, xr, yi, ALU.mult))
            st.do(tt(t1, xi, yr, ALU.mult))
            st.sync()
            if neg_im:
                st.do(nc.vector.scalar_tensor_tensor(out[1], t0, -1.0, t1, ALU.mult, ALU.subtract))
            else:
                st.do(tt(out[1], t0, t1, ALU.subtract if conj_x else ALU.add))

        v = lambda n: sm[:, S[n], :]
        MAGIC = 12582912.0

        def chain_exp(st, out, x):
            ts, stt = nc.vector.tensor_scalar, nc.vector.scalar_tensor_tensor
            st.sync(); st.do(ts(v("x"), x, -87.0, 87.0, ALU.max, ALU.min))
            st.sync(); st.do(ts(v("t0"), v("x"), 1.4426950408889634, MAGIC, ALU.mult, ALU.add))
            st.sync(); st.do(ts(v("n"), v("t0"), MAGIC, None, ALU.subtract))
            st.sync(); st.do(stt(v("r"), v("n"), -0.693359375, v("x"), ALU.mult, ALU.add))
            st.do(ts(smi[:, :], v("n"), 127.0, 8388608.0, ALU.add, ALU.mult))
            st.sync(); st.do(stt(v("x"), v("n"), 2.12194440054690583e-4, v("r"), ALU.mult, ALU.add))
            st.sync(); st.do(ts(v("p"), v("x"), 1 / 5040, None, ALU.mult))
            for c in (1 / 720, 1 / 120, 1 / 24, 1 / 6, 0.5, 1.0):
                st.sync(); st.do(stt(v("p"), v("p"), c, v("x"), ALU.add, ALU.mult))
            st.sync(); st.do(stt(out, v("p"), 1.0, smi[:, :].bitcast(F32), ALU.add, ALU.mult))

        def dve_prep_a(dve):
            ts, stt, tt, cp = nc.vector.tensor_scalar, nc.vector.scalar_tensor_tensor, nc.vector.tensor_tensor, nc.vector.tensor_copy
            dve.wait_ge(sp_loaded, PREP_DMAS)
            nc.vector.tensor_copy(srow[LST:LST + 16, :].rearrange("j (g s) -> j g s", g=2),
                                  lsrow[LST:LST + 16, :].unsqueeze(2).broadcast_to([16, 2, NS])).then_inc(prep_dve, 1)
            st = Steps(dve, own["dve_prep"])
            dve.wait_ge(sp_mm, 1)
            st.do(cp(sp_[:, :], PB[0][:, 0:80]))
            st.do(cp(hcol[:, :, :].rearrange("p g r -> p (g r)"), PB[0][:, P:P + 64]))
            for c in range(2):
                for h in range(2):
                    half = slice(64 * h, 64 * h + 64)
                    st.do(cp(cc[half, c], PB[1 + c][half, :].rearrange("p (j g c) -> p j g c", g=2, c=GC)[:, :, h, :]))
            chain_exp(st, v("dt"), sp_[:, LST:LST + 16])
            st.sync()
            st.do(tt(v("lrdt"), sp_[:, LRE:LRE + 16], v("dt"), ALU.mult))
            st.do(tt(v("th"), sp_[:, LIM:LIM + 16], v("dt"), ALU.mult))
            chain_exp(st, v("mag"), v("lrdt"))
            st.sync(); st.do(ts(v("t0"), v("th"), 1 / (2 * pi), MAGIC, ALU.mult, ALU.add))
            st.sync(); st.do(ts(v("n"), v("t0"), MAGIC, None, ALU.subtract))
            x = v("th")
            for c in (6.28125, 0.00193500518798828125, 3.0199159819567e-7):
                st.sync(); st.do(stt(v("r"), v("n"), -c, x, ALU.mult, ALU.add))
                x = v("r")
            st.sync(); st.do(ts(v("r"), v("r"), -3.1415925, 3.1415925, ALU.max, ALU.min))
            st.sync()
            dve.sem_inc(prep_dve, 1)
            return st

        def unit_modulus(st, re, im, t0, t1):
            tt = nc.vector.tensor_tensor
            st.sync()
            st.do(tt(t0, re, re, ALU.mult))
            st.do(tt(t1, im, im, ALU.mult))
            st.sync(); st.do(tt(t0, t0, t1, ALU.add))
            st.sync(); st.do(nc.vector.tensor_scalar(t0, t0, -0.5, 1.5, ALU.mult, ALU.add))
            st.sync()
            st.do(tt(re, re, t0, ALU.mult))
            st.do(tt(im, im, t0, ALU.mult))
            st.sync()

        def act_prep(act):
            act.wait_ge(prep_dve, 2)
            nc.scalar.activation(v("sn"), v("r"), ACT.Sin).then_inc(prep_act, 1)
            nc.scalar.activation(v("sh"), v("r"), ACT.Sin, scale=0.5).then_inc(prep_act, 1)

        def dve_prep_b(dve, st):
            ts, stt, tt, cp = nc.vector.tensor_scalar, nc.vector.scalar_tensor_tensor, nc.vector.tensor_tensor, nc.vector.tensor_copy
            dve.wait_ge(prep_act, 2)
            st.do(tt(v("t0"), v("sh"), v("sh"), ALU.mult))
            st.sync(); st.do(ts(v("cs"), v("t0"), -2.0, 1.0, ALU.mult, ALU.add))
            st.sync()
            st.do(tt(v("ar"), v("mag"), v("cs"), ALU.mult))
            st.do(tt(v("ai"), v("mag"), v("sn"), ALU.mult))
            lr, li = sp_[:, LRE:LRE + 16], sp_[:, LIM:LIM + 16]
            st.do(tt(v("t0"), lr, lr, ALU.mult))
            st.do(tt(v("t1"), li, li, ALU.mult))
            st.sync()
            st.do(tt(v("den"), v("t0"), v("t1"), ALU.add))
            st.do(ts(v("nr"), v("ar"), 1.0, None, ALU.subtract))
            st.sync(); st.do(nc.vector.reciprocal(v("rden"), v("den")))
            cmul(st, (v("fr"), v("fi")), (lr, li), (v("nr"), v("ai")), (v("t0"), v("t1")), conj_x=True)
            st.sync()
            st.do(tt(v("fr"), v("fr"), v("rden"), ALU.mult))
            st.do(tt(v("fi"), v("fi"), v("rden"), ALU.mult))
            st.sync()
            f3 = lambda n: v(n).unsqueeze(2).broadcast_to([P, NPAIR, GC])
            tmp = [ctmp[:, c, :].rearrange("p (j c) -> p j c", c=GC) for c in range(2)]
            cmul(st, (bb[:, 0], bb[:, 1]), (f3("fr"), f3("fi")), (braw[:, 0], braw[:, 1]), tmp)
            st.do(nc.vector.memset(apw[:, 0, :, 0:1], 1.0))
            st.do(nc.vector.memset(apw[:, 1, :, 0:1], 0.0))
            st.do(cp(apw[:, 0, :, 1:2], v("ar").unsqueeze(2)))
            st.do(cp(apw[:, 1, :, 1:2], v("ai").unsqueeze(2)))

            def powers(tab, lo, n, by):
                st.sync()
                t = [ctmp[:, c, 0:NPAIR * n].rearrange("p (j k) -> p j k", k=n) for c in range(2)]
                cmul(st, [tab[:, c, :, by + 1 if lo else by + 1:by + 1 + n] for c in range(2)],
                     [tab[:, c, :, lo:lo + n] for c in range(2)],
                     [tab[:, c, :, by:by + 1].broadcast_to([P, NPAIR, n]) for c in range(2)], t)
            powers(apw, 1, 1, 1)
            powers(apw, 1, 2, 2)
            powers(apw, 1, 4, 4)
            st.sync()
            for c in range(2):
                for k in range(L):
                    st.do(cp(arev[:, c, :, L - 1 - k:L - k], apw[:, c, :, k:k + 1]))
            x = ("cs", "sn")
            for y in (("w2r", "w2i"), ("w4r", "w4i"), ("w8r", "w8i")):
                st.sync()
                cmul(st, (v(y[0]), v(y[1])), (v(x[0]), v(x[1])), (v(x[0]), v(x[1])), (v("t0"), v("t1")))
                x = y
            unit_modulus(st, v("w8r"), v("w8i"), v("t0"), v("t1"))
            x = "mag"
            for y in ("m2", "m4", "m8"):
                st.sync(); st.do(tt(v(y), v(x), v(x), ALU.mult))
                x = y
            st.sync()
            for c, n in enumerate(("w8r", "w8i")):
                st.do(cp(wlo[:, c, :, 0:1], v(n).unsqueeze(2)))
                st.do(nc.vector.memset(whi[:, c, :, 0:1], 1.0 - c))
                st.do(tt(v(("rhr", "rhi")[c]), v("m8"), sp_[:, (H0R, H0I)[c]:(H0R, H0I)[c] + 16], ALU.mult))

            def spread(tab, lo, n, by):
                st.sync()
                t = [ctmp[:, c, 0:NPAIR * n].rearrange("p (j k) -> p j k", k=n) for c in range(2)]
                cmul(st, [tab[:, c, :, by + 1:by + 1 + n] for c in range(2)],
                     [tab[:, c, :, lo:lo + n] for c in range(2)],
                     [tab[:, c, :, by:by + 1].broadcast_to([P, NPAIR, n]) for c in range(2)], t)
            for n in (1, 2, 4, 8):
                spread(wlo, 0, n, n - 1)
            flat = lambda tab, c: tab[:, c].rearrange("p j k -> p (j k)")
            unit_modulus(st, flat(wlo, 0), flat(wlo, 1), ctmp[:, 0, :], ctmp[:, 1, :])
            for c in range(2):
                st.do(cp(whi[:, c, :, 1:2], wlo[:, c, :, 15:16]))
            spread(whi, 1, 1, 1)
            spread(whi, 1, 1, 2)
            spread(whi, 1, 3, 3)
            spread(whi, 1, 1, 6)
            unit_modulus(st, flat(whi, 0), flat(whi, 1), ctmp[:, 0, 0:8 * NPAIR], ctmp[:, 1, 0:8 * NPAIR])

        def mix_unit(i, q):
            return Along(i, 4, 6, plan.unit[("mix", 0)] + q)

        def mix_block(i, q, b):
            v0 = plan.block[("mix", 0)]
            return i * 18 + (v0 + 3 * q + b + 1)

        def pe_mix(pe):
            for b in range(NB):
                stats_h(pe, 1, b)
            pe.wait_ge(z_ready, 48)
            with pe.Fori(0, 4) as i:
                for q in range(6):
                    pe.wait_ge(w_ready, i * 6 + (plan.unit[("mix", 0)] + q + 1))
                    slot = (plan.unit[("mix", 0)] + q) % SPLIT_SLOTS
                    for b in range(NB):
                        pe.wait_ge(m_scaled, i * 18 + (3 * q + b + 1))
                        for k in range(DT):
                            mm = three(PA[b][:, 0:BW], wslices(slot, k * P, k * P + P),
                                       (z_hi[:, k, cols(b)], z_lo[:, k, cols(b)]), k == 0, k == DT - 1)
                        mm.then_inc(pe_block, 1)
                    if q == 1:
                        pe_tables(pe, i)
                    if q in (2, 4):
                        pe_states(pe, i, q // 2 - 1)
                    if q in (3, 5):
                        pe_y(pe, i, q // 2 - 1)

        def pe_tables(pe, i):
            pe.wait_ge(pq_ready, i + 1)
            pe.wait_ge(e_read, i * 2 + 1)
            for c in range(2):
                for p in range(4):
                    mm = nc.tensor.transpose(PB[c][:, p * P:(p + 1) * P], pt[:, c, p].rearrange("p s c -> p (s c)"), ident[:, :])
                mm.then_inc(prep_mm, 1)
            for p in range(4):
                for c in range(2):
                    mm = nc.tensor.matmul(PB[2][32 * p:32 * p + 32, 0:P], bbst[:, c, p].rearrange("p g c -> p (g c)"),
                                          qt[:, c, p, 0:L, :].rearrange("p k c -> p (k c)"), start=(c == 0), stop=(c == 1))
            mm.then_inc(prep_mm, 1)

        def pe_states(pe, i, hf):
            if hf == 0:
                pe.wait_ge(prep_ev, i * 3 + 3)
                pe.wait_ge(ur_loaded, (i + 1) * 128)
            else:
                pe.wait_ge(e_read, i * 2 + 2)
            for c in range(2):
                for qq in range(2):
                    for h in range(2):
                        p = 2 * hf + qq
                        mm = nc.tensor.matmul(PB[c][64 * h:64 * h + 64, qq * K:(qq + 1) * K], bint[:, c, p, 64 * h:64 * h + 64],
                                              ur[:, 2 * p + h, :], start=True, stop=True)
            mm.then_inc(e_mm, 1)

        def pe_y(pe, i, hf):
            if hf == 0:
                pe.wait_ge(toep_loaded, (i + 1) * 128)
            pe.wait_ge(hb_ready, i * 2 + (hf + 1))
            pe.wait_ge(y_ev, i * 2 + (hf + 1))
            for qq in range(2):
                p = 2 * hf + qq
                out = [PC[h][:, qq * K:(qq + 1) * K] for h in range(2)]
                for h in range(2):
                    nc.tensor.matmul(out[h], toep[:, 2 * p + h, :], ur[:, 2 * p + h, :], start=True, stop=False)
                for h in range(2):
                    rows = slice(64 * h, 64 * h + 64)
                    for c in range(2):
                        mm = nc.tensor.matmul(out[h], qt[rows, c, p, 1:L + 1, :].rearrange("p k c -> p (k c)"),
                                              hb[rows, c, qq, 0:K], start=False, stop=(c == 1))
            mm.then_inc(y_mm, 1)

        DVE_PER = 82

        def dve_mix(dve):
            tt, stt, cp = nc.vector.tensor_tensor, nc.vector.scalar_tensor_tensor, nc.vector.tensor_copy
            dve.wait_ge(h_spilled, 48)
            dve.sem_inc(m_scaled, 3)
            dve.sem_inc(e_read, 1)
            dve.sem_inc(y_ev, 1)
            pre = Steps(dve, own["dve_mix"])
            pre.do(nc.vector.memset(taps[:, 0:P], 0.0))
            pre.do(nc.vector.memset(hb[:, :, :, 0:1], 0.0))
            pre.sync()
            with dve.Fori(0, 4) as i:
                st = Steps(dve, own["dve_mix"], i, DVE_PER, 2)
                st.sync()
                pairs = lambda tab, c: tab[:, c, ds(i * 4, 4)]

                def evac(q):
                    for b in range(NB):
                        dve.wait_ge(pe_block, mix_block(i, q, b))
                        dve.wait_ge(m_out, i * 18 + (3 * q + b + 1))
                        tt(mt[b], PA[b][:, 0:BW], rstd[:, cols(b)], ALU.mult).then_inc(m_scaled, 1)

                split_lo(dve, mix_unit(i, 2))
                dve.wait_ge(y_mm, i * 2 + 1)
                shp = lambda k: [P, 4, k, GC]
                tmp = lambda k: [mtmp[:, c, :, 0:k * GC].rearrange("p j (k c) -> p j k c", c=GC) for c in range(2)]
                per_k = lambda tab, c, k: pairs(tab, c).unsqueeze(3).broadcast_to(shp(k))
                per_c = lambda tab, c, k: pairs(tab, c).unsqueeze(2).broadcast_to(shp(k))
                cmul(st, (pt[:, 0], pt[:, 1]), [per_k(arev, c, L) for c in range(2)], [per_c(bb, c, L) for c in range(2)], tmp(L))
                st.do(take(dst_[:, :], vecs[:, ds(i * 8 + V_D, 8)]))
                st.do(take(bst[:, 0:1], vecs[:, ds(i * 1 + V_BIN, 1)]))
                st.do(take(bst[:, 1:2], vecs[:, ds(i * 1 + (V_BIN + 4), 1)]))
                st.do(take(bst[:, 2:6], vecs[:, ds(i * 4 + (V_BIN + 8), 4)]))
                st.sync()
                evac(0)
                cmul(st, (qt[:, 0], qt[:, 1]), [per_k(apw, c, L + 1) for c in range(2)], [per_c(cc, c, L + 1) for c in range(2)],
                     tmp(L + 1), neg_im=True)
                for c in range(2):
                    st.do(nc.vector.memset(bbst[:, c], 0.0))
                st.sync()
                for c in range(2):
                    for h in range(2):
                        rows = slice(64 * h, 64 * h + 64)
                        st.do(take(bbst[rows, c, :, h, :], bb[rows, c, ds(i * 4, 4)]))
                st.sync()
                dve.sem_inc(pq_ready, 1)
                split_lo(dve, mix_unit(i, 3))
                evac(1)
                for c in range(2):
                    dve.wait_ge(prep_mm, i * 3 + (c + 1))
                    cp(bint[:, c].rearrange("p j s -> p (j s)"), PB[c][:, :]).then_inc(prep_ev, 1)
                dve.wait_ge(prep_mm, i * 3 + 3)
                cp(taps[:, P:2 * P], PB[2][:, 0:P]).then_inc(prep_ev, 1)
                split_lo(dve, mix_unit(i, 4))
                w4 = [P, 4, L, 16]
                wtv = [wt[:, c, :, 0:KP].rearrange("p j (a b) -> p j a b", b=16) for c in range(2)]
                tw = [mtmp[:, c, :, 0:KP].rearrange("p j (a b) -> p j a b", b=16) for c in range(2)]
                cmul(st, wtv, [pairs(whi, c).unsqueeze(3).broadcast_to(w4) for c in range(2)],
                     [pairs(wlo, c).unsqueeze(2).broadcast_to(w4) for c in range(2)], tw)
                st.sync()
                st.do(cp(wt[:, :, :, KP:K], wt[:, :, :, 0:KS]))
                st.do(tt(dec[:, :, :], sm[:, S["m8"], ds(i * 4, 4)].unsqueeze(2).broadcast_to([P, 4, K]),
                         mask[:, :].unsqueeze(1).broadcast_to([P, 4, K]), ALU.mult))
                st.sync()
                evac(2)
                split_lo(dve, mix_unit(i, 5))
                dve_states(dve, st, i, 0)
                evac(3)
                split_lo(dve, mix_unit(i, 6))
                dve_y(dve, st, i, 0)
                evac(4)
                split_lo(dve, mix_unit(i, 7))
                dve_states(dve, st, i, 1)
                evac(5)
                dve_y(dve, st, i, 1)
                assert st.n == DVE_PER, st.n

        def dve_states(dve, st, i, hf):
            tt, stt, cp = nc.vector.tensor_tensor, nc.vector.scalar_tensor_tensor, nc.vector.tensor_copy
            dve.wait_ge(e_mm, i * 2 + (hf + 1))
            E = [PB[c][:, 0:2 * K].rearrange("p (q k) -> p q k", k=K) for c in range(2)]
            w = [wt[:, c, 2 * hf:2 * hf + 2, :] for c in range(2)]
            st.do(tt(r1[:, :, :], E[0], w[0], ALU.mult))
            st.do(tt(r2[:, :, :], E[1], w[1], ALU.mult))
            st.do(tt(r3[:, :, :], E[1], w[0], ALU.mult))
            tt(r4[:, :, :], E[0], w[1], ALU.mult).then_inc(e_read, 1)
            dve.wait_ge(e_read, i * 2 + (hf + 2))
            st.sync()
            st.do(tt(vr[:, :, :], r1[:, :, :], r2[:, :, :], ALU.add))
            st.do(tt(vi[:, :, :], r3[:, :, :], r4[:, :, :], ALU.subtract))
            st.sync()
            pr = lambda n: sm[:, S[n], ds(i * 4 + 2 * hf, 2)].unsqueeze(2)
            st.do(tt(vr[:, :, KP:KP + 1], vr[:, :, KP:KP + 1], pr("rhr"), ALU.add))
            st.do(tt(vi[:, :, KP:KP + 1], vi[:, :, KP:KP + 1], pr("rhi"), ALU.add))
            st.sync()
            flat = lambda x: x.rearrange("p q k -> p (q k)")
            dd = flat(dec[:, 2 * hf:2 * hf + 2, :])
            st.do(nc.vector.tensor_tensor_scan(flat(r1[:, :, :]), dd, flat(vr[:, :, :]), 0.0, ALU.mult, ALU.add))
            st.do(nc.vector.tensor_tensor_scan(flat(r2[:, :, :]), dd, flat(vi[:, :, :]), 0.0, ALU.mult, ALU.add))
            st.sync()
            cmul(st, [hb[:, c, :, 1:K + 1] for c in range(2)], w, (r1[:, :, :], r2[:, :, :]), (r3[:, :, :], r4[:, :, :]))
            st.sync()
            for c in range(2):
                st.do(take(hfin[:, c, ds(i * 4 + 2 * hf, 2)].unsqueeze(2), hb[:, c, :, KP:KP + 1]))
                st.do(take(hfin[:, 2 + c, ds(i * 4 + 2 * hf, 2)].unsqueeze(2), hb[:, c, :, K:K + 1]))
            st.sync()
            for c in range(2):
                st.do(take(hb[:, c, :, KP:KP + 1], sp_[:, ds(i * 4 + (2 * hf + (H0R, H0I)[c]), 2)].unsqueeze(2)))
            st.sync()
            dve.sem_inc(hb_ready, 1)

        def dve_y(dve, st, i, hf):
            tt, stt = nc.vector.tensor_tensor, nc.vector.scalar_tensor_tensor
            dve.wait_ge(y_mm, i * 2 + (hf + 2))
            dve.wait_ge(y_stored, i * 256 + 128 * (hf + 1))
            for j in range(4):
                qq, h = j // 2, j % 2
                g = 4 * hf + j
                ins = stt(yv[:, j, :], ur[:, g, :], dst_[:, g:g + 1], PC[h][:, qq * K:(qq + 1) * K], ALU.mult, ALU.add)
                if j < 3:
                    st.do(ins)
            ins.then_inc(y_ev, 1)
            dve.wait_ge(y_ev, i * 2 + (hf + 2))
            st.sync()
            st.do(tt(ya[:, :, :], yv[:, :, :], yv[:, :, :], ALU.mult))
            st.sync()
            st.do(nc.vector.tensor_scalar(ya[:, :, :], ya[:, :, :], 0.044715, 1.0, ALU.mult, ALU.add))
            st.sync()
            tt(ya[:, :, :], ya[:, :, :], yv[:, :, :], ALU.mult).then_inc(gelu_in, 1)
            dve.wait_ge(sig_done, i * 2 + (hf + 1))
            tt(yv[:, :, :], yv[:, :, :], ya[:, :, :], ALU.mult).then_inc(y_full, 1)

        def act_mix(act):
            act.wait_ge(h_spilled, 48)
            act.sem_inc(m_out, 3)
            for b in range(NB):
                act.sem_inc(m_stored[b], 16)
            with act.Fori(0, 4) as i:
                def evac(q):
                    for b in range(NB):
                        act.wait_ge(m_scaled, i * 18 + (3 * q + b + 1 + 3))
                        fn = ACT.Sigmoid if q > 1 else ACT.Identity
                        if q == 1:
                            nc.scalar.activation(up[:, ds(i * T + b * BW, BW)], mt[b], fn, bias=bst[:, 1:2]).then_inc(m_out, 1)
                            continue
                        n = (0, None, 1, 2, 3, 4)[q]
                        act.wait_ge(m_stored[b], i * 80 + 16 * (n + 1))
                        nc.scalar.activation(og[b], mt[b], fn, bias=bst[:, q:q + 1]).then_inc(m_out, 1)
                    for b in range(NB):
                        if q == 1:
                            continue
                        act.wait_ge(m_out, i * 18 + (3 * q + b + 1 + 3))
                        if q == 0:
                            act.dma_start(u_dram[ds(i, 1), :, cols(b)].rearrange("o p t -> p (o t)"), og[b]).then_inc(m_stored[b], 16)
                        else:
                            act.dma_start(gate_dram[ds(i * 4 + q - 2, 1), :, cols(b)].rearrange("o p t -> p (o t)"),
                                          og[b]).then_inc(m_stored[b], 16)

                def gelu(hf):
                    act.wait_ge(gelu_in, i * 2 + (hf + 1))
                    nc.scalar.activation(ya[:, :, :], ya[:, :, :], ACT.Sigmoid, scale=2 * sqrt(2 / pi)).then_inc(sig_done, 1)
                for q in range(6):
                    if q < 4:
                        split_hi(act, mix_unit(i, q + 2))
                    evac(q)
                    if q in (3, 4):
                        split_hi(act, mix_unit(i, q + 3))
                    if q in (3, 5):
                        gelu(q // 2 - 1)

        def sp_mix(sp):
            sp.wait_ge(h_spilled, 48)
            sp.sem_inc(y_stored, 128)

            def store_y(i, hf):
                sp.wait_ge(y_full, i * 2 + (hf + 1))
                for t in range(L):
                    sp.dma_start(y_dram.rearrange("(g c) t k -> c g t k", c=GC)[:, ds(i * 8 + 4 * hf, 4), t, :],
                                 yv[GC * t:GC * t + GC, :, :]).then_inc(y_stored, 16)

            def side(i):
                for b in range(NB):
                    sp.wait_ge(m_stored[b], i * 80 + 32)
                sp.wait_ge(y_mm, i * 2 + 1)
                sp.wait_ge(y_ev, i * 2 + 1)
                for s in range(L):
                    sp.dma_start(ur[GC * s:GC * s + GC, :, :],
                                 u_dram.rearrange("j (g c) (s k) -> j s c g k", c=GC, s=L)[ds(i, 1), s]
                                 .rearrange("o c g k -> (o c) g k")).then_inc(ur_loaded, 16)
                sp.wait_ge(prep_ev, i * 3 + 3)
                sp.dma_start(taps_dram, taps[:, :]).then_inc(taps_stored, 16)
                sp.wait_ge(taps_stored, i * 16 + 16)
                for s in range(L):
                    sp.dma_start(toep[GC * s:GC * s + GC, :, :],
                                 taps_dram.rearrange("(g c) x -> c g x", c=GC)[:, :, P - GC * s:2 * P - GC * s]).then_inc(toep_loaded, 16)
            for q in range(3, 6):
                load_unit(sp, "mix", 0, q)
            with sp.Fori(0, 3) as j:
                load_unit(sp, "mix", Along(j, 3, 1, 1), 0)
                side(j)
                for q in range(1, 6):
                    load_unit(sp, "mix", Along(j, 3, 1, 1), q)
                    if q in (3, 4):
                        store_y(j, q - 3)
            side(3)
            load_unit(sp, "pool", 0, 0)
            store_y(3, 0)
            load_unit(sp, "glu", 0, 0)
            store_y(3, 1)

        def pool_windows(pool):
            pool.wait_ge(h_spilled, 48)
            st = Steps(pool, own["pool_prep"])
            tt, cp, ts = nc.gpsimd.tensor_tensor, nc.gpsimd.tensor_copy, nc.gpsimd.tensor_scalar
            for g in range(4):
                w = 2 << g
                pool.wait_ge(m_out, 18 * g + 6 + 3)
                if g == 0:
                    pool.wait_ge(own["dve_prep"], 2)
                u = up[:, g * T:(g + 1) * T].rearrange("p (s k) -> p s k", s=L)
                st.sync()
                st.do(nc.gpsimd.memset(ext[:, :, 0:2], 0.0))
                st.do(cp(ext[:, :, 2:2 + KP], u[:, :, 0:KP]))
                st.do(cp(ext[:, :, 2 + KP:4 + KP], hcol[:, g, :].rearrange("p (k s) -> p s k", s=L)))
                st.do(cp(ext[:, :, 4 + KP:4 + K], u[:, :, KP:K]))
                st.do(cp(tail[:, g, 0, :].rearrange("p (k s) -> p s k", s=L), u[:, :, KP - 2:KP]))
                st.do(cp(tail[:, g, 1, :].rearrange("p (k s) -> p s k", s=L), u[:, :, K - 2:K]))
                src, dst = ext, sum_a
                for level in range(g + 1):
                    d = 1 << level
                    st.sync()
                    if d < L:
                        st.do(tt(dst[:, d:L, :], src[:, d:L, :], src[:, 0:L - d, :], ALU.add))
                    st.do(tt(dst[:, 0:d, 1:], src[:, 0:d, 1:], src[:, L - d:L, 0:K + 3], ALU.add))
                    st.do(cp(dst[:, 0:d, 0:1], src[:, 0:d, 0:1]))
                    src, dst = dst, src
                st.sync()
                st.do(tt(src[:, :, 2:4], src[:, :, 2:4], cnt[:, g, :].rearrange("p (s k) -> p s k", s=L), ALU.mult))
                st.sync()
                st.do(ts(src[:, :, 2:4 + K], src[:, :, 2:4 + K], 1.0 / w, 1.0, ALU.mult, ALU.mult))
                st.sync()
                st.do(tt(u[:, :, 0:KP], src[:, :, 2:2 + KP], u[:, :, 0:KP], ALU.subtract))
                st.do(tt(u[:, :, KP:K], src[:, :, 4 + KP:4 + K], u[:, :, KP:K], ALU.subtract))
                st.sync()
                pool.sem_inc(pooled, 1)

        MIX_END = plan.block["pool"]

        def pe_after(pe):
            pe.wait_ge(tail_ready, 1)
            nc.tensor.transpose(PB[0][0:64, 0:P], hfin[:, :, :].rearrange("p a j -> p (a j)"), ident[:, :])
            for w in range(2):
                for g in range(4):
                    mm = nc.tensor.transpose(PB[1 + w][0:16, g * P:(g + 1) * P], tail[:, g, w, :], ident[:, :])
            mm.then_inc(last_mm, 1)
            pe.wait_ge(pl_ready, 4)
            u = plan.unit["pool"]
            pe.wait_ge(w_ready, u + 1)
            for m in range(DT):
                for b in range(NB):
                    n = NB * m + b
                    if n >= 2:
                        pe.wait_ge(gp_done, n - 1)
                    three(PC[n % 2][:, 0:BW], wslices(u % SPLIT_SLOTS, m * P, m * P + P),
                          (pl_hi[:, m // 2, cols(b)], pl_lo[:, m // 2, cols(b)]), True, True).then_inc(pe_block, 1)

        def dve_after(dve):
            dve.wait_ge(pooled, 4)
            dve.sem_inc(tail_ready, 1)
            for g in range(4):
                dve.wait_ge(pl_hi_done, g + 1)
                nc.vector.tensor_tensor(pl_lo[:, g, :], up[:, g * T:(g + 1) * T], pl_hi[:, g, :].bitcast(F32),
                                        ALU.subtract).then_inc(pl_ready, 1)
            for j in range(4):
                dve.wait_ge(y_hi_done, j + 1)
                y = y_lo[:, j]
                nc.vector.tensor_tensor(y, y.bitcast(F32), y_hi[:, j].bitcast(F32), ALU.subtract).then_inc(y_ready, 1)
            split_lo(dve, plan.unit["pool"] + 2)
            for m in range(DT):
                dve.wait_ge(gp_loaded[m % 2], 16 * (m // 2 + 1))
                if m >= 2:
                    dve.wait_ge(gp_stored[m % 2], 16 * (m // 2))
                for b in range(NB):
                    n = NB * m + b
                    dve.wait_ge(pe_block, MIX_END + n + 1)
                    nc.vector.scalar_tensor_tensor(gp_out[:, m % 2, cols(b)], PC[n % 2][:, 0:BW], vecs[:, V_PSC + m:V_PSC + m + 1],
                                                   gp_in[:, m % 2, cols(b)], ALU.mult, ALU.mult).then_inc(gp_done, 1)

        def act_after(act):
            act.wait_ge(pe_block, MIX_END)
            for g in range(4):
                act.wait_ge(pooled, g + 1)
                nc.scalar.activation(pl_hi[:, g, :], up[:, g * T:(g + 1) * T], ACT.Copy).then_inc(pl_hi_done, 1)
            for j in range(4):
                act.wait_ge(y_loaded[j], 16)
                nc.scalar.activation(y_hi[:, j], y_lo[:, j].bitcast(F32), ACT.Copy).then_inc(y_hi_done, 1)
            act.wait_ge(last_mm, 1)
            nc.scalar.activation(hfrow[:, :], PB[0][0:64, 0:P], ACT.Copy).then_inc(last_ev, 1)
            for w in range(2):
                nc.scalar.activation(prow[:, w, :], PB[1 + w][0:16, :], ACT.Copy).then_inc(last_ev, 1)
            split_hi(act, plan.unit["pool"] + 2)
            act.wait_ge(last_ev, 3)
            for n, out in enumerate((re_prompt, im_prompt, re_sample, im_sample)):
                act.dma_start(out.rearrange("(j g) s -> j (g s)", g=2), hfrow[16 * n:16 * n + 16, :]).then_inc(state_out, 16)
            for w, out in enumerate((pool_prompt, pool_sample)):
                act.dma_start(out, prow[1:16, w, :]).then_inc(state_out, 16)
            act.wait_ge(state_out, 96)

        def sp_after(sp):
            load_unit(sp, "glu", 0, 1)
            sp.wait_ge(pe_block, MIX_END)
            sp.wait_ge(y_stored, 128 * 9)
            for j in range(4):
                sp.dma_start(y_lo[:, j].bitcast(F32), y_dram[j * P:(j + 1) * P].rearrange("p t k -> p (t k)")).then_inc(y_loaded[j], 16)
            sp.wait_ge(tail_ready, 1)
            for b in range(NB):
                sp.wait_ge(m_stored[b], 16 * 21)
            for m in range(DT + 1):
                if m < DT:
                    if m >= 2:
                        sp.wait_ge(gp_done, NB * (m - 1))
                    sp.dma_start(gp_in[:, m % 2, :], gate_dram[DT + m]).then_inc(gp_loaded[m % 2], 16)
                if m:
                    sp.wait_ge(gp_done, NB * m)
                    sp.dma_start(prod_dram[m - 1], gp_out[:, (m - 1) % 2, :]).then_inc(gp_stored[(m - 1) % 2], 16)
            sp.wait_ge(pl_ready, 4)
            sp.wait_ge(last_mm, 1)
            sp.wait_ge(state_out, 96)
            for b in range(NB):
                sp.dma_start(xres[:, :, cols(b)], h_dram[:, :, cols(b)]).then_inc(h_back, 16)

        side_slot = [(std[:, :], rpost[:, :]), (rstd[:, 0:BW], rstd[:, BW:2 * BW])]

        def pool_side(pool):
            for i in range(2):
                pool.wait_ge(gp_stored[i], 64)
            for n in range(NB * DT):
                if n >= 2:
                    pool.wait_ge(h_mul[3], n - 1)
                m, b = divmod(n, NB)
                gs, pr = side_slot[n % 2]
                pool.dma_start(gs, gate_dram[m, :, cols(b)]).then_inc(side_loaded[n % 2], 16)
                pool.dma_start(pr, prod_dram[m, :, cols(b)]).then_inc(side_loaded[n % 2], 16)

        def pe_glu(pe, g):
            for q in range(2):
                u = plan.unit[("glu", g)] + q
                m = 2 * g + q
                pe.wait_ge(w_ready, u + 1)
                for b in range(NB):
                    pe.wait_ge(in_free[3], 3 * m + b + 1)
                    for h, out in ((0, PA), (1, PB)):
                        for k in range(4):
                            c0 = (2 * k + h) * P
                            mm = three(out[b][:, 0:BW], wslices(u % SPLIT_SLOTS, c0, c0 + P),
                                       (y_hi[:, k, cols(b)], y_lo[:, k, cols(b)]), k == 0, k == 3)
                    mm.then_inc(pe_block, 1)

        def pe_merge(pe):
            pe.wait_ge(y_ready, 4)
            pe.wait_ge(last_ev, 3)
            pe_glu(pe, 0)
            pe_glu(pe, 1)
            for g in range(2, MG):
                pe_out(pe, 3, g - 2)
                pe_glu(pe, g)
            pe_fin(pe, 3)

        def dve_glu(dve, g):
            stt, tt = nc.vector.scalar_tensor_tensor, nc.vector.tensor_tensor
            for q in range(2):
                m = 2 * g + q
                split_lo(dve, plan.unit[("glu", g)] + q + 2)
                for b in range(NB):
                    n = NB * m + b
                    s = n % 2
                    gs, pr = side_slot[s]
                    dve.wait_ge(sig_m, n + 1)
                    stt(ta[:, s, :], PA[b][:, 0:BW], vecs[:, V_BGLU + m:V_BGLU + m + 1], tb[:, s, :], ALU.add, ALU.mult).then_inc(in_free[3], 1)
                    dve.wait_ge(in_free[3], n + 1 + 3)
                    dve.wait_ge(side_loaded[s], 32 * (n // 2 + 1))
                    tt(ta[:, s, :], ta[:, s, :], gs, ALU.mult).then_inc(merge_a, 1)
                    dve.wait_ge(merge_a, n + 1)
                    tt(tb[:, s, :], ta[:, s, :], pr, ALU.add).then_inc(h_mul[3], 1)
                    dve.wait_ge(hid_hi_done[3], n + 1)
                    hs = m % 4
                    tt(hid_lo[:, hs, cols(b)], tb[:, s, :], hid_hi[:, hs, cols(b)].bitcast(F32), ALU.subtract).then_inc(hid_ready[3], 1)

        def act_glu(act, g):
            for q in range(2):
                m = 2 * g + q
                split_hi(act, plan.unit[("glu", g)] + q + 2)
                for b in range(NB):
                    n = NB * m + b
                    s = n % 2
                    act.wait_ge(pe_block, plan.block[("glu", g)] + 3 * q + b + 1)
                    if n >= 2:
                        act.wait_ge(hid_ready[3], n - 1)
                    nc.scalar.activation(tb[:, s, :], PB[b][:, 0:BW], ACT.Sigmoid,
                                         bias=vecs[:, V_BGLU + 8 + m:V_BGLU + 9 + m]).then_inc(sig_m, 1)
                    act.wait_ge(h_mul[3], n + 1)
                    if q == 0 and b == 0:
                        if g >= 2:
                            act.wait_ge(pe_block, plan.block[("merge", g - 2)] + 24)
                        else:
                            act.wait_ge(gp_stored[0], 64)
                            act.wait_ge(gp_stored[1], 64)
                    hs = m % 4
                    nc.scalar.activation(hid_hi[:, hs, cols(b)], tb[:, s, :], ACT.Copy).then_inc(hid_hi_done[3], 1)

        def dve_merge(dve, next_units):
            dve.wait_ge(acc_zero, 2)
            dve.sem_inc(in_free[3], 3)
            dve.sem_inc(out_free[3], 26)
            dve_glu(dve, 0)
            dve_glu(dve, 1)
            for g in range(2, MG):
                dve_outs(dve, 3, g - 2)
                dve_glu(dve, g)
            dve_last(dve, 3, next_units)

        def act_merge(act, next_units):
            act_glu(act, 0)
            act_glu(act, 1)
            for g in range(2, MG):
                act_outs(act, 3, g - 2)
                act_glu(act, g)
            act_last(act, 3, next_units)

        def sp_merge(sp):
            for q in range(2):
                load_unit(sp, "glu", 1, q)
            for g in range(2, MG):
                for q in range(2):
                    load_unit(sp, "merge", g - 2, q)
                for q in range(2):
                    load_unit(sp, "glu", g, q)
            for q in range(4):
                load_unit(sp, "fin", 3, q)

        TILES = list(range(9))
        dcol = ta.rearrange("p a b -> p (a b)")[:, 0:DT * DEC].rearrange("p (m t) -> p m t", m=DT)

        def dve_end(dve):
            dve.wait_ge(h_done, 72)
            nc.vector.tensor_copy(dcol.rearrange("p m (k s) -> p m k s", s=L),
                                  xres.rearrange("p m (s k) -> p m k s", s=L)[:, :, KP:K, :]).then_inc(dcol_done, 1)

        def pe_end(pe):
            F = 0
            for tile in TILES:
                b = 2 if tile == 8 else (tile * K + KP - 1) // BW
                pe.wait_ge(h_done, 48 + 8 * b + 8)
                if tile == 8:
                    pe.wait_ge(dcol_done, 1)
                for half in range(2):
                    if F >= 3:
                        pe.wait_ge(yrow_ready, F - 2)
                    rows = DEC if tile == 8 else P
                    for j in range(4):
                        m = 4 * half + j
                        src = xres[:, m, :]
                        if tile == 8:
                            src = dcol[:, m, :]
                        else:
                            src = src[:, tile * K:tile * K + KP]
                        mm = nc.tensor.transpose(PB[F % 3][0:rows, j * P:(j + 1) * P], src, ident[:, :])
                    mm.then_inc(y_turned, 1)
                    F += 1

        def act_end(act):
            F = 0
            for tile in TILES:
                rows = DEC if tile == 8 else P
                for half in range(2):
                    act.wait_ge(y_turned, F + 1)
                    if half == 0 and tile >= 4:
                        act.wait_ge(y_out[tile % 4], 16 * (tile // 4))
                    nc.scalar.activation(yrow[0:rows, tile % 4, 512 * half:512 * half + 512], PB[F % 3][0:rows, :],
                                         ACT.Copy).then_inc(yrow_ready, 1)
                    F += 1

        def sp_end(sp):
            yp = y_prompt.rearrange("(k s) d -> s k d", s=L)
            for tile in TILES:
                sp.wait_ge(yrow_ready, 2 * tile + 2)
                if tile == 8:
                    sp.dma_start(y_sample, yrow[0:DEC, 0, :]).then_inc(y_out[0], 16)
                else:
                    sp.dma_start(yp[tile], yrow[:, tile % 4, :]).then_inc(y_out[tile % 4], 16)
            for i, n in enumerate((3, 2, 2, 2)):
                sp.wait_ge(y_out[i], 16 * n)

        FIRST_MIX, FIRST_F2 = plan.unit[("mix", 0)], plan.unit[(2, "in", 0)]

        @block.sync
        def _(sp):
            sp_start(sp)
            sp_ffn(sp, 1, skip=3)
            for q in range(3):
                load_unit(sp, "mix", 0, q)
            for b in range(NB):
                sp.wait_ge(h_done, 8 * b + 8)
                sp.dma_start(h_dram[:, :, cols(b)], xres[:, :, cols(b)]).then_inc(h_spilled, 16)
                if b == 0:
                    sp_prep(sp)
            sp_mix(sp)
            sp_after(sp)
            sp_merge(sp)
            sp_ffn(sp, 2)
            sp_end(sp)

        @block.gpsimd
        def _(pool):
            nc.gpsimd.memset(ident[:, :], 0.0).then_inc(const_ready, 1)
            nc.gpsimd.memset(ones[:, :], 1.0).then_inc(const_ready, 1)
            nc.gpsimd.memset(epsc[:, :], EPS).then_inc(const_ready, 1)
            pool.wait_ge(const_ready, 3)
            nc.gpsimd.affine_select(out=ident[:, :], in_=ident[:, :], compare_op=ALU.not_equal, fill=1.0, base=0,
                                    pattern=[[-1, P]], channel_multiplier=1).then_inc(const_ready, 2)
            pool.wait_ge(x_turned, 18)
            nc.gpsimd.memset(acc[:, :, :], 0.0).then_inc(acc_zero, 1)
            for b in range(NB):
                add_squares(pool, job(0, "x", b))
            pool_stage(pool, 1)
            pool_windows(pool)
            pool.wait_ge(pl_ready, 4)
            pool.wait_ge(last_mm, 1)
            pool.wait_ge(state_out, 96)
            nc.gpsimd.memset(acc[:, :, :], 0.0).then_inc(acc_zero, 1)
            pool_side(pool)
            pool_stage(pool, 2)
            pool.wait_ge(h_done, 48)
            nc.gpsimd.memset(acc[:, :, :], 0.0).then_inc(acc_zero, 1)
            pool_stage(pool, 3)

        @block.scalar
        def _(act):
            split_hi(act, 0)
            split_hi(act, 1)
            act.wait_ge(const_ready, 5)
            empty_x(act, lambda d, s: nc.scalar.activation(d, s, ACT.Copy), 1, x_act)
            act.wait_ge(x_dve, 9)
            act.wait_ge(vec_ready, 1)
            act.wait_ge(x_act, 9)
            for b in range(NB):
                for m in range(DT):
                    z_hi_part(act, 0, b, m, V_PRE1)
                    square(act, job(0, "x", b), m, xres[:, m, cols(b)])
            act_ffn(act, 1, [FIRST_MIX, FIRST_MIX + 1])
            act_prep(act)
            act_mix(act)
            act_after(act)
            act_merge(act, [FIRST_F2, FIRST_F2 + 1])
            act_ffn(act, 2, [])
            act_end(act)

        @block.vector
        def _(dve):
            dve.wait_ge(vec_mm, 1)
            nc.vector.tensor_copy(vecs[:, :], PC[0][:, 0:P]).then_inc(vec_ready, 1)
            empty_x(dve, nc.vector.tensor_copy, 0, x_dve)
            split_lo(dve, 0)
            split_lo(dve, 1)
            dve.wait_ge(vec_ready, 1)
            dve.wait_ge(x_dve, 9)
            dve.wait_ge(x_act, 9)
            dve.sem_inc(in_free[1], 3)
            for b in range(NB):
                for m in range(DT):
                    z_lo_part(dve, 0, b, m, V_PRE1)
            before = lambda st: (lambda b: recip_row(dve, st, b))

            def recip_row(dve, st, b):
                recip(dve, job(st, "h", b), rstd[:, cols(b)])
                dve.wait_ge(recip_done, job(st, "h", b) + 1)
            dve_ffn(dve, 1, before(0), [FIRST_MIX, FIRST_MIX + 1])
            steps = dve_prep_a(dve)
            for b in range(NB):
                recip_row(dve, 1, b)
            dve_prep_b(dve, steps)
            dve_mix(dve)
            dve_after(dve)
            dve_merge(dve, [FIRST_F2, FIRST_F2 + 1])
            dve_ffn(dve, 2, before(2), [])
            dve_end(dve)

        @block.tensor
        def _(pe):
            pe_start(pe)
            pe_ffn(pe, 1)
            stat_fin(pe, 1)
            pe.sem_inc(y_mm, 1)
            pe_prep(pe)
            pe_mix(pe)
            pe_after(pe)
            pe_merge(pe)
            pe_ffn(pe, 2)
            pe_end(pe)


_INS = ["x_prompt", "x_sample", "state_ssm_re", "state_ssm_im", "cache_pool", "ffn1_pre_g", "ffn1_w_in", "ffn1_w_out",
        "ffn1_post_g", "mix_pre_g", "w_in", "b_in", "ssm_lambda_re", "ssm_lambda_im", "ssm_log_step", "ssm_b_re", "ssm_b_im",
        "ssm_c_re", "ssm_c_im", "ssm_d", "ssm_w_glu", "ssm_b_glu", "pool_w", "pool_scale", "w_out", "mix_post_g",
        "ffn2_pre_g", "ffn2_w_in", "ffn2_w_out", "ffn2_post_g"]
_OUTS = [((1, SEQ, D), (SEQ, D)), ((1, DEC, D), (DEC, D)), ((1, 1, G, NS), (G, NS)), ((1, 1, G, NS), (G, NS)),
         ((1, 1, HIST, DS), (HIST, DS)), ((1, 1, G, NS), (G, NS)), ((1, 1, G, NS), (G, NS)), ((1, 1, HIST, DS), (HIST, DS))]


def constants():
    counts = np.ones((P, 4, L, 2), np.float32)
    for g in range(4):
        w = 2 << g
        for t in range(w - 1):
            counts[:, g, t % L, t // L] = w / (t + 1)
    mask = np.ones((P, K), np.float32)
    mask[:, [0, KP]] = 0.0
    return {"window_counts": counts.reshape(P, 4, 2 * L), "scan_mask": mask}


def kernel(**inputs):
    import concourse.bacc as bacc
    from concourse.bass_utils import run_bass_kernel_spmd

    nc = bacc.Bacc("TRN2", target_bir_lowering=False, num_devices=1, dynamic_dma_scratch_size=1024)
    arrays, args = {}, {}
    for name in _INS:
        x = np.ascontiguousarray(inputs[name])
        x = x[0] if x.shape[0] == 1 else x
        if name in ("state_ssm_re", "state_ssm_im", "cache_pool"):
            x = x[0]
        arrays[name] = np.ascontiguousarray(x)
    arrays.update(constants())
    for name, x in arrays.items():
        args[name] = nc.dram_tensor(name, x.shape, mybir.dt.from_np(x.dtype), kind="ExternalInput").ap()
    outs = [nc.dram_tensor(f"out_{n}", flat, F32, kind="ExternalOutput").ap() for n, (_, flat) in enumerate(_OUTS)]
    layer(nc, args, outs)
    r = run_bass_kernel_spmd(nc, [arrays], core_ids=[0])
    return tuple(r.results[0][f"out_{n}"].reshape(shape) for n, (shape, _) in enumerate(_OUTS))
```

```python
from contextlib import ExitStack
from itertools import islice
from math import pi, sqrt

import numpy as np

import concourse.bass as bass
from concourse import mybir

F32 = mybir.dt.float32
F32R = mybir.dt.float32r
I32 = mybir.dt.int32
ACT = mybir.ActivationFunctionType
ALU = mybir.AluOpType
ds = bass.ds

P = 128
D = 1024
DT = D // P
DFF = 2816
HT = DFF // P
SEQ, DEC = 1024, 32
L = 8
KP, KS = SEQ // L, DEC // L
K = KP + KS
T = L * K
NB = 3
BW = T // NB
G, GC, NS = 32, 16, 64
NPAIR = G // 2
DS = 512
HIST = 15
EPS = 1e-6
RAW_SLOTS, SPLIT_SLOTS = 3, 3
WU = D

V_PRE1, V_POST1, V_PREM, V_POSTM, V_PRE2, V_POST2, V_PSC, V_BIN, V_BGLU, V_D = 0, 8, 16, 24, 32, 40, 48, 56, 80, 96


class Along:

    def __init__(self, i, n, a, b):
        self.i, self.n, self.a, self.b = i, n, a, b

    def __add__(self, k):
        return Along(self.i, self.n, self.a, self.b + k)


def of(f, x):
    if not isinstance(x, Along):
        return f(x)
    v = [f(x.a * k + x.b) for k in range(x.n)]
    step = v[1] - v[0]
    assert all(q - p == step for p, q in zip(v, v[1:])), v
    return v[0] if step == 0 else x.i * step + v[0]


class Plan:

    def __init__(self):
        self.unit, self.block, self.last = {}, {}, []
        self.n = 0

    def add(self, key, units, blocks_of_unit, together=False):
        self.unit[key], self.block[key] = len(self.last), self.n
        for _ in range(units):
            self.n += 0 if together else blocks_of_unit
            self.last.append(self.n)
        if together:
            self.n += blocks_of_unit
            for u in range(units):
                self.last[-1 - u] = self.n


def groups(n):
    order = [("in", 0), ("in", 1)]
    for g in range(2, n):
        order += [("out", g - 2), ("in", g)]
    return order + [("fin", n - 2)]


FG = HT // 2
MG = DT // 2
PRE, MQ = 3, 5
PASS = MQ * NB
plan = Plan()
for f in (1, 2):
    if f == 2:
        plan.add("pre", PRE, NB)
        plan.last[-PRE:] = [plan.n - PRE + 1 + u for u in range(PRE)]
        for t in range(4):
            plan.add(("mix", t), MQ, NB)
            plan.last.append(plan.n)
        plan.add("post", 1, NB)
        for what, g in groups(MG):
            if what == "fin":
                plan.add(("fin", 3), 4, NB * DT, True)
            else:
                plan.add(("glu" if what == "in" else "merge", g), 2, *((NB,) if what == "in" else (NB * DT, True)))
            if (what, g) == ("in", 0):
                plan.add("pool", 1, 0)
    for what, g in groups(FG):
        if what == "fin":
            plan.add(("fin", f), 4, NB * DT, True)
            continue
        plan.add((f, what, g), *((4, NB) if what == "in" else (2, NB * DT, True)))
        if (what, g) == ("in", 0):
            first = plan.block[(f, "in", 0)]
            plan.last[-4:-2] = first + 2 * NB - 1, first + 2 * NB
UNITS = len(plan.last)


def layer(nc, a, outs):
    (y_prompt, y_sample, re_prompt, im_prompt, pool_prompt, re_sample, im_sample, pool_sample) = outs
    ctx = ExitStack()
    with ctx:
        def sb(name, shape, dt=F32, on=ctx):
            return on.enter_context(nc.sbuf_tensor(name, shape, dt))

        def sem(name):
            return ctx.enter_context(nc.semaphore(name))

        def scratch(name, shape):
            return nc.dram_tensor(name, shape, F32, kind="Internal").ap()

        h_dram = scratch("h_dram", (P, DT, T))
        u_dram = scratch("u_dram", (4, P, T))
        gate_dram = scratch("gate_dram", (2 * DT, P, T))
        taps_dram = scratch("taps_dram", (P, 2 * P))
        y_dram = scratch("y_dram", (DS, L, K))

        w_raw = sb("w_raw", [P, RAW_SLOTS, WU])
        w_hi = sb("w_hi", [P, SPLIT_SLOTS, WU], F32R)
        w_lo = sb("w_lo", [P, SPLIT_SLOTS, WU], F32R)
        rstd = sb("rstd", [P, T])
        ident = sb("ident", [P, P])
        ones = sb("ones", [P, P])
        vecs = sb("vecs", [P, P])
        ta = sb("ta", [P, 2, BW])
        tb = sb("tb", [P, 2, BW])
        std = sb("std", [P, BW])
        rpost = sb("rpost", [P, BW])
        sq = sb("sq", [P, 2, BW])
        ssum = sb("ssum", [P, 2, BW])
        epsc = sb("epsc", [P, 1])

        with ExitStack() as s:
            yrow = sb("yrow", [P, 4, D], F32, s)
        z_hi = sb("z_hi", [P, DT, T], F32R)
        z_lo = sb("z_lo", [P, DT, T], F32R)
        y_hi, y_lo, pl_hi, pl_lo = z_hi[:, 0:4], z_lo[:, 0:4], z_hi[:, 4:8], z_lo[:, 4:8]

        with ExitStack() as s:
            hid_hi = sb("hid_hi", [P, 4, T], F32R, s)
            hid_lo = sb("hid_lo", [P, 4, T], F32R, s)
            acc = sb("acc", [P, DT, T], F32, s)
            xres = sb("xres", [P, DT, T], F32, s)
        with ExitStack() as s:
            xrow = sb("xrow", [P, 9, D], F32, s)
            vrow = sb("vrow", [P, P], F32, s)
        with ExitStack() as s:
            sb("below", [P, (2 * 4 + DT + DT - 2) * T], F32, s)
            wp_hi = sb("wp_hi", [P, WU], F32R, s)
            wp_lo = sb("wp_lo", [P, WU], F32R, s)
        with ExitStack() as s:
            srow = sb("srow", [P, P], F32, s)
            crow = sb("crow", [P, 2, 4, 2, NS], F32, s)
            lsrow = sb("lsrow", [P, 2], F32, s)
            sp_ = sb("sp_", [P, 80], F32, s)
            sm = sb("sm", [P, 34, NPAIR], F32, s)
            smi = sb("smi", [P, NPAIR], I32, s)
            apw = sb("apw", [P, 2, NPAIR, 9], F32, s)
            arev = sb("arev", [P, 2, NPAIR, 8], F32, s)
            braw = sb("braw", [P, 2, NPAIR, GC], F32, s)
            bb = sb("bb", [P, 2, NPAIR, GC], F32, s)
            cc = sb("cc", [P, 2, NPAIR, GC], F32, s)
            wlo = sb("wlo", [P, 2, NPAIR, 16], F32, s)
            whi = sb("whi", [P, 2, NPAIR, 8], F32, s)
            ctmp = sb("ctmp", [P, 2, NPAIR * GC], F32, s)
            hfin = sb("hfin", [P, 4, NPAIR], F32, s)
            hfrow = sb("hfrow", [64, P], F32, s)
            mask = sb("mask", [P, K], F32, s)
            hrow = sb("hrow", [16, DS], F32, s)
            hcol = sb("hcol", [P, 4, 16], F32, s)
            cnt = sb("cnt", [P, 4, 16], F32, s)
            pt = sb("pt", [P, 2, 4, L, GC], F32, s)
            qt = sb("qt", [P, 2, 4, L + 1, GC], F32, s)
            mtmp = sb("mtmp", [P, 2, 4, (L + 1) * GC], F32, s)
            bbst = sb("bbst", [P, 2, 4, 2, GC], F32, s)
            bint = sb("bint", [P, 2, 4, P], F32, s)
            taps = sb("taps", [P, 2 * P], F32, s)
            toep = sb("toep", [P, 8, P], F32, s)
            ur = sb("ur", [P, 8, K], F32, s)
            wt = sb("wt", [P, 2, 4, K], F32, s)
            dec = sb("dec", [P, 4, K], F32, s)
            dst_ = sb("dst_", [P, 8], F32, s)
            bst = sb("bst", [P, 6], F32, s)
            r1 = sb("r1", [P, 2, K], F32, s)
            r2 = sb("r2", [P, 2, K], F32, s)
            r3 = sb("r3", [P, 2, K], F32, s)
            r4 = sb("r4", [P, 2, K], F32, s)
            vr = sb("vr", [P, 2, K], F32, s)
            vi = sb("vi", [P, 2, K], F32, s)
            hb = sb("hb", [P, 2, 2, K + 1], F32, s)
            yv = sb("yv", [P, 2, 4, K], F32, s)
            ya = sb("ya", [P, 4, K], F32, s)
            up = sb("up", [P, 4 * T], F32, s)
            ext = sb("ext", [P, L, K + 4], F32, s)
            sum_a = sb("sum_a", [P, L, K + 4], F32, s)
            tail = sb("tail", [P, 4, 2, 16], F32, s)
        mt = [ta[:, 0, :], ta[:, 1, :], tb[:, 0, :]]
        og = [tb[:, 1, :], std[:, :], rpost[:, :]]
        prow = mtmp[0:16].rearrange("p a b c -> p (a b c)")[:, 0:2 * DS].rearrange("p (w d) -> p w d", w=2)

        bank = [ctx.enter_context(nc.psum_tensor(f"bank{i}", [P, 512], F32)) for i in range(8)]
        PA, PB, PC = bank[0:3], bank[3:6], bank[6:8]

        w_loaded = [sem(f"w_loaded{i}") for i in range(RAW_SLOTS)]
        glu_value_loaded = sem("glu_value_loaded")
        w_hi_done, w_ready, pe_block = sem("w_hi_done"), sem("w_ready"), sem("pe_block")
        const_ready, vec_loaded = sem("const_ready"), sem("vec_loaded")
        vec_mm, vec_ready = sem("vec_mm"), sem("vec_ready")
        x_loaded = [sem(f"x_loaded{i}") for i in range(9)]
        x_turned, x_dve, x_act = sem("x_turned"), sem("x_dve"), sem("x_act")
        sq_done, sum_done, stat_done, std_done, recip_done = (sem(n) for n in ("sq_done", "sum_done", "stat_done", "std_done", "recip_done"))
        zhi_done, z_ready, h_done, t_done = sem("zhi_done"), sem("z_ready"), sem("h_done"), sem("t_done")
        acc_zero = sem("acc_zero")
        in_free, ta_done, silu_done, h_mul, hid_hi_done, hid_ready, out_free = (
            {f: sem(f"{n}{f}") for f in (1, 2, 3)} for n in ("in_free", "ta_done", "silu_done", "h_mul", "hid_hi_done", "hid_ready", "out_free"))
        h_spilled, h_back, h_back_last = sem("h_spilled"), sem("h_back"), sem("h_back_last")
        own = {n: sem(f"{n}_step") for n in ("dve_prep", "dve_mix", "pool_prep", "pool_turns")}
        pre_scaled, pre_gate, pre_stored = sem("pre_scaled"), sem("pre_gate"), [sem(f"pre_stored{n}") for n in range(3)]
        row_loaded = sem("row_loaded")
        sp_loaded, sp_mm = sem("sp_loaded"), sem("sp_mm")
        turns_ready = sem("turns_ready")
        prep_act, prep_dve = sem("prep_act"), sem("prep_dve")
        m_scaled, m_out = sem("m_scaled"), sem("m_out")
        m_stored = [sem(f"m_stored{b}") for b in range(NB)]
        pq_ready, prep_mm, prep_ev = sem("pq_ready"), sem("prep_mm"), sem("prep_ev")
        taps_stored, toep_loaded, ur_loaded = sem("taps_stored"), sem("toep_loaded"), sem("ur_loaded")
        e_mm, e_read, hb_ready, y_mm, y_ev, gelu_in, sig_done, y_full, y_stored = (
            sem(n) for n in ("e_mm", "e_read", "hb_ready", "y_mm", "y_ev", "gelu_in", "sig_done", "y_full", "y_stored"))
        y_loaded = [sem(f"y_loaded{j}") for j in range(4)]
        y_hi_done, y_ready, pooled, pl_hi_done, pl_ready = sem("y_hi_done"), sem("y_ready"), sem("pooled"), sem("pl_hi_done"), sem("pl_ready")
        tail_ready, last_mm, last_ev = sem("tail_ready"), sem("last_mm"), sem("last_ev")
        gp_mm, gp_done = sem("gp_mm"), sem("gp_done")
        side_loaded = [sem(f"side_loaded{i}") for i in range(2)]
        sig_m, merge_a = sem("sig_m"), sem("merge_a")
        dcol_done, y_turned, yrow_ready = sem("dcol_done"), sem("y_turned"), sem("yrow_ready")
        y_out = [sem(f"y_out{i}") for i in range(4)]
        state_out = sem("state_out")

        block = ctx.enter_context(nc.Block())
        cols = lambda b: slice(b * BW, (b + 1) * BW)

        def fin_group(ph):
            return (MG if ph == 3 else FG) - 2

        def unit_source(key, g, q):
            if isinstance(key, tuple) and key[0] in (1, 2):
                f, what = key
                if what == "in":
                    c = of(lambda x: (2 * x + q // 2) * P + (q % 2) * DFF, g)
                    return a[f"ffn{f}_w_in"].rearrange("(k p) n -> p k n", p=P)[:, :, ds(c, P)], "k"
                return a[f"ffn{f}_w_out"][ds(of(lambda x: (2 * x + q) * P, g), P), :], None
            if key == "fin":
                t = 2 * (fin_group(g)) + q
                return (a["w_out"] if g == 3 else a[f"ffn{g}_w_out"])[t * P:(t + 1) * P, :], None
            if key in ("mix", "pre", "post"):
                c = {"pre": (8 + q) * P, "post": (8 + 2 * DT - 1) * P}.get(key) or of(
                    lambda x: (x * P, 4 * P + x * P)[q] if q < 2 else (8 + PRE + 3 * x + q - 2) * P, g)
                return a["w_in"].rearrange("(k p) n -> p k n", p=P)[:, :, ds(c, P)], "k"
            if key == "pool":
                return a["pool_w"].rearrange("g c o -> c g o"), "g"
            if key == "glu":
                c = (2 * g + q) * P
                return a["ssm_w_glu"].rearrange("(k p) (h n) -> p k h n", p=P, h=2)[:, :, :, c:c + P], "kh"
            return a["w_out"][(2 * g + q) * P:(2 * g + q + 1) * P, :], None

        def load_unit(sp, key, g, q):
            name = key if isinstance(key, tuple) else (key,)
            u_of = lambda x: plan.unit[key if key in ("pool", "pre", "post") else (*name, x)] + q
            slot = of(lambda x: u_of(x) % RAW_SLOTS, g)
            if isinstance(g, Along) or u_of(g) >= RAW_SLOTS:
                sp.wait_ge(w_ready, of(lambda x: u_of(x) - RAW_SLOTS + 1, g))
            if key == "mix" and q == MQ:
                sp.sem_inc(w_loaded[slot], 16)
                return
            src, form = unit_source(key, g, q)
            dst = w_raw[:, slot, :]
            if form == "k":
                dst = dst.rearrange("p (k n) -> p k n", k=DT)
            elif form == "g":
                dst = dst.rearrange("p (g o) -> p g o", g=4)
            elif form == "kh":
                dst = dst.rearrange("p (k h n) -> p k h n", k=4, h=2)
                sp.dma_start(dst[:, :, 0, :], src[:, :, 0, :]).then_inc(glu_value_loaded, 16)
                sp.wait_ge(glu_value_loaded, 16 * (2 * g + q + 1))
                sp.dma_start(dst[:, :, 1, :], src[:, :, 1, :]).then_inc(w_loaded[slot], 16)
                return
            sp.dma_start(dst, src).then_inc(w_loaded[slot], 16)

        def loaded_value(u):
            return 16 * (u // RAW_SLOTS + 1)

        IN_Z = {plan.unit[("fin", ph)] + k: (plan.block[("fin", ph)], 2 * BW + P * (k - 2)) for ph in (1, 2, 3) for k in (2, 3)}

        MIX_END = plan.block[("glu", 0)]

        def split_place(u):
            raw = w_raw[:, of(lambda x: x % RAW_SLOTS, u), :]
            if not isinstance(u, Along) and u in IN_Z:
                free, c = IN_Z[u]
                return z_hi[:, :, c:c + P], z_lo[:, :, c:c + P], raw.rearrange("p (m n) -> p m n", m=DT), free
            if not isinstance(u, Along) and u == plan.unit["pool"]:
                return wp_hi[:, :], wp_lo[:, :], raw, MIX_END
            slot = of(lambda x: x % SPLIT_SLOTS, u)
            free = of(lambda x: plan.last[x - SPLIT_SLOTS], u) if isinstance(u, Along) or u >= SPLIT_SLOTS else 0
            return w_hi[:, slot, :], w_lo[:, slot, :], raw, free

        def split_hi(act, u):
            hi, _, raw, free = split_place(u)
            act.wait_ge(w_loaded[of(lambda x: x % RAW_SLOTS, u)], of(loaded_value, u))
            if isinstance(u, Along) or u >= SPLIT_SLOTS:
                act.wait_ge(pe_block, free)
            nc.scalar.activation(hi, raw, ACT.Copy).then_inc(w_hi_done, 1)

        def split_lo(dve, u):
            hi, lo, raw, _ = split_place(u)
            dve.wait_ge(w_hi_done, of(lambda x: x + 1, u))
            nc.vector.tensor_tensor(lo, raw, hi.bitcast(F32), ALU.subtract).then_inc(w_ready, 1)

        def three(out, lhs, rhs, first, last):
            (lh, ll), (rh, rl) = lhs, rhs
            nc.tensor.matmul(out, lh, rh, start=first, stop=False)
            nc.tensor.matmul(out, lh, rl, start=False, stop=False)
            return nc.tensor.matmul(out, ll, rh, start=False, stop=last)

        def wslices(slot, lo, hi):
            return w_hi[:, slot, lo:hi], w_lo[:, slot, lo:hi]

        def job(stage, kind, b):
            return {0: 0, 1: 3, 2: 9, 3: 15}[stage] + (3 if kind == "h" and stage else 0) + b

        def square(act, J, m, src):
            need = {0: 7 * (J - 1) + 6, 1: 7 * (J - 1) + 7, 2: 7 * J + 1}.get(m, 7 * J + m - 2)
            if need > 0:
                act.wait_ge(sum_done, need)
            nc.scalar.activation(sq[:, m % 2, :], src, ACT.Square).then_inc(sq_done, 1)

        def add_squares(pool, J):
            for m in range(1, DT):
                pool.wait_ge(sq_done, DT * J + m + 1)
                if m == 1 and J >= 2:
                    pool.wait_ge(stat_done, J - 1)
                if m > 1:
                    pool.wait_ge(sum_done, 7 * J + m - 1)
                nc.gpsimd.tensor_tensor(ssum[:, J % 2, :], sq[:, 0, :] if m == 1 else ssum[:, J % 2, :],
                                        sq[:, m % 2, :], ALU.add).then_inc(sum_done, 1)

        def stat(pe, J, out, free=None):
            pe.wait_ge(sum_done, 7 * J + 7)
            if free is not None:
                pe.wait_ge(*free)
            nc.tensor.matmul(out[:, 0:BW], ones[:, :], ssum[:, J % 2, :], start=True, stop=True).then_inc(stat_done, 1)

        def root(act, J, src):
            act.wait_ge(stat_done, J + 1)
            if J:
                act.wait_ge(recip_done, J)
            nc.scalar.activation(std[:, :], src[:, 0:BW], ACT.Sqrt, bias=epsc[:, 0:1], scale=1.0 / D).then_inc(std_done, 1)

        def recip(dve, J, dst):
            dve.wait_ge(std_done, J + 1)
            nc.vector.reciprocal(dst, std[:, :]).then_inc(recip_done, 1)

        def recip_row(dve, stage, b):
            recip(dve, job(stage, "h", b), rstd[:, cols(b)])
            dve.wait_ge(recip_done, job(stage, "h", b) + 1)

        STAT_H = [PC[0], PC[1], PC[0]]

        def z_hi_part(act, stage, b, m, gain):
            if stage:
                act.wait_ge(h_done, 24 * (stage - 1) + 8 * b + m + 1)
            nc.scalar.activation(z_hi[:, m, cols(b)], xres[:, m, cols(b)], ACT.Copy,
                                 scale=vecs[:, gain + m:gain + m + 1]).then_inc(zhi_done, 1)

        def z_lo_part(dve, stage, b, m, gain):
            dve.wait_ge(zhi_done, 24 * stage + 8 * b + m + 1)
            nc.vector.scalar_tensor_tensor(z_lo[:, m, cols(b)], xres[:, m, cols(b)], vecs[:, gain + m:gain + m + 1],
                                           z_hi[:, m, cols(b)].bitcast(F32), ALU.mult, ALU.subtract).then_inc(z_ready, 1)

        GAIN = {0: V_PRE1, 1: V_PREM, 2: V_PRE2}
        POST = {1: V_POST1, 2: V_POSTM, 3: V_POST2}
        def residual(dve, stage, b):
            for m in range(DT + 2):
                if m < DT:
                    yield b, "t", m
                if 1 <= m <= DT:
                    yield b, "h", m - 1
                if m >= 2 and stage < 3:
                    yield b, "z", m - 2

        def residual_step(dve, stage, b, what, m):
            done = {1: 0, 2: 24, 3: 48}[stage] + 8 * b + m
            slot = m % 2
            if what == "z":
                z_lo_part(dve, stage, b, m, GAIN[stage])
            elif what == "t":
                if done >= 2:
                    dve.wait_ge(h_done, done - 1)
                g = POST[stage] + m
                nc.vector.scalar_tensor_tensor(ta[:, slot, :], acc[:, m, cols(b)], vecs[:, g:g + 1], rpost[:, :],
                                               ALU.mult, ALU.mult).then_inc(t_done, 1)
            else:
                dve.wait_ge(t_done, done + 1)
                if stage == 2 and m == 0:
                    dve.wait_ge(h_back, 16 * (b + 1))
                if stage == 2 and m == DT - 2 and b == 0:
                    dve.wait_ge(h_back_last, 16)
                nc.vector.scalar_tensor_tensor(xres[:, m, cols(b)], ta[:, slot, :], 0.5 if stage != 2 else 1.0,
                                               xres[:, m, cols(b)], ALU.mult, ALU.add).then_inc(h_done, 1)

        def out_key(ph, g):
            return (ph, "out", g) if ph != 3 else ("merge", g)

        def in_key(ph, g):
            return (ph, "in", g) if ph != 3 else ("glu", g)

        AROUND = [PC[0], PC[1], PA[0], PB[0], PA[1], PB[1], PA[2], PB[2]]

        def out_bank(n):
            index = lambda k: k % 8 if k < 16 else k % 2
            before = [k for k in range(n) if index(k) == index(n)]
            return AROUND[index(n)], before[-1] if before else None

        def pe_out(pe, ph, g):
            u = of(lambda x: plan.unit[out_key(ph, x)], g)
            s0 = of(lambda x: plan.unit[out_key(ph, x)] % SPLIT_SLOTS, g)
            hs = of(lambda x: 2 * (x % 2), g)
            pe.wait_ge(w_ready, u + 2)
            if ph == 3:
                pe.wait_ge(gp_done, 6 * (g + 2))
            for b in range(NB):
                pe.wait_ge(hid_ready[ph], of(lambda x: 6 * x + 3 + b + 1, g))
                for m in range(DT):
                    n = 8 * b + m
                    out, before = out_bank(n)
                    out = out[:, 0:BW]
                    if before is not None:
                        pe.wait_ge(out_free[ph], of(lambda x: 24 * x + before + 27, g))
                    elif n < 2:
                        pe.wait_ge(out_free[ph], of(lambda x: 24 * x + n + 25, g))
                    else:
                        pe.wait_ge(in_free[ph], of(lambda x: 3 * (2 * min(x + 1, last_group(ph)) + 1) + (n - 2) // 2 + 4, g))
                    for k in range(2):
                        mm = three(out, wslices((s0 + k) % SPLIT_SLOTS, m * P, m * P + P),
                                   (hid_hi[:, hs + k, cols(b)], hid_lo[:, hs + k, cols(b)]), k == 0, k == 1)
                    mm.then_inc(pe_block, 1)

        def dve_out(dve, ph, g, b, m, bank=None):
            dve.wait_ge(pe_block, of(lambda x: plan.block[out_key(ph, x) if bank is None else ("fin", ph)] + 8 * b + m + 1, g))
            dst = acc[:, m, cols(b)]
            dve.wait_ge(out_free[ph], of(lambda x: 24 * x + 8 * b + m + 3, g))
            nc.vector.tensor_tensor(dst, dst, (bank or out_bank(8 * b + m)[0])[:, 0:BW], ALU.add).then_inc(out_free[ph], 1)

        def last_group(ph):
            return (FG if ph != 3 else MG) - 1

        def stage_of(ph):
            return {1: 1, 3: 2, 2: 3}[ph]

        FIN_ROUND, FIN_BEFORE = [PB[0], PB[1], PB[2], PC[0]], [3, 5, 7, 0]
        STAT_ACC = [PA[0], PA[1], PC[1]]

        def fin_bank(n):
            return AROUND[n] if n < DT else FIN_ROUND[(n - DT) % 4]

        def pe_fin(pe, ph):
            g, st = fin_group(ph), stage_of(ph)
            u0 = plan.unit[("fin", ph)]

            def lhs(k, m):
                if u0 + k in IN_Z:
                    c = IN_Z[u0 + k][1]
                    return z_hi[:, m, c:c + P], z_lo[:, m, c:c + P]
                return wslices((u0 + k) % SPLIT_SLOTS, m * P, m * P + P)

            def part(b, m, ks):
                for k in ks:
                    h = (2 * g + k) % 4
                    mm = three(fin_bank(8 * b + m)[:, 0:BW], lhs(k, m), (hid_hi[:, h, cols(b)], hid_lo[:, h, cols(b)]),
                               k == 0, k == 3)
                return mm
            pe.wait_ge(w_ready, u0 + 2)
            pe.wait_ge(hid_ready[ph], 6 * (g + 1) + 3 + 1)
            if ph == 3:
                pe.wait_ge(gp_done, NB * DT)
            for m in range(DT):
                if m < 2:
                    pe.wait_ge(out_free[ph], 24 * g + m + 25)
                else:
                    pe.wait_ge(in_free[ph], 3 * (2 * (g + 1) + 1) + (m - 2) // 2 + 4)
                part(0, m, (0, 1))
            pe.wait_ge(w_ready, u0 + 4)
            for m in range(DT):
                part(0, m, (2, 3)).then_inc(pe_block, 1)
            for b in (1, 2):
                pe.wait_ge(hid_ready[ph], 6 * (g + 1) + 3 + b + 1)
                for m in range(DT):
                    r = 8 * (b - 1) + m
                    before = FIN_BEFORE[r] if r < 4 else 8 + r - 4
                    pe.wait_ge(out_free[ph], 24 * g + 26 + before + 1)
                    part(b, m, range(4)).then_inc(pe_block, 1)
                    if m == 2:
                        stat(pe, job(st, "acc", b - 1), STAT_ACC[b - 1])

        def stat_fin(pe, ph):
            stat(pe, job(stage_of(ph), "acc", 2), STAT_ACC[2], (out_free[ph], 24 * fin_group(ph) + 26 + 24))

        def dve_last(dve, ph, next_units):
            st, g = stage_of(ph), fin_group(ph)
            last = plan.unit[("fin", ph)] + 2
            split_lo(dve, last)
            split_lo(dve, last + 1)

            def take(steps, n):
                for b, what, m in islice(steps, n):
                    residual_step(dve, st, b, what, m)
            per = 3 if st < 3 else 2
            steps = iter(())
            for b in range(NB):
                for m in range(DT):
                    dve_out(dve, ph, g, b, m, fin_bank(8 * b + m))
                    if b and m == 3:
                        take(steps, 3 * per)
                        recip(dve, job(st, "acc", b - 1), rpost[:, :])
                        dve.wait_ge(recip_done, job(st, "acc", b - 1) + 1)
                        steps = residual(dve, st, b - 1)
                    elif b:
                        take(steps, per)
            if ph == 3:
                dve.sem_inc(in_free[2], 3)
            for u in next_units:
                split_lo(dve, u)
            take(steps, 3 * DT)
            recip(dve, job(st, "acc", 2), rpost[:, :])
            dve.wait_ge(recip_done, job(st, "acc", 2) + 1)
            take(residual(dve, st, 2), 3 * DT)

        def act_last(act, ph, next_units):
            st, g = stage_of(ph), fin_group(ph)
            last = plan.unit[("fin", ph)] + 2
            split_hi(act, last)
            split_hi(act, last + 1)

            def sqa(b, m):
                act.wait_ge(out_free[ph], 24 * g + 8 * b + m + 1 + 26)
                square(act, job(st, "acc", b), m, acc[:, m, cols(b)])

            def zh(b, m):
                if st < 3:
                    z_hi_part(act, st, b, m, GAIN[st])

            def sqh(b, m):
                if st < 3:
                    square(act, job(st, "h", b), m, xres[:, m, cols(b)])
            for m in range(DT):
                sqa(0, m)
            for b in (1, 2):
                for m in range(DT):
                    sqa(b, m)
                    if m < 4 and b == 2:
                        zh(0, m + 4)
                    if m == 3:
                        root(act, job(st, "acc", b - 1), STAT_ACC[b - 1])
                    if m >= 4:
                        zh(b - 1, m - 4)
            for u in next_units:
                split_hi(act, u)
            for m in range(4):
                zh(1, m + 4)
                sqh(0, 2 * m)
                sqh(0, 2 * m + 1)
            root(act, job(st, "acc", 2), STAT_ACC[2])
            for m in range(DT):
                zh(2, m)
                sqh(1, m)
            if st == 1:
                root(act, job(st, "h", 0), STAT_H[0])
            for m in range(DT):
                sqh(2, m)

        def pool_stage(pool, st):
            for b in range(NB):
                add_squares(pool, job(st, "acc", b))
            if st == 1:
                pool.wait_ge(pe_block, plan.block["pre"])
                nc.gpsimd.memset(hrow[:, :], 0.0).then_inc(const_ready, 1)
            if st < 3:
                for b in range(NB):
                    add_squares(pool, job(st, "h", b))

        def stats_h(pe, stage, b):
            J = job(stage, "h", b)
            stat(pe, J, STAT_H[b], (std_done, J - 1) if b == 2 else None)

        def pe_in(pe, f, g, hooks=None):
            z_before = 24 * (0 if f == 1 else 2)
            turns = [(q, b) for q in range(4) for b in range(NB)]
            if hooks:
                turns[:6] = [(q, b) for b in range(NB) for q in range(2)]
            for q, b in turns:
                u = of(lambda x: plan.unit[(f, "in", x)] + q, g)
                slot = of(lambda x: (plan.unit[(f, "in", x)] + q) % SPLIT_SLOTS, g)
                out = (PA, PB)[q % 2][b][:, 0:BW]
                if b == 0:
                    pe.wait_ge(w_ready, u + 1)
                if q % 2 == 0:
                    pe.wait_ge(in_free[f], of(lambda x: 3 * (2 * x + q // 2) + b + 1, g))
                if hooks and q == 0:
                    pe.wait_ge(z_ready, z_before + 8 * b + 8)
                for k in range(DT):
                    mm = three(out, wslices(slot, k * P, k * P + P), (z_hi[:, k, cols(b)], z_lo[:, k, cols(b)]),
                               k == 0, k == DT - 1)
                mm.then_inc(pe_block, 1)
                if hooks and (q, b) in hooks:
                    hooks[q, b]()

        def pe_ffn(pe, f):
            st = 0 if f == 1 else 2
            pe_in(pe, f, 0, {(0, 0): (lambda: stat_fin(pe, 3)) if f == 2 else (lambda: None),
                             (0, 1): lambda: stats_h(pe, st, 0), (0, 2): lambda: stats_h(pe, st, 1),
                             (1, 2): lambda: stats_h(pe, st, 2)})
            pe_in(pe, f, 1)
            with pe.Fori(0, 4) as i:
                g = Along(i, 4, 2, 0)
                pe_out(pe, f, g)
                pe_in(pe, f, g + 2)
                pe_out(pe, f, g + 1)
                pe_in(pe, f, g + 3)
            pe_out(pe, f, 8)
            pe_in(pe, f, 10)
            pe_fin(pe, f)
            if f == 2:
                stat_fin(pe, 2)

        def tile_blocks(g):
            return [(j, b, of(lambda x: 3 * (2 * x + j) + b, g)) for j in range(2) for b in range(NB)]

        def dve_ffn_in(dve, f, g, before=None):
            for j, b, n in tile_blocks(g):
                if b == 0:
                    for q in (0, 1):
                        split_lo(dve, unit_along(f, g, 2 * j + q + 2))
                if before and j == 0:
                    before(b)
                if before and j == 0:
                    dve.wait_ge(pe_block, plan.block[(f, "in", 0)] + 2 * b + 2)
                else:
                    dve.wait_ge(pe_block, of(lambda x: plan.block[(f, "in", x)] + 6 * j + 3 + b + 1, g))
                s = (3 * j + b) % 2
                nc.vector.tensor_tensor(ta[:, s, :], PA[b][:, 0:BW], rstd[:, cols(b)], ALU.mult).then_inc(ta_done[f], 1)
                nc.vector.tensor_tensor(tb[:, s, :], PB[b][:, 0:BW], rstd[:, cols(b)], ALU.mult).then_inc(in_free[f], 1)
                dve.wait_ge(silu_done[f], n + 1)
                dve.wait_ge(in_free[f], n + 1 + 3)
                nc.vector.tensor_tensor(tb[:, s, :], tb[:, s, :], ta[:, s, :], ALU.mult).then_inc(h_mul[f], 1)
                dve.wait_ge(hid_hi_done[f], n + 1)
                hs = of(lambda x: 2 * (x % 2) + j, g)
                nc.vector.tensor_tensor(hid_lo[:, hs, cols(b)], tb[:, s, :], hid_hi[:, hs, cols(b)].bitcast(F32),
                                        ALU.subtract).then_inc(hid_ready[f], 1)

        def unit_along(f, g, ahead):
            if isinstance(g, Along):
                v = [plan.unit[(f, "in", g.a * k + g.b)] + ahead for k in range(g.n)]
                return Along(g.i, g.n, v[1] - v[0], v[0])
            return plan.unit[(f, "in", g)] + ahead

        def act_ffn_in(act, f, g, first=False, before=None):
            for j, b, n in tile_blocks(g):
                if b == 0:
                    for q in (0, 1):
                        split_hi(act, unit_along(f, g, 2 * j + q + 2))
                s = (3 * j + b) % 2
                if before and j == 0:
                    before(b)
                act.wait_ge(ta_done[f], n + 1)
                nc.scalar.activation(ta[:, s, :], ta[:, s, :], ACT.Silu).then_inc(silu_done[f], 1)
                act.wait_ge(h_mul[f], n + 1)
                if not first and j == 0 and b == 0:
                    act.wait_ge(pe_block, of(lambda x: plan.block[(f, "out", x - 2)] + 24, g))
                hs = of(lambda x: 2 * (x % 2) + j, g)
                nc.scalar.activation(hid_hi[:, hs, cols(b)], tb[:, s, :], ACT.Copy).then_inc(hid_hi_done[f], 1)

        def out_unit(ph, g):
            if isinstance(g, Along):
                v = [plan.unit[out_key(ph, g.a * k + g.b)] for k in range(g.n)]
                return Along(g.i, g.n, v[1] - v[0], v[0])
            return plan.unit[out_key(ph, g)]

        def dve_outs(dve, ph, g):
            split_lo(dve, out_unit(ph, g) + 2)
            for b in range(NB):
                for m in range(DT):
                    dve_out(dve, ph, g, b, m)
            split_lo(dve, out_unit(ph, g) + 3)

        def act_outs(act, ph, g):
            split_hi(act, out_unit(ph, g) + 2)
            split_hi(act, out_unit(ph, g) + 3)

        def dve_ffn(dve, f, before, next_units):
            dve_ffn_in(dve, f, 0, before)
            dve_ffn_in(dve, f, 1)
            dve.wait_ge(acc_zero, 1 if f == 1 else 3)
            dve.sem_inc(out_free[f], 26)
            with dve.Fori(0, 4) as i:
                g = Along(i, 4, 2, 0)
                dve_outs(dve, f, g)
                dve_ffn_in(dve, f, g + 2)
                dve_outs(dve, f, g + 1)
                dve_ffn_in(dve, f, g + 3)
            dve_outs(dve, f, 8)
            dve_ffn_in(dve, f, 10)
            dve_last(dve, f, next_units)

        def act_ffn(act, f, next_units):
            st = 0 if f == 1 else 2
            act_ffn_in(act, f, 0, True, lambda b: root(act, job(st, "h", b), STAT_H[b]))
            act_ffn_in(act, f, 1, True)
            with act.Fori(0, 4) as i:
                g = Along(i, 4, 2, 0)
                act_outs(act, f, g)
                act_ffn_in(act, f, g + 2)
                act_outs(act, f, g + 1)
                act_ffn_in(act, f, g + 3)
            act_outs(act, f, 8)
            act_ffn_in(act, f, 10)
            act_last(act, f, next_units)

        def sp_ffn(sp, f, skip=0):
            def ins(g, start=0):
                for q in range(start, 4):
                    load_unit(sp, (f, "in"), g, q)

            def outs(g):
                for q in range(2):
                    load_unit(sp, (f, "out"), g, q)
            ins(0, skip)
            ins(1)
            with sp.Fori(0, 4) as i:
                g = Along(i, 4, 2, 0)
                outs(g)
                ins(g + 2)
                outs(g + 1)
                ins(g + 3)
            outs(8)
            ins(10)
            for q in range(4):
                load_unit(sp, "fin", f, q)

        def vec_rows(sp):
            names = [("ffn1_pre_g", V_PRE1), ("ffn1_post_g", V_POST1), ("mix_pre_g", V_PREM), ("mix_post_g", V_POSTM),
                     ("ffn2_pre_g", V_PRE2), ("ffn2_post_g", V_POST2), ("pool_scale", V_PSC), ("b_in", V_BIN),
                     ("ssm_b_glu", V_BGLU)]
            for name, r in names:
                n = a[name].shape[0] // P
                sp.dma_start(vrow[r:r + n, :], a[name].rearrange("(n p) -> n p", p=P)).then_inc(vec_loaded, 16)
            for t in range(L):
                sp.dma_start(vrow[V_D:V_D + G, t * GC:(t + 1) * GC],
                             a["ssm_d"].rearrange("(g c) -> g c", c=GC)).then_inc(vec_loaded, 16)
            return 16 * (len(names) + L)
        VEC_DMAS = 16 * 17
        ORDER = [8, 0, 1, 2, 3, 4, 5, 6, 7]

        def sp_start(sp):
            xp = a["x_prompt"].rearrange("(k s) d -> s k d", s=L)
            for tile in ORDER:
                if tile == 8:
                    sp.dma_start(xrow[0:DEC, 8, :], a["x_sample"]).then_inc(x_loaded[8], 16)
                else:
                    sp.dma_start(xrow[:, tile, :], xp[tile]).then_inc(x_loaded[tile], 16)
            for q in range(3):
                load_unit(sp, (1, "in"), 0, q)
            vec_rows(sp)

        def pe_start(pe):
            pe.wait_ge(const_ready, 5)
            F = 0
            for tile in ORDER:
                rows = DEC if tile == 8 else P
                pe.wait_ge(x_loaded[tile], 16)
                for half in range(2):
                    if F >= 6:
                        pe.wait_ge(x_dve if F % 2 == 0 else x_act, (F - 6) // 2 + 1)
                    for j in range(4):
                        m = 4 * half + j
                        mm = nc.tensor.transpose(bank[F % 6][:, j * P:j * P + rows], xrow[0:rows, tile, m * P:(m + 1) * P],
                                                 ident[0:rows, 0:rows])
                    mm.then_inc(x_turned, 1)
                    F += 1
            pe.wait_ge(vec_loaded, VEC_DMAS)
            nc.tensor.transpose(PC[0][:, 0:P], vrow[:, :], ident[:, :]).then_inc(vec_mm, 1)

        def empty_x(eng, copy, which, done):
            F = 0
            for tile in ORDER:
                for half in range(2):
                    if F % 2 == which:
                        eng.wait_ge(x_turned, F + 1)
                        src = bank[F % 6][:, :].rearrange("p (j t) -> p j t", j=4)
                        dst = xres[:, 4 * half:4 * half + 4, :]
                        if tile < 8:
                            copy(dst[:, :, tile * K:tile * K + KP], src[:, :, 0:P]).then_inc(done, 1)
                        else:
                            for j in range(4):
                                ins = copy(dst[:, j, :].rearrange("p (s k) -> p s k", s=L)[:, :, KP:K],
                                           src[:, j, 0:DEC].rearrange("p (k s) -> p s k", s=L))
                            ins.then_inc(done, 1)
                    F += 1

        S = {n: k for k, n in enumerate("dt mag th n r sn sh cs ar ai den rden nr fr fi t0 t1 p x w2r w2i w4r w4i w8r w8i m2 m4 m8 rhr rhi lrdt e0 e1".split())}
        LRE, LIM, H0R, H0I, LST = range(0, 80, 16)
        ROW_DMAS, PREP_DMAS = 16 * 6, 16 * 8

        def sp_prep(sp):
            sp.wait_ge(pe_block, plan.block["pre"])
            rows = lambda n: a[n].rearrange("(j g) s -> j (g s)", g=2)
            sp.dma_start(lsrow[LST:LST + 16, :], a["ssm_log_step"].rearrange("(j g) -> j g", g=2)).then_inc(row_loaded, 16)
            for r, n in ((LRE, "ssm_lambda_re"), (LIM, "ssm_lambda_im"), (H0R, "state_ssm_re"), (H0I, "state_ssm_im")):
                sp.dma_start(srow[r:r + 16, :], rows(n)).then_inc(row_loaded, 16)
            sp.wait_ge(const_ready, 6)
            sp.dma_start(hrow[1:16, :], a["cache_pool"]).then_inc(row_loaded, 16)

        def sp_prep_tables(sp):
            for c, n in enumerate(("ssm_b_re", "ssm_b_im")):
                sp.dma_start(braw[:, c], a[n].rearrange("(j g) s c -> g s j c", g=2).rearrange("g s j c -> (g s) j c")
                             ).then_inc(sp_loaded, 16)
            for c, n in enumerate(("ssm_c_re", "ssm_c_im")):
                for twice in range(2):
                    sp.dma_start(crow[:, c, :, twice, :], a[n].rearrange("g c s -> (g c) s").rearrange("(t p) s -> p t s", p=P)
                                 ).then_inc(sp_loaded, 16)
            sp.dma_start(cnt[:, :, :], a["window_counts"]).then_inc(sp_loaded, 16)
            sp.dma_start(mask[:, :], a["scan_mask"]).then_inc(sp_loaded, 16)

        PREP_PSUM = PC[1][:, BW:BW + 144]

        def pe_prep(pe):
            pe.wait_ge(row_loaded, ROW_DMAS)
            pe.wait_ge(prep_dve, 1)
            pe.wait_ge(std_done, job(1, "h", 1) + 1)
            nc.tensor.transpose(PREP_PSUM[:, 0:80], srow[0:80, :], ident[0:80, 0:80])
            for g in range(4):
                mm = nc.tensor.transpose(PREP_PSUM[:, 80 + 16 * g:96 + 16 * g], hrow[:, g * P:(g + 1) * P], ident[0:16, 0:16])
            mm.then_inc(sp_mm, 1)

        def pe_prep_c(pe):
            pe.wait_ge(sp_loaded, PREP_DMAS)
            pe.wait_ge(std_done, job(1, "h", 2) + 1)
            pe.wait_ge(own["dve_prep"], 2)
            for c in range(2):
                for t in range(4):
                    mm = nc.tensor.transpose(PC[c][:, t * P:(t + 1) * P],
                                             crow[:, c, t].rearrange("p a s -> p (a s)"), ident[:, :])
            mm.then_inc(sp_mm, 1)

        class Steps:

            def __init__(self, eng, s, i=None, per=0, base=0, ops=nc.vector):
                self.ops = ops
                self.eng, self.s, self.i, self.per, self.base, self.n = eng, s, i, per, base, 0

            def do(self, ins):
                self.n += 1
                ins.then_inc(self.s, 1)

            def sync(self):
                if self.base + self.n > 0 or self.i is not None:
                    v = self.base + self.n
                    self.eng.wait_ge(self.s, v if self.i is None else self.i * self.per + v)

        def take(dst, src):
            return nc.vector.tensor_scalar(dst, src, 1.0, None, ALU.mult)

        def cmul(st, out, x, y, tmp, conj_x=False, neg_im=False):
            tt = st.ops.tensor_tensor
            (xr, xi), (yr, yi), (t0, t1) = x, y, tmp
            st.do(tt(t0, xr, yr, ALU.mult))
            st.do(tt(t1, xi, yi, ALU.mult))
            st.sync()
            st.do(tt(out[0], t0, t1, ALU.add if conj_x else ALU.subtract))
            st.sync()
            st.do(tt(t0, xr, yi, ALU.mult))
            st.do(tt(t1, xi, yr, ALU.mult))
            st.sync()
            if neg_im:
                st.do(nc.vector.scalar_tensor_tensor(out[1], t0, -1.0, t1, ALU.mult, ALU.subtract))
            else:
                st.do(tt(out[1], t0, t1, ALU.subtract if conj_x else ALU.add))

        v = lambda n: sm[:, S[n], :]
        MAGIC = 12582912.0

        def chain_exp(st, out, x):
            ts, stt = nc.vector.tensor_scalar, nc.vector.scalar_tensor_tensor
            st.sync(); st.do(ts(v("x"), x, -87.0, 87.0, ALU.max, ALU.min))
            st.sync(); st.do(ts(v("t0"), v("x"), 1.4426950408889634, MAGIC, ALU.mult, ALU.add))
            st.sync(); st.do(ts(v("n"), v("t0"), MAGIC, None, ALU.subtract))
            st.sync(); st.do(stt(v("r"), v("n"), -0.693359375, v("x"), ALU.mult, ALU.add))
            st.do(ts(smi[:, :], v("n"), 127.0, 8388608.0, ALU.add, ALU.mult))
            st.sync(); st.do(stt(v("x"), v("n"), 2.12194440054690583e-4, v("r"), ALU.mult, ALU.add))
            st.sync(); st.do(ts(v("p"), v("x"), 1 / 5040, None, ALU.mult))
            for c in (1 / 720, 1 / 120, 1 / 24, 1 / 6, 0.5, 1.0):
                st.sync(); st.do(stt(v("p"), v("p"), c, v("x"), ALU.add, ALU.mult))
            st.sync(); st.do(stt(out, v("p"), 1.0, smi[:, :].bitcast(F32), ALU.add, ALU.mult))

        def dve_prep_a(dve):
            ts, stt, tt, cp = nc.vector.tensor_scalar, nc.vector.scalar_tensor_tensor, nc.vector.tensor_tensor, nc.vector.tensor_copy
            dve.wait_ge(row_loaded, ROW_DMAS)
            nc.vector.tensor_copy(srow[LST:LST + 16, :].rearrange("j (g s) -> j g s", g=2),
                                  lsrow[LST:LST + 16, :].unsqueeze(2).broadcast_to([16, 2, NS])).then_inc(prep_dve, 1)
            recip_row(dve, 1, 0)
            for r in range(3):
                dve_pre_evac(dve, r)
            recip_row(dve, 1, 1)
            for r in range(3, 6):
                dve_pre_evac(dve, r)
            dve.sem_inc(m_scaled, 3)
            st = Steps(dve, own["dve_prep"])
            dve.wait_ge(sp_mm, 1)
            st.do(cp(sp_[:, :], PREP_PSUM[:, 0:80]))
            st.do(cp(hcol[:, :, :].rearrange("p g r -> p (g r)"), PREP_PSUM[:, 80:144]))
            chain_exp(st, v("dt"), sp_[:, LST:LST + 16])
            recip_row(dve, 1, 2)
            dve_pre_evac(dve, 6)
            split_lo(dve, plan.unit["pre"] + PRE)
            st.sync()
            st.do(tt(v("lrdt"), sp_[:, LRE:LRE + 16], v("dt"), ALU.mult))
            st.do(tt(v("th"), sp_[:, LIM:LIM + 16], v("dt"), ALU.mult))
            chain_exp(st, v("mag"), v("lrdt"))
            dve_pre_evac(dve, 7)
            split_lo(dve, plan.unit["pre"] + PRE + 1)
            st.sync(); st.do(ts(v("t0"), v("th"), 1 / (2 * pi), MAGIC, ALU.mult, ALU.add))
            st.sync(); st.do(ts(v("n"), v("t0"), MAGIC, None, ALU.subtract))
            x = v("th")
            for c in (6.28125, 0.00193500518798828125, 3.0199159819567e-7):
                st.sync(); st.do(stt(v("r"), v("n"), -c, x, ALU.mult, ALU.add))
                x = v("r")
            st.sync(); st.do(ts(v("r"), v("r"), -3.1415925, 3.1415925, ALU.max, ALU.min))
            st.sync()
            dve.sem_inc(prep_dve, 1)
            dve_pre_evac(dve, 8)
            return st

        def unit_modulus(st, re, im, t0, t1):
            tt = st.ops.tensor_tensor
            st.sync()
            st.do(tt(t0, re, re, ALU.mult))
            st.do(tt(t1, im, im, ALU.mult))
            st.sync(); st.do(tt(t0, t0, t1, ALU.add))
            st.sync(); st.do(st.ops.tensor_scalar(t0, t0, -0.5, 1.5, ALU.mult, ALU.add))
            st.sync()
            st.do(tt(re, re, t0, ALU.mult))
            st.do(tt(im, im, t0, ALU.mult))
            st.sync()

        def act_prep(act):
            act.wait_ge(prep_dve, 2)
            nc.scalar.activation(v("sn"), v("r"), ACT.Sin).then_inc(prep_act, 1)
            nc.scalar.activation(v("sh"), v("r"), ACT.Sin, scale=0.5).then_inc(prep_act, 1)

        def dve_prep_b(dve, st):
            ts, stt, tt, cp = nc.vector.tensor_scalar, nc.vector.scalar_tensor_tensor, nc.vector.tensor_tensor, nc.vector.tensor_copy
            dve.wait_ge(sp_mm, 2)
            for c in range(2):
                for h in range(2):
                    half = slice(64 * h, 64 * h + 64)
                    st.do(cp(cc[half, c], PC[c][half, :].rearrange("p (j g c) -> p j g c", g=2, c=GC)[:, :, h, :]))
            dve.wait_ge(prep_act, 2)
            st.do(tt(v("t0"), v("sh"), v("sh"), ALU.mult))
            st.sync(); st.do(ts(v("cs"), v("t0"), -2.0, 1.0, ALU.mult, ALU.add))
            st.sync()
            dve.sem_inc(prep_dve, 1)
            st.do(tt(v("ar"), v("mag"), v("cs"), ALU.mult))
            st.do(tt(v("ai"), v("mag"), v("sn"), ALU.mult))
            lr, li = sp_[:, LRE:LRE + 16], sp_[:, LIM:LIM + 16]
            st.do(tt(v("t0"), lr, lr, ALU.mult))
            st.do(tt(v("t1"), li, li, ALU.mult))
            st.sync()
            st.do(tt(v("den"), v("t0"), v("t1"), ALU.add))
            st.do(ts(v("nr"), v("ar"), 1.0, None, ALU.subtract))
            st.sync(); st.do(nc.vector.reciprocal(v("rden"), v("den")))
            cmul(st, (v("fr"), v("fi")), (lr, li), (v("nr"), v("ai")), (v("t0"), v("t1")), conj_x=True)
            st.sync()
            st.do(tt(v("fr"), v("fr"), v("rden"), ALU.mult))
            st.do(tt(v("fi"), v("fi"), v("rden"), ALU.mult))
            st.sync()
            f3 = lambda n: v(n).unsqueeze(2).broadcast_to([P, NPAIR, GC])
            tmp = [ctmp[:, c, :].rearrange("p (j c) -> p j c", c=GC) for c in range(2)]
            cmul(st, (bb[:, 0], bb[:, 1]), (f3("fr"), f3("fi")), (braw[:, 0], braw[:, 1]), tmp)
            st.do(nc.vector.memset(apw[:, 0, :, 0:1], 1.0))
            st.do(nc.vector.memset(apw[:, 1, :, 0:1], 0.0))
            st.do(cp(apw[:, 0, :, 1:2], v("ar").unsqueeze(2)))
            st.do(cp(apw[:, 1, :, 1:2], v("ai").unsqueeze(2)))

            def powers(tab, lo, n, by):
                st.sync()
                t = [ctmp[:, c, 0:NPAIR * n].rearrange("p (j k) -> p j k", k=n) for c in range(2)]
                cmul(st, [tab[:, c, :, by + 1:by + 1 + n] for c in range(2)],
                     [tab[:, c, :, lo:lo + n] for c in range(2)],
                     [tab[:, c, :, by:by + 1].broadcast_to([P, NPAIR, n]) for c in range(2)], t)
            powers(apw, 1, 1, 1)
            powers(apw, 1, 2, 2)
            powers(apw, 1, 4, 4)
            st.sync()
            for c in range(2):
                for k in range(L):
                    st.do(cp(arev[:, c, :, L - 1 - k:L - k], apw[:, c, :, k:k + 1]))
            st.sync()

        def pool_prep(pool):
            tp = nc.gpsimd
            tt, cp = tp.tensor_tensor, tp.tensor_copy
            st = Steps(pool, own["pool_turns"], ops=nc.gpsimd)
            ptmp = [x.rearrange("p s k -> p (s k)")[:, 0:16 * NPAIR] for x in (ext[:, :, :], sum_a[:, :, :])]
            pool.wait_ge(h_spilled, 48)
            pool.wait_ge(prep_dve, 3)
            x = ("cs", "sn")
            for y in (("w2r", "w2i"), ("w4r", "w4i"), ("w8r", "w8i")):
                st.sync()
                cmul(st, (v(y[0]), v(y[1])), (v(x[0]), v(x[1])), (v(x[0]), v(x[1])), (v("e0"), v("e1")))
                x = y
            unit_modulus(st, v("w8r"), v("w8i"), v("e0"), v("e1"))
            x = "mag"
            for y in ("m2", "m4", "m8"):
                st.sync(); st.do(tt(v(y), v(x), v(x), ALU.mult))
                x = y
            st.sync()
            for c, n in enumerate(("w8r", "w8i")):
                st.do(cp(wlo[:, c, :, 0:1], v(n).unsqueeze(2)))
                st.do(tp.memset(whi[:, c, :, 0:1], 1.0 - c))
                st.do(tt(v(("rhr", "rhi")[c]), v("m8"), sp_[:, (H0R, H0I)[c]:(H0R, H0I)[c] + 16], ALU.mult))

            def spread(tab, lo, n, by):
                st.sync()
                t = [ptmp[c][:, 0:NPAIR * n].rearrange("p (j k) -> p j k", k=n) for c in range(2)]
                cmul(st, [tab[:, c, :, by + 1:by + 1 + n] for c in range(2)],
                     [tab[:, c, :, lo:lo + n] for c in range(2)],
                     [tab[:, c, :, by:by + 1].broadcast_to([P, NPAIR, n]) for c in range(2)], t)
            for n in (1, 2, 4, 8):
                spread(wlo, 0, n, n - 1)
            flat = lambda tab, c: tab[:, c].rearrange("p j k -> p (j k)")
            unit_modulus(st, flat(wlo, 0), flat(wlo, 1), ptmp[0], ptmp[1])
            for c in range(2):
                st.do(cp(whi[:, c, :, 1:2], wlo[:, c, :, 15:16]))
            spread(whi, 1, 1, 1)
            spread(whi, 1, 1, 2)
            spread(whi, 1, 3, 3)
            spread(whi, 1, 1, 6)
            unit_modulus(st, flat(whi, 0), flat(whi, 1), ptmp[0][:, 0:8 * NPAIR], ptmp[1][:, 0:8 * NPAIR])
            pool.sem_inc(turns_ready, 1)

        def mix_unit(i, q):
            return Along(i, 4, 6, plan.unit[("mix", 0)] + q)

        def mix_block(i, q, b):
            v0 = plan.block[("mix", 0)]
            return i * PASS + (v0 + 3 * q + b + 1)

        def skip_hi(act, i):
            act.wait_ge(w_hi_done, i * 6 + (plan.unit[("mix", 0)] + MQ))
            act.sem_inc(w_hi_done, 1)

        def skip_lo(dve, i):
            dve.wait_ge(w_ready, i * 6 + (plan.unit[("mix", 0)] + MQ))
            dve.sem_inc(w_ready, 1)

        PRE_BANK = [PB, PA, PB]

        def pe_pre(pe):
            u0 = plan.unit["pre"]
            for b in range(NB):
                for u in range(PRE):
                    r = PRE * b + u
                    if b == 0:
                        pe.wait_ge(w_ready, u0 + u + 1)
                        pe.wait_ge(out_free[1], 24 * fin_group(1) + 26 + 24)
                    if u == 0:
                        pe.wait_ge(z_ready, 24 + 8 * b + 8)
                    if b == 2:
                        pe.wait_ge(pre_scaled, u + 1)
                    for k in range(DT):
                        mm = three(PRE_BANK[b][u][:, 0:BW], wslices((u0 + u) % SPLIT_SLOTS, k * P, k * P + P),
                                   (z_hi[:, k, cols(b)], z_lo[:, k, cols(b)]), k == 0, k == DT - 1)
                    mm.then_inc(pe_block, 1)
                    if r == 0:
                        stat_fin(pe, 1)
                    if r in (3, 5, 7):
                        stats_h(pe, 1, (r - 3) // 2)
                    if r == 6:
                        pe_prep(pe)
            pe_prep_c(pe)

        def dve_pre_evac(dve, r):
            b, u = divmod(r, PRE)
            dve.wait_ge(pe_block, plan.block["pre"] + r + 1)
            if r >= 3:
                dve.wait_ge(pre_stored[r % 3], 16 * (r // 3))
            nc.vector.tensor_tensor(mt[r % 3], PRE_BANK[b][u][:, 0:BW], rstd[:, cols(b)], ALU.mult).then_inc(pre_scaled, 1)

        def act_pre(act):
            def gate(r):
                b, u = divmod(r, PRE)
                act.wait_ge(pre_scaled, r + 1)
                nc.scalar.activation(mt[r % 3], mt[r % 3], ACT.Sigmoid, bias=vecs[:, V_BIN + 8 + u:V_BIN + 9 + u]).then_inc(pre_gate, 1)
                act.wait_ge(pre_gate, r + 1)
                act.dma_start(gate_dram[u, :, cols(b)], mt[r % 3]).then_inc(pre_stored[r % 3], 16)
            root(act, job(1, "h", 1), STAT_H[1])
            for r in range(3):
                gate(r)
            root(act, job(1, "h", 2), STAT_H[2])
            for r in range(3, 7):
                gate(r)
            split_hi(act, plan.unit["pre"] + PRE)
            gate(7)
            split_hi(act, plan.unit["pre"] + PRE + 1)
            gate(8)

        def pe_mix(pe):
            with pe.Fori(0, 4) as i:
                for q in range(MQ):
                    pe.wait_ge(w_ready, i * 6 + (plan.unit[("mix", 0)] + q + 1))
                    slot = (plan.unit[("mix", 0)] + q) % SPLIT_SLOTS
                    for b in range(NB):
                        pe.wait_ge(m_scaled, i * PASS + (3 * q + b + 1))
                        for k in range(DT):
                            mm = three(PA[b][:, 0:BW], wslices(slot, k * P, k * P + P),
                                       (z_hi[:, k, cols(b)], z_lo[:, k, cols(b)]), k == 0, k == DT - 1)
                        mm.then_inc(pe_block, 1)
                    if q == 1:
                        pe_tables(pe, i)
                    if q == 2:
                        pe_states(pe, i, 0)
                    if q == 3:
                        pe_y(pe, i, 0)
                        pe_states(pe, i, 1)
                    if q == 4:
                        pe_y(pe, i, 1)
            u = plan.unit["post"]
            pe.wait_ge(w_ready, u + 1)
            for b in range(NB):
                pe.wait_ge(m_scaled, 4 * PASS + b + 1)
                for k in range(DT):
                    mm = three(PA[b][:, 0:BW], wslices(u % SPLIT_SLOTS, k * P, k * P + P),
                               (z_hi[:, k, cols(b)], z_lo[:, k, cols(b)]), k == 0, k == DT - 1)
                mm.then_inc(pe_block, 1)

        def pe_tables(pe, i):
            pe.wait_ge(pq_ready, i + 1)
            pe.wait_ge(e_read, i * 2 + 1)
            for c in range(2):
                for p in range(4):
                    mm = nc.tensor.transpose(PB[c][:, p * P:(p + 1) * P], pt[:, c, p].rearrange("p s c -> p (s c)"), ident[:, :])
                mm.then_inc(prep_mm, 1)
            for p in range(4):
                for c in range(2):
                    mm = nc.tensor.matmul(PB[2][32 * p:32 * p + 32, 0:P], bbst[:, c, p].rearrange("p g c -> p (g c)"),
                                          qt[:, c, p, 0:L, :].rearrange("p k c -> p (k c)"), start=(c == 0), stop=(c == 1))
            mm.then_inc(prep_mm, 1)

        def pe_states(pe, i, hf):
            if hf == 0:
                pe.wait_ge(prep_ev, i * 3 + 3)
                pe.wait_ge(ur_loaded, (i + 1) * 128)
            else:
                pe.wait_ge(e_read, i * 2 + 2)
            for c in range(2):
                for qq in range(2):
                    for h in range(2):
                        p = 2 * hf + qq
                        mm = nc.tensor.matmul(PB[c][64 * h:64 * h + 64, qq * K:(qq + 1) * K], bint[:, c, p, 64 * h:64 * h + 64],
                                              ur[:, 2 * p + h, :], start=True, stop=True)
            mm.then_inc(e_mm, 1)

        def pe_y(pe, i, hf):
            if hf == 0:
                pe.wait_ge(toep_loaded, (i + 1) * 128)
            pe.wait_ge(hb_ready, i * 2 + (hf + 1))
            pe.wait_ge(y_ev, i * 2 + (hf + 1))
            for qq in range(2):
                p = 2 * hf + qq
                out = [PC[h][:, qq * K:(qq + 1) * K] for h in range(2)]
                for h in range(2):
                    nc.tensor.matmul(out[h], toep[:, 2 * p + h, :], ur[:, 2 * p + h, :], start=True, stop=False)
                for h in range(2):
                    rows = slice(64 * h, 64 * h + 64)
                    for c in range(2):
                        mm = nc.tensor.matmul(out[h], qt[rows, c, p, 1:L + 1, :].rearrange("p k c -> p (k c)"),
                                              hb[rows, c, qq, 0:K], start=False, stop=(c == 1))
            mm.then_inc(y_mm, 1)

        DVE_PER = 82

        def dve_mix_evac(dve, i, q, blocks=range(NB)):
            for b in blocks:
                dve.wait_ge(pe_block, mix_block(i, q, b))
                dve.wait_ge(m_out, i * PASS + (3 * q + b + 1))
                nc.vector.tensor_tensor(mt[b], PA[b][:, 0:BW], rstd[:, cols(b)], ALU.mult).then_inc(m_scaled, 1)

        def dve_mix(dve):
            tt, stt, cp = nc.vector.tensor_tensor, nc.vector.scalar_tensor_tensor, nc.vector.tensor_copy
            dve.wait_ge(h_spilled, 48)
            dve.sem_inc(e_read, 1)
            dve.sem_inc(y_ev, 1)
            pre = Steps(dve, own["dve_mix"])
            pre.do(nc.vector.memset(taps[:, 0:P], 0.0))
            pre.do(nc.vector.memset(hb[:, :, :, 0:1], 0.0))
            pre.sync()
            with dve.Fori(0, 4) as i:
                st = Steps(dve, own["dve_mix"], i, DVE_PER, 2)
                st.sync()
                pairs = lambda tab, c: tab[:, c, ds(i * 4, 4)]

                def evac(q, blocks=range(NB)):
                    dve_mix_evac(dve, i, q, blocks)

                split_lo(dve, mix_unit(i, 2))
                dve.wait_ge(y_mm, i * 2 + 1)
                st.do(take(dst_[:, :], vecs[:, ds(i * 8 + V_D, 8)]))
                st.do(take(bst[:, 0:1], vecs[:, ds(i * 1 + V_BIN, 1)]))
                st.do(take(bst[:, 1:2], vecs[:, ds(i * 1 + (V_BIN + 4), 1)]))
                st.do(take(bst[:, 2:5], vecs[:, ds(i * 3 + (V_BIN + 8 + PRE), 3)]))
                st.sync()
                evac(0, (0,))
                shp = lambda k: [P, 4, k, GC]
                tmp = lambda k: [mtmp[:, c, :, 0:k * GC].rearrange("p j (k c) -> p j k c", c=GC) for c in range(2)]
                per_k = lambda tab, c, k: pairs(tab, c).unsqueeze(3).broadcast_to(shp(k))
                per_c = lambda tab, c, k: pairs(tab, c).unsqueeze(2).broadcast_to(shp(k))
                cmul(st, (pt[:, 0], pt[:, 1]), [per_k(arev, c, L) for c in range(2)], [per_c(bb, c, L) for c in range(2)], tmp(L))
                evac(0, (1, 2))
                st.sync()
                cmul(st, (qt[:, 0], qt[:, 1]), [per_k(apw, c, L + 1) for c in range(2)], [per_c(cc, c, L + 1) for c in range(2)],
                     tmp(L + 1), neg_im=True)
                for c in range(2):
                    st.do(nc.vector.memset(bbst[:, c], 0.0))
                st.sync()
                for c in range(2):
                    for h in range(2):
                        rows = slice(64 * h, 64 * h + 64)
                        st.do(take(bbst[rows, c, :, h, :], bb[rows, c, ds(i * 4, 4)]))
                st.sync()
                dve.sem_inc(pq_ready, 1)
                split_lo(dve, mix_unit(i, 3))
                evac(1)
                for c in range(2):
                    dve.wait_ge(prep_mm, i * 3 + (c + 1))
                    cp(bint[:, c].rearrange("p j s -> p (j s)"), PB[c][:, :]).then_inc(prep_ev, 1)
                dve.wait_ge(prep_mm, i * 3 + 3)
                cp(taps[:, P:2 * P], PB[2][:, 0:P]).then_inc(prep_ev, 1)
                split_lo(dve, mix_unit(i, 4))
                dve.wait_ge(turns_ready, 1)
                w4 = [P, 4, L, 16]
                wtv = [wt[:, c, :, 0:KP].rearrange("p j (a b) -> p j a b", b=16) for c in range(2)]
                tw = [mtmp[:, c, :, 0:KP].rearrange("p j (a b) -> p j a b", b=16) for c in range(2)]
                cmul(st, wtv, [pairs(whi, c).unsqueeze(3).broadcast_to(w4) for c in range(2)],
                     [pairs(wlo, c).unsqueeze(2).broadcast_to(w4) for c in range(2)], tw)
                st.sync()
                st.do(cp(wt[:, :, :, KP:K], wt[:, :, :, 0:KS]))
                st.do(tt(dec[:, :, :], sm[:, S["m8"], ds(i * 4, 4)].unsqueeze(2).broadcast_to([P, 4, K]),
                         mask[:, :].unsqueeze(1).broadcast_to([P, 4, K]), ALU.mult))
                st.sync()
                evac(2)
                dve_states(dve, st, i, 0)
                evac(3)
                skip_lo(dve, i)
                split_lo(dve, mix_unit(i, 6))
                dve_y_sum(dve, st, i, 0)
                dve_states(dve, st, i, 1)
                dve_gelu(dve, st, i, 0)
                evac(4)
                dve_y_sum(dve, st, i, 1)
                dve_gelu(dve, st, i, 1, mix_unit(i, 7))
                assert st.n == DVE_PER, st.n

        def dve_states(dve, st, i, hf):
            tt, stt, cp = nc.vector.tensor_tensor, nc.vector.scalar_tensor_tensor, nc.vector.tensor_copy
            dve.wait_ge(e_mm, i * 2 + (hf + 1))
            E = [PB[c][:, 0:2 * K].rearrange("p (q k) -> p q k", k=K) for c in range(2)]
            w = [wt[:, c, 2 * hf:2 * hf + 2, :] for c in range(2)]
            st.do(tt(r1[:, :, :], E[0], w[0], ALU.mult))
            st.do(tt(r2[:, :, :], E[1], w[1], ALU.mult))
            st.do(tt(r3[:, :, :], E[1], w[0], ALU.mult))
            tt(r4[:, :, :], E[0], w[1], ALU.mult).then_inc(e_read, 1)
            dve.wait_ge(e_read, i * 2 + (hf + 2))
            st.sync()
            st.do(tt(vr[:, :, :], r1[:, :, :], r2[:, :, :], ALU.add))
            st.do(tt(vi[:, :, :], r3[:, :, :], r4[:, :, :], ALU.subtract))
            st.sync()
            pr = lambda n: sm[:, S[n], ds(i * 4 + 2 * hf, 2)].unsqueeze(2)
            st.do(tt(vr[:, :, KP:KP + 1], vr[:, :, KP:KP + 1], pr("rhr"), ALU.add))
            st.do(tt(vi[:, :, KP:KP + 1], vi[:, :, KP:KP + 1], pr("rhi"), ALU.add))
            st.sync()
            flat = lambda x: x.rearrange("p q k -> p (q k)")
            dd = flat(dec[:, 2 * hf:2 * hf + 2, :])
            st.do(nc.vector.tensor_tensor_scan(flat(r1[:, :, :]), dd, flat(vr[:, :, :]), 0.0, ALU.mult, ALU.add))
            st.do(nc.vector.tensor_tensor_scan(flat(r2[:, :, :]), dd, flat(vi[:, :, :]), 0.0, ALU.mult, ALU.add))
            st.sync()
            cmul(st, [hb[:, c, :, 1:K + 1] for c in range(2)], w, (r1[:, :, :], r2[:, :, :]), (r3[:, :, :], r4[:, :, :]))
            st.sync()
            for c in range(2):
                st.do(take(hfin[:, c, ds(i * 4 + 2 * hf, 2)].unsqueeze(2), hb[:, c, :, KP:KP + 1]))
                st.do(take(hfin[:, 2 + c, ds(i * 4 + 2 * hf, 2)].unsqueeze(2), hb[:, c, :, K:K + 1]))
            st.sync()
            for c in range(2):
                st.do(take(hb[:, c, :, KP:KP + 1], sp_[:, ds(i * 4 + (2 * hf + (H0R, H0I)[c]), 2)].unsqueeze(2)))
            st.sync()
            dve.sem_inc(hb_ready, 1)

        def dve_y_sum(dve, st, i, hf):
            stt = nc.vector.scalar_tensor_tensor
            dve.wait_ge(y_mm, i * 2 + (hf + 2))
            dve.wait_ge(y_stored, i * 256 + 128 * (hf + 1))
            for j in range(4):
                qq, h = j // 2, j % 2
                g = 4 * hf + j
                ins = stt(yv[:, hf, j, :], ur[:, g, :], dst_[:, g:g + 1], PC[h][:, qq * K:(qq + 1) * K], ALU.mult, ALU.add)
                if j < 3:
                    st.do(ins)
            ins.then_inc(y_ev, 1)

        def dve_gelu(dve, st, i, hf, split_meanwhile=None):
            tt = nc.vector.tensor_tensor
            y = yv[:, hf]
            dve.wait_ge(y_ev, i * 2 + (hf + 2))
            st.sync()
            st.do(tt(ya[:, :, :], y, y, ALU.mult))
            st.sync()
            st.do(nc.vector.tensor_scalar(ya[:, :, :], ya[:, :, :], 0.044715, 1.0, ALU.mult, ALU.add))
            st.sync()
            tt(ya[:, :, :], ya[:, :, :], y, ALU.mult).then_inc(gelu_in, 1)
            if split_meanwhile:
                split_lo(dve, split_meanwhile)
            dve.wait_ge(sig_done, i * 2 + (hf + 1))
            tt(y, y, ya[:, :, :], ALU.mult).then_inc(y_full, 1)

        def act_mix(act):
            act.wait_ge(h_spilled, 48)
            for n in range(3):
                act.wait_ge(pre_stored[n], 48)
            act.sem_inc(m_out, 3)
            for b in range(NB):
                act.sem_inc(m_stored[b], 16)
            def evac(i, q, bias=None):
                for b in range(NB):
                    act.wait_ge(m_scaled, i * PASS + (3 * q + b + 1 + 3))
                    fn = ACT.Identity if q < 2 and bias is None else ACT.Sigmoid
                    if q == 1:
                        nc.scalar.activation(up[:, ds(i * T + b * BW, BW)], mt[b], fn, bias=bst[:, 1:2]).then_inc(m_out, 1)
                        continue
                    act.wait_ge(m_stored[b], i * 64 + 16 * (max(q - 1, 0) + 1))
                    nc.scalar.activation(og[b], mt[b], fn, bias=bst[:, q:q + 1] if bias is None else bias).then_inc(m_out, 1)
                if q == 1:
                    return
                for b in range(NB):
                    act.wait_ge(m_out, i * PASS + (3 * q + b + 1 + 3))
                    if bias is not None:
                        dst = gate_dram[2 * DT - 1, :, cols(b)]
                    elif q == 0:
                        dst = u_dram[ds(i, 1), :, cols(b)].rearrange("o p t -> p (o t)")
                    else:
                        dst = gate_dram[ds(i * 3 + (PRE + q - 2), 1), :, cols(b)].rearrange("o p t -> p (o t)")
                    act.dma_start(dst, og[b]).then_inc(m_stored[b], 16)

            with act.Fori(0, 4) as i:
                def gelu(hf):
                    act.wait_ge(gelu_in, i * 2 + (hf + 1))
                    nc.scalar.activation(ya[:, :, :], ya[:, :, :], ACT.Sigmoid, scale=2 * sqrt(2 / pi)).then_inc(sig_done, 1)
                for q in range(MQ):
                    if q < 3:
                        split_hi(act, mix_unit(i, q + 2))
                    evac(i, q)
                    if q == 3:
                        skip_hi(act, i)
                        split_hi(act, mix_unit(i, 6))
                        gelu(0)
                    if q == 4:
                        split_hi(act, mix_unit(i, 7))
                        gelu(1)
            split_hi(act, plan.unit["post"] + 2)
            evac(4, 0, vecs[:, V_BIN + 23:V_BIN + 24])

        def sp_mix(sp):
            sp.wait_ge(h_spilled, 48)
            sp.sem_inc(y_stored, 256)

            def store_y(i, hf):
                sp.wait_ge(y_full, i * 2 + (hf + 1))
                for t in range(L):
                    sp.dma_start(y_dram.rearrange("(g c) t k -> c g t k", c=GC)[:, ds(i * 8 + 4 * hf, 4), t, :],
                                 yv[GC * t:GC * t + GC, hf]).then_inc(y_stored, 16)

            def side(i):
                for b in range(NB):
                    sp.wait_ge(m_stored[b], i * 64 + 32)
                sp.wait_ge(y_mm, i * 2 + 1)
                sp.wait_ge(y_ev, i * 2 + 1)
                for s in range(L):
                    sp.dma_start(ur[GC * s:GC * s + GC, :, :],
                                 u_dram.rearrange("j (g c) (s k) -> j s c g k", c=GC, s=L)[ds(i, 1), s]
                                 .rearrange("o c g k -> (o c) g k")).then_inc(ur_loaded, 16)
                sp.wait_ge(prep_ev, i * 3 + 3)
                sp.dma_start(taps_dram, taps[:, :]).then_inc(taps_stored, 16)
                sp.wait_ge(taps_stored, i * 16 + 16)
                for s in range(L):
                    sp.dma_start(toep[GC * s:GC * s + GC, :, :],
                                 taps_dram.rearrange("(g c) x -> c g x", c=GC)[:, :, P - GC * s:2 * P - GC * s]).then_inc(toep_loaded, 16)
            for q in range(3, 6):
                load_unit(sp, "mix", 0, q)
            with sp.Fori(0, 3) as j:
                load_unit(sp, "mix", Along(j, 3, 1, 1), 0)
                side(j)
                for q in range(1, 6):
                    load_unit(sp, "mix", Along(j, 3, 1, 1), q)
                    if q in (3, 4):
                        store_y(j, q - 3)
            load_unit(sp, "post", 0, 0)
            side(3)
            for q in range(2):
                load_unit(sp, "glu", 0, q)
            for hf in range(2):
                store_y(3, hf)
            load_unit(sp, "pool", 0, 0)

        def pool_windows(pool):
            pool.wait_ge(h_spilled, 48)
            st = Steps(pool, own["pool_prep"])
            tt, cp, ts = nc.gpsimd.tensor_tensor, nc.gpsimd.tensor_copy, nc.gpsimd.tensor_scalar
            for g in range(4):
                w = 2 << g
                pool.wait_ge(m_out, PASS * g + 6 + 3)
                if g == 0:
                    pool.wait_ge(own["dve_prep"], 2)
                u = up[:, g * T:(g + 1) * T].rearrange("p (s k) -> p s k", s=L)
                st.sync()
                st.do(nc.gpsimd.memset(ext[:, :, 0:2], 0.0))
                st.do(cp(ext[:, :, 2:2 + KP], u[:, :, 0:KP]))
                st.do(cp(ext[:, :, 2 + KP:4 + KP], hcol[:, g, :].rearrange("p (k s) -> p s k", s=L)))
                st.do(cp(ext[:, :, 4 + KP:4 + K], u[:, :, KP:K]))
                st.do(cp(tail[:, g, 0, :].rearrange("p (k s) -> p s k", s=L), u[:, :, KP - 2:KP]))
                st.do(cp(tail[:, g, 1, :].rearrange("p (k s) -> p s k", s=L), u[:, :, K - 2:K]))
                src, dst = ext, sum_a
                for level in range(g + 1):
                    d = 1 << level
                    st.sync()
                    if d < L:
                        st.do(tt(dst[:, d:L, :], src[:, d:L, :], src[:, 0:L - d, :], ALU.add))
                    st.do(tt(dst[:, 0:d, 1:], src[:, 0:d, 1:], src[:, L - d:L, 0:K + 3], ALU.add))
                    st.do(cp(dst[:, 0:d, 0:1], src[:, 0:d, 0:1]))
                    src, dst = dst, src
                st.sync()
                st.do(tt(src[:, :, 2:4], src[:, :, 2:4], cnt[:, g, :].rearrange("p (s k) -> p s k", s=L), ALU.mult))
                st.sync()
                st.do(ts(src[:, :, 2:4 + K], src[:, :, 2:4 + K], 1.0 / w, 1.0, ALU.mult, ALU.mult))
                st.sync()
                st.do(tt(u[:, :, 0:KP], src[:, :, 2:2 + KP], u[:, :, 0:KP], ALU.subtract))
                st.do(tt(u[:, :, KP:K], src[:, :, 4 + KP:4 + K], u[:, :, KP:K], ALU.subtract))
                st.sync()
                pool.sem_inc(pooled, 1)

        def pe_after(pe):
            pe.wait_ge(tail_ready, 1)
            nc.tensor.transpose(PB[0][0:64, 0:P], hfin[:, :, :].rearrange("p a j -> p (a j)"), ident[:, :])
            for w in range(2):
                for g in range(4):
                    mm = nc.tensor.transpose(PB[1 + w][0:16, g * P:(g + 1) * P], tail[:, g, w, :], ident[:, :])
            mm.then_inc(last_mm, 1)

        def dve_after(dve):
            dve.wait_ge(pooled, 4)
            dve.sem_inc(tail_ready, 1)
            for g in range(4):
                dve.wait_ge(pl_hi_done, g + 1)
                nc.vector.tensor_tensor(pl_lo[:, g, :], up[:, g * T:(g + 1) * T], pl_hi[:, g, :].bitcast(F32),
                                        ALU.subtract).then_inc(pl_ready, 1)
            split_lo(dve, plan.unit["pool"])
            for j in range(4):
                dve.wait_ge(y_hi_done, j + 1)
                y = y_lo[:, j]
                nc.vector.tensor_tensor(y, y.bitcast(F32), y_hi[:, j].bitcast(F32), ALU.subtract).then_inc(y_ready, 1)

        def act_after(act):
            act.wait_ge(pe_block, MIX_END)
            for g in range(4):
                act.wait_ge(pooled, g + 1)
                nc.scalar.activation(pl_hi[:, g, :], up[:, g * T:(g + 1) * T], ACT.Copy).then_inc(pl_hi_done, 1)
            act.wait_ge(pl_ready, 4)
            act.wait_ge(last_mm, 1)
            split_hi(act, plan.unit["pool"])
            for j in range(4):
                act.wait_ge(y_loaded[j], 16)
                nc.scalar.activation(y_hi[:, j], y_lo[:, j].bitcast(F32), ACT.Copy).then_inc(y_hi_done, 1)
            act.wait_ge(last_mm, 1)
            nc.scalar.activation(hfrow[:, :], PB[0][0:64, 0:P], ACT.Copy).then_inc(last_ev, 1)
            for w in range(2):
                nc.scalar.activation(prow[:, w, :], PB[1 + w][0:16, :], ACT.Copy).then_inc(last_ev, 1)
            act.wait_ge(last_ev, 3)
            for n, out in enumerate((re_prompt, im_prompt, re_sample, im_sample)):
                act.dma_start(out.rearrange("(j g) s -> j (g s)", g=2), hfrow[16 * n:16 * n + 16, :]).then_inc(state_out, 16)
            for w, out in enumerate((pool_prompt, pool_sample)):
                act.dma_start(out, prow[1:16, w, :]).then_inc(state_out, 16)
            act.wait_ge(state_out, 96)

        def sp_after(sp):
            sp.wait_ge(pe_block, MIX_END)
            sp.wait_ge(y_stored, 128 * 10)
            for j in range(4):
                sp.dma_start(y_lo[:, j].bitcast(F32), y_dram[j * P:(j + 1) * P].rearrange("p t k -> p (t k)")).then_inc(y_loaded[j], 16)
            sp.wait_ge(pl_ready, 4)
            sp.wait_ge(last_mm, 1)
            sp.wait_ge(state_out, 96)
            for b in range(NB):
                sp.dma_start(xres[:, 0:DT - 2, cols(b)], h_dram[:, 0:DT - 2, cols(b)]).then_inc(h_back, 16)

        side_slot = [(std[:, :], rpost[:, :]), (rstd[:, 0:BW], rstd[:, BW:2 * BW])]

        def pool_side(pool):
            for b in range(NB):
                pool.wait_ge(m_stored[b], 16 * 18)
                pool.wait_ge(pre_stored[b], 48)
            pool.wait_ge(m_scaled, 4 * PASS + 6)
            for n in range(NB * DT):
                if n == 2:
                    pool.wait_ge(pl_ready, 4)
                    pool.wait_ge(last_mm, 1)
                    pool.wait_ge(state_out, 96)
                    nc.gpsimd.memset(acc[:, :, :], 0.0).then_inc(acc_zero, 1)
                if n >= 2:
                    pool.wait_ge(h_mul[3], n - 1)
                m, b = divmod(n, NB)
                gs, pr = side_slot[n % 2]
                pool.dma_start(gs, gate_dram[m, :, cols(b)]).then_inc(side_loaded[n % 2], 16)
                pool.dma_start(pr, gate_dram[DT + m, :, cols(b)]).then_inc(side_loaded[n % 2], 16)

        def pe_glu(pe, g):
            for q in range(2):
                u = plan.unit[("glu", g)] + q
                m = 2 * g + q
                pe.wait_ge(w_ready, u + 1)
                for b in range(NB):
                    n = NB * m + b
                    if n >= 2:
                        pe.wait_ge(gp_done, n - 1)
                    if q == 0 and g >= 2:
                        pe.wait_ge(out_free[3], 24 * (g - 1) + 26)
                    if n == 0:
                        pe.wait_ge(w_ready, plan.unit["pool"] + 1)
                    three(PC[n % 2][:, 0:BW], (wp_hi[:, m * P:m * P + P], wp_lo[:, m * P:m * P + P]),
                          (pl_hi[:, m // 2, cols(b)], pl_lo[:, m // 2, cols(b)]), True, True).then_inc(gp_mm, 1)
                    if n == 0:
                        pe.wait_ge(y_ready, 4)
                    pe.wait_ge(in_free[3], 3 * m + b + 1)
                    for h, out in ((0, PA), (1, PB)):
                        for k in range(4):
                            c0 = (2 * k + h) * P
                            mm = three(out[b][:, 0:BW], wslices(u % SPLIT_SLOTS, c0, c0 + P),
                                       (y_hi[:, k, cols(b)], y_lo[:, k, cols(b)]), k == 0, k == 3)
                    mm.then_inc(pe_block, 1)

        def pe_merge(pe):
            pe.wait_ge(last_ev, 3)
            pe_glu(pe, 0)
            pe_glu(pe, 1)
            for g in range(2, MG):
                pe_out(pe, 3, g - 2)
                pe_glu(pe, g)
            pe_fin(pe, 3)

        GLU_SPLITS = {(g, q): [plan.unit[("glu", g)] + q + 2] for g in range(MG) for q in range(2)}
        GLU_SPLITS[0, 0], GLU_SPLITS[0, 1] = [], [plan.unit[("glu", 1)]]
        GLU_SPLITS[1, 0] = [plan.unit[("glu", 1)] + 1, plan.unit[("glu", 1)] + 2]

        def dve_glu(dve, g):
            stt, tt = nc.vector.scalar_tensor_tensor, nc.vector.tensor_tensor
            for q in range(2):
                m = 2 * g + q
                for u in GLU_SPLITS[g, q]:
                    split_lo(dve, u)
                for b in range(NB):
                    n = NB * m + b
                    s = n % 2
                    gs, pr = side_slot[s]
                    dve.wait_ge(sig_m, n + 1)
                    stt(ta[:, s, :], PA[b][:, 0:BW], vecs[:, V_BGLU + m:V_BGLU + m + 1], tb[:, s, :], ALU.add, ALU.mult).then_inc(in_free[3], 1)
                    dve.wait_ge(in_free[3], n + 1 + 3)
                    dve.wait_ge(side_loaded[s], 32 * (n // 2 + 1))
                    dve.wait_ge(gp_mm, n + 1)
                    stt(pr, PC[n % 2][:, 0:BW], vecs[:, V_PSC + m:V_PSC + m + 1], pr, ALU.mult, ALU.mult).then_inc(gp_done, 1)
                    tt(ta[:, s, :], ta[:, s, :], gs, ALU.mult).then_inc(merge_a, 1)
                    dve.wait_ge(merge_a, n + 1)
                    dve.wait_ge(gp_done, n + 1)
                    tt(tb[:, s, :], ta[:, s, :], pr, ALU.add).then_inc(h_mul[3], 1)
                    dve.wait_ge(hid_hi_done[3], n + 1)
                    hs = m % 4
                    tt(hid_lo[:, hs, cols(b)], tb[:, s, :], hid_hi[:, hs, cols(b)].bitcast(F32), ALU.subtract).then_inc(hid_ready[3], 1)

        def act_glu(act, g):
            for q in range(2):
                m = 2 * g + q
                for u in GLU_SPLITS[g, q]:
                    split_hi(act, u)
                for b in range(NB):
                    n = NB * m + b
                    s = n % 2
                    act.wait_ge(pe_block, plan.block[("glu", g)] + 3 * q + b + 1)
                    if n >= 2:
                        act.wait_ge(hid_ready[3], n - 1)
                    nc.scalar.activation(tb[:, s, :], PB[b][:, 0:BW], ACT.Sigmoid,
                                         bias=vecs[:, V_BGLU + 8 + m:V_BGLU + 9 + m]).then_inc(sig_m, 1)
                    act.wait_ge(h_mul[3], n + 1)
                    if q == 0 and b == 0:
                        if g >= 2:
                            act.wait_ge(pe_block, plan.block[("merge", g - 2)] + 24)
                    hs = m % 4
                    nc.scalar.activation(hid_hi[:, hs, cols(b)], tb[:, s, :], ACT.Copy).then_inc(hid_hi_done[3], 1)

        def dve_merge(dve, next_units):
            dve.sem_inc(in_free[3], 3)
            dve_glu(dve, 0)
            dve_glu(dve, 1)
            dve.wait_ge(acc_zero, 2)
            dve.sem_inc(out_free[3], 26)
            for g in range(2, MG):
                dve_outs(dve, 3, g - 2)
                dve_glu(dve, g)
            dve_last(dve, 3, next_units)

        def act_merge(act, next_units):
            act_glu(act, 0)
            act_glu(act, 1)
            for g in range(2, MG):
                act_outs(act, 3, g - 2)
                act_glu(act, g)
            act_last(act, 3, next_units)

        def sp_merge(sp):
            for q in range(2):
                load_unit(sp, "glu", 1, q)
            for g in range(2, MG):
                for q in range(2):
                    load_unit(sp, "merge", g - 2, q)
                for q in range(2):
                    load_unit(sp, "glu", g, q)
            for q in range(4):
                load_unit(sp, "fin", 3, q)
            sp.wait_ge(pe_block, plan.block[("fin", 3)])
            sp.dma_start(xres[:, DT - 2:, :], h_dram[:, DT - 2:, :]).then_inc(h_back_last, 16)

        TILES = list(range(9))
        dcol = ta.rearrange("p a b -> p (a b)")[:, 0:DT * DEC].rearrange("p (m t) -> p m t", m=DT)

        def dve_end(dve):
            dve.wait_ge(h_done, 72)
            nc.vector.tensor_copy(dcol.rearrange("p m (k s) -> p m k s", s=L),
                                  xres.rearrange("p m (s k) -> p m k s", s=L)[:, :, KP:K, :]).then_inc(dcol_done, 1)

        def pe_end(pe):
            F = 0
            for tile in TILES:
                b = 2 if tile == 8 else (tile * K + KP - 1) // BW
                pe.wait_ge(h_done, 48 + 8 * b + 8)
                if tile == 8:
                    pe.wait_ge(dcol_done, 1)
                for half in range(2):
                    if F >= 3:
                        pe.wait_ge(yrow_ready, F - 2)
                    rows = DEC if tile == 8 else P
                    for j in range(4):
                        m = 4 * half + j
                        src = xres[:, m, :]
                        if tile == 8:
                            src = dcol[:, m, :]
                        else:
                            src = src[:, tile * K:tile * K + KP]
                        mm = nc.tensor.transpose(PB[F % 3][0:rows, j * P:(j + 1) * P], src, ident[:, :])
                    mm.then_inc(y_turned, 1)
                    F += 1

        def act_end(act):
            F = 0
            for tile in TILES:
                rows = DEC if tile == 8 else P
                for half in range(2):
                    act.wait_ge(y_turned, F + 1)
                    if half == 0 and tile >= 4:
                        act.wait_ge(y_out[tile % 4], 16 * (tile // 4))
                    nc.scalar.activation(yrow[0:rows, tile % 4, 512 * half:512 * half + 512], PB[F % 3][0:rows, :],
                                         ACT.Copy).then_inc(yrow_ready, 1)
                    F += 1

        def sp_end(sp):
            yp = y_prompt.rearrange("(k s) d -> s k d", s=L)
            for tile in TILES:
                sp.wait_ge(yrow_ready, 2 * tile + 2)
                if tile == 8:
                    sp.dma_start(y_sample, yrow[0:DEC, 0, :]).then_inc(y_out[0], 16)
                else:
                    sp.dma_start(yp[tile], yrow[:, tile % 4, :]).then_inc(y_out[tile % 4], 16)
            for i, n in enumerate((3, 2, 2, 2)):
                sp.wait_ge(y_out[i], 16 * n)

        FIRST_PRE, FIRST_F2 = plan.unit["pre"], plan.unit[(2, "in", 0)]

        @block.sync
        def _(sp):
            sp_start(sp)
            sp_ffn(sp, 1, skip=3)
            for q in range(PRE):
                load_unit(sp, "pre", 0, q)
            for b in range(NB):
                sp.wait_ge(h_done, 8 * b + 8)
                sp.dma_start(h_dram[:, :, cols(b)], xres[:, :, cols(b)]).then_inc(h_spilled, 16)
                if b == 0:
                    sp_prep(sp)
                    for q in range(3):
                        load_unit(sp, "mix", 0, q)
                    sp_prep_tables(sp)
            sp_mix(sp)
            sp_after(sp)
            sp_merge(sp)
            sp_ffn(sp, 2)
            sp_end(sp)

        @block.gpsimd
        def _(pool):
            nc.gpsimd.memset(ident[:, :], 0.0).then_inc(const_ready, 1)
            nc.gpsimd.memset(ones[:, :], 1.0).then_inc(const_ready, 1)
            nc.gpsimd.memset(epsc[:, :], EPS).then_inc(const_ready, 1)
            pool.wait_ge(const_ready, 3)
            nc.gpsimd.affine_select(out=ident[:, :], in_=ident[:, :], compare_op=ALU.not_equal, fill=1.0, base=0,
                                    pattern=[[-1, P]], channel_multiplier=1).then_inc(const_ready, 2)
            pool.wait_ge(x_turned, 18)
            pool.wait_ge(vec_mm, 1)
            nc.gpsimd.memset(acc[:, :, :], 0.0).then_inc(acc_zero, 1)
            for b in range(NB):
                add_squares(pool, job(0, "x", b))
            pool_stage(pool, 1)
            pool_prep(pool)
            pool_windows(pool)
            pool_side(pool)
            pool_stage(pool, 2)
            pool.wait_ge(h_done, 48)
            nc.gpsimd.memset(acc[:, :, :], 0.0).then_inc(acc_zero, 1)
            pool_stage(pool, 3)

        @block.scalar
        def _(act):
            act.wait_ge(const_ready, 5)
            empty_x(act, lambda d, s: nc.scalar.activation(d, s, ACT.Copy), 1, x_act)
            split_hi(act, 0)
            split_hi(act, 1)
            act.wait_ge(x_dve, 9)
            act.wait_ge(vec_ready, 1)
            act.wait_ge(x_act, 9)
            for b in range(NB + 1):
                for m in range(DT):
                    if b < NB:
                        z_hi_part(act, 0, b, m, V_PRE1)
                    if b:
                        square(act, job(0, "x", b - 1), m, xres[:, m, cols(b - 1)])
            act_ffn(act, 1, [FIRST_PRE + u for u in range(PRE)])
            act_pre(act)
            act_prep(act)
            act_mix(act)
            act_after(act)
            act_merge(act, [FIRST_F2, FIRST_F2 + 1])
            act_ffn(act, 2, [])
            act_end(act)

        @block.vector
        def _(dve):
            empty_x(dve, nc.vector.tensor_copy, 0, x_dve)
            dve.wait_ge(vec_mm, 1)
            nc.vector.tensor_copy(vecs[:, :], PC[0][:, 0:P]).then_inc(vec_ready, 1)
            split_lo(dve, 0)
            split_lo(dve, 1)
            dve.wait_ge(vec_ready, 1)
            dve.wait_ge(x_dve, 9)
            dve.wait_ge(x_act, 9)
            dve.sem_inc(in_free[1], 3)
            for b in range(NB):
                for m in range(DT):
                    z_lo_part(dve, 0, b, m, V_PRE1)
            before = lambda st: (lambda b: recip_row(dve, st, b))
            dve_ffn(dve, 1, before(0), [FIRST_PRE + u for u in range(PRE)])
            steps = dve_prep_a(dve)
            dve_prep_b(dve, steps)
            dve_mix(dve)
            split_lo(dve, plan.unit["post"] + 2)
            dve_mix_evac(dve, 4, 0)
            dve_after(dve)
            dve_merge(dve, [FIRST_F2, FIRST_F2 + 1])
            dve_ffn(dve, 2, before(2), [])
            dve_end(dve)

        @block.tensor
        def _(pe):
            pe_start(pe)
            pe_ffn(pe, 1)
            pe_pre(pe)
            pe.sem_inc(y_mm, 1)
            pe_mix(pe)
            pe_after(pe)
            pe_merge(pe)
            pe_ffn(pe, 2)
            pe_end(pe)


_INS = ["x_prompt", "x_sample", "state_ssm_re", "state_ssm_im", "cache_pool", "ffn1_pre_g", "ffn1_w_in", "ffn1_w_out",
        "ffn1_post_g", "mix_pre_g", "w_in", "b_in", "ssm_lambda_re", "ssm_lambda_im", "ssm_log_step", "ssm_b_re", "ssm_b_im",
        "ssm_c_re", "ssm_c_im", "ssm_d", "ssm_w_glu", "ssm_b_glu", "pool_w", "pool_scale", "w_out", "mix_post_g",
        "ffn2_pre_g", "ffn2_w_in", "ffn2_w_out", "ffn2_post_g"]
_OUTS = [((1, SEQ, D), (SEQ, D)), ((1, DEC, D), (DEC, D)), ((1, 1, G, NS), (G, NS)), ((1, 1, G, NS), (G, NS)),
         ((1, 1, HIST, DS), (HIST, DS)), ((1, 1, G, NS), (G, NS)), ((1, 1, G, NS), (G, NS)), ((1, 1, HIST, DS), (HIST, DS))]


def constants():
    counts = np.ones((P, 4, L, 2), np.float32)
    for g in range(4):
        w = 2 << g
        for t in range(w - 1):
            counts[:, g, t % L, t // L] = w / (t + 1)
    mask = np.ones((P, K), np.float32)
    mask[:, [0, KP]] = 0.0
    return {"window_counts": counts.reshape(P, 4, 2 * L), "scan_mask": mask}


def kernel(**inputs):
    import concourse.bacc as bacc
    from concourse.bass_utils import run_bass_kernel_spmd

    nc = bacc.Bacc("TRN2", target_bir_lowering=False, num_devices=1, dynamic_dma_scratch_size=1024)
    arrays, args = {}, {}
    for name in _INS:
        x = np.ascontiguousarray(inputs[name])
        x = x[0] if x.shape[0] == 1 else x
        if name in ("state_ssm_re", "state_ssm_im", "cache_pool"):
            x = x[0]
        arrays[name] = np.ascontiguousarray(x)
    arrays.update(constants())
    for name, x in arrays.items():
        args[name] = nc.dram_tensor(name, x.shape, mybir.dt.from_np(x.dtype), kind="ExternalInput").ap()
    outs = [nc.dram_tensor(f"out_{n}", flat, F32, kind="ExternalOutput").ap() for n, (_, flat) in enumerate(_OUTS)]
    layer(nc, args, outs)
    r = run_bass_kernel_spmd(nc, [arrays], core_ids=[0])
    return tuple(r.results[0][f"out_{n}"].reshape(shape) for n, (shape, _) in enumerate(_OUTS))
```
